# Optimizing a Trainium2 kernel written in Bass

```python
import jax, jax.numpy as jnp
from jax import lax
import numpy as np

'''One inference step of a 4-layer hybrid streaming encoder trunk; two request groups share every weight.

Layer pattern (sandwich RMSNorm before and after every sub-layer; the post-norm output is added to the residual):
  even layers: A (chunked spatial-gating MLP, 4 head groups) in parallel with B (sliding-window GQA with
               learned sinks, 8 q / 2 kv heads, partial rotary); one combined input projection, outputs
               concatenated into one output projection
  odd layers : C (multi-scale trailing mean pooling over 4 channel groups, windows 2/4/8/16)
  every layer: dense SwiGLU FFN
Chunk-causal: CHUNK = 64 frames; no frame reads a later chunk.

Inputs:
  x_prompt (BATCH, SEQ, D_MODEL)           first SEQ frames of new streams, positions 0..SEQ-1
  x_sample (DEC_BATCH, DEC_SEQ, D_MODEL)   next frames of running streams, positions PAST_LEN..PAST_LEN+DEC_SEQ-1
  cache_b_k, cache_b_v (N_EVEN, DEC_BATCH, B_WINDOW, B_KV_HEADS, B_HEAD_DIM)
      rotated keys / values of positions PAST_LEN-B_WINDOW..PAST_LEN-1 for each even layer
  state_c_pool (N_ODD, DEC_BATCH, C_HIST, D_MODEL)  last C_HIST normalised inputs of mixer C per odd layer
Returns (y_prompt, y_sample, new_b_k_prompt, new_b_v_prompt, new_c_pool_prompt,
         new_b_k_sample, new_b_v_sample, new_c_pool_sample, new_a_v_sample):
  y_prompt (BATCH, SEQ, D_MODEL); y_sample (DEC_BATCH, DEC_SEQ, D_MODEL)
  new_b_k_prompt, new_b_v_prompt (N_EVEN, BATCH, B_WINDOW, B_KV_HEADS, B_HEAD_DIM)   last B_WINDOW rows
  new_c_pool_prompt (N_ODD, BATCH, C_HIST, D_MODEL)                                  last C_HIST rows
  new_b_k_sample, new_b_v_sample (N_EVEN, DEC_BATCH, DEC_SEQ, B_KV_HEADS, B_HEAD_DIM) new rows
  new_c_pool_sample (N_ODD, DEC_BATCH, C_HIST, D_MODEL)                              updated buffer
  new_a_v_sample (N_EVEN, DEC_BATCH, DEC_SEQ, A_HEADS, A_GROUP)   v rows opening the new 128-chunk of mixer A
'''

D_MODEL = 1024
BATCH = 1
SEQ = 512
DEPTH = 2
DEC_BATCH = 1
DEC_SEQ = 32
PAST_LEN = 1024

CHUNK = 64
N_EVEN = (DEPTH + 1) // 2
N_ODD = DEPTH // 2
EPS = 1e-6
A_CHUNK = 128
A_WIDTH = D_MODEL // 2
A_HEADS = 4
A_GROUP = A_WIDTH // A_HEADS
B_HEAD_DIM = 64
B_Q_HEADS = (D_MODEL // 2) // B_HEAD_DIM
B_KV_HEADS = 2
B_GROUPS = B_Q_HEADS // B_KV_HEADS
B_WINDOW = 128
B_WIN_CHUNKS = B_WINDOW // CHUNK
B_QW = B_Q_HEADS * B_HEAD_DIM
B_KW = B_KV_HEADS * B_HEAD_DIM
ROPE_DIMS = B_HEAD_DIM // 4
ROPE_THETA = 500000.0
AB_IN = 2 * A_WIDTH + B_QW + 2 * B_KW
AB_OUT = A_WIDTH + B_QW
C_WINDOWS = (2, 4, 8, 16)
C_GROUPS = len(C_WINDOWS)
C_GROUP = D_MODEL // C_GROUPS
C_HIST = max(C_WINDOWS) - 1
D_FF = -(-8 * D_MODEL // (3 * 256)) * 256

kernel_name = 'hybrid_streaming_encoder_step'

def rms_norm(x, g):
    xf = x.astype(jnp.float32)
    y = xf * lax.rsqrt(jnp.mean(xf * xf, axis=-1, keepdims=True) + EPS)
    return (y * g.astype(jnp.float32)).astype(x.dtype)

def layer_norm(x, g, b):
    xf = x.astype(jnp.float32)
    mu = jnp.mean(xf, axis=-1, keepdims=True)
    xc = xf - mu
    y = xc * lax.rsqrt(jnp.mean(xc * xc, axis=-1, keepdims=True) + EPS)
    return (y * g.astype(jnp.float32) + b.astype(jnp.float32)).astype(x.dtype)

def rope_partial(x, pos):
    half = ROPE_DIMS // 2
    inv = ROPE_THETA ** (-jnp.arange(half, dtype=jnp.float32) * 2.0 / ROPE_DIMS)
    ang = pos.astype(jnp.float32)[:, None] * inv[None, :]
    cos = jnp.cos(ang)[:, None, :]
    sin = jnp.sin(ang)[:, None, :]
    x1 = x[..., :half].astype(jnp.float32)
    x2 = x[..., half:ROPE_DIMS].astype(jnp.float32)
    rot = jnp.concatenate([x1 * cos - x2 * sin, x2 * cos + x1 * sin], axis=-1)
    return jnp.concatenate([rot.astype(x.dtype), x[..., ROPE_DIMS:]], axis=-1)

def ab_project(h, pos, w_in, ln_g, ln_b):
    b, s = h.shape[:2]
    z = h @ w_in
    u = jax.nn.gelu(z[..., :A_WIDTH])
    va = layer_norm(jax.nn.gelu(z[..., A_WIDTH:2 * A_WIDTH]), ln_g, ln_b)
    o = 2 * A_WIDTH
    q = z[..., o:o + B_QW].reshape(b, s, B_Q_HEADS, B_HEAD_DIM)
    k = z[..., o + B_QW:o + B_QW + B_KW].reshape(b, s, B_KV_HEADS, B_HEAD_DIM)
    v = z[..., o + B_QW + B_KW:].reshape(b, s, B_KV_HEADS, B_HEAD_DIM)
    return u, va, rope_partial(q, pos), rope_partial(k, pos), v

def spatial_gate(u, va, ws, bs):
    b, n, L = va.shape[:3]
    cidx = jnp.arange(L) // CHUNK
    mask = cidx[None, :] <= cidx[:, None]
    wm = jnp.where(mask[None], ws[:, :L, :L], 0.0).astype(va.dtype)
    vh = va.reshape(b, n, L, A_HEADS, A_GROUP)
    z = jnp.einsum('hij,bnjhc->bnihc', wm, vh) + bs[:, :L].T[None, None, :, :, None].astype(va.dtype)
    return (u.reshape(b, n, L, A_HEADS, A_GROUP) * z).reshape(b, n * L, A_WIDTH)

def sink_attention(q, k, v, mask, sinks):
    s = jnp.einsum('bnqkgd,bnskd->bnkgqs', q, k, preferred_element_type=jnp.float32) * (B_HEAD_DIM ** -0.5)
    s = jnp.where(mask[None, :, None, None], s, -jnp.inf)
    sink = sinks.astype(jnp.float32).reshape(1, 1, B_KV_HEADS, B_GROUPS, 1, 1)
    m = jnp.maximum(jnp.max(s, axis=-1, keepdims=True), sink)
    p = jnp.exp(s - m)
    p = p / (jnp.sum(p, axis=-1, keepdims=True) + jnp.exp(sink - m))
    return jnp.einsum('bnkgqs,bnskd->bnqkgd', p.astype(v.dtype), v)

def ab_mixer_prompt(h, pos, w_in, ln_g, ln_b, ws, bs, sinks, w_out):
    b, s = h.shape[:2]
    u, va, q, k, v = ab_project(h, pos, w_in, ln_g, ln_b)
    n_a = s // A_CHUNK
    ya = spatial_gate(u.reshape(b, n_a, A_CHUNK, A_WIDTH), va.reshape(b, n_a, A_CHUNK, A_WIDTH), ws, bs)
    n_c = s // CHUNK
    qb = q.reshape(b, n_c, CHUNK, B_KV_HEADS, B_GROUPS, B_HEAD_DIM)
    kb = k.reshape(b, n_c, CHUNK, B_KV_HEADS, B_HEAD_DIM)
    vb = v.reshape(b, n_c, CHUNK, B_KV_HEADS, B_HEAD_DIM)

    def band(xb):
        pads = ((0, 0), (B_WIN_CHUNKS - 1, 0), (0, 0), (0, 0), (0, 0))
        xp = jnp.pad(xb, pads)
        return jnp.concatenate([xp[:, d:d + n_c] for d in range(B_WIN_CHUNKS)], axis=2)

    key_chunk = jnp.arange(n_c)[:, None] - (B_WIN_CHUNKS - 1) + jnp.arange(B_WIN_CHUNKS * CHUNK)[None, :] // CHUNK
    mask = (key_chunk >= 0)[:, None, :]
    ob = sink_attention(qb, band(kb), band(vb), mask, sinks).reshape(b, s, B_QW)
    out = jnp.concatenate([ya, ob], axis=-1) @ w_out
    return out, k[:, -B_WINDOW:], v[:, -B_WINDOW:]

def ab_mixer_sample(h, pos, cache_k, cache_v, w_in, ln_g, ln_b, ws, bs, sinks, w_out):
    b, t = h.shape[:2]
    u, va, q, k, v = ab_project(h, pos, w_in, ln_g, ln_b)
    ya = spatial_gate(u[:, None], va[:, None], ws, bs)
    win = cache_k.shape[1]
    kk = jnp.concatenate([cache_k, k], axis=1)[:, None]
    vv = jnp.concatenate([cache_v, v], axis=1)[:, None]
    key_pos = jnp.concatenate([PAST_LEN - win + jnp.arange(win, dtype=jnp.int32), pos])
    qc = pos // CHUNK
    kc = key_pos // CHUNK
    mask = ((kc[None, :] <= qc[:, None]) & (kc[None, :] > qc[:, None] - B_WIN_CHUNKS) & (key_pos[None, :] >= 0))[None]
    qb = q.reshape(b, 1, t, B_KV_HEADS, B_GROUPS, B_HEAD_DIM)
    ob = sink_attention(qb, kk, vv, mask, sinks).reshape(b, t, B_QW)
    out = jnp.concatenate([ya, ob], axis=-1) @ w_out
    return out, k, v, va.reshape(b, t, A_HEADS, A_GROUP)

def pool_mixer(xn, hist, pos, c_w, c_scale):
    b, t = xn.shape[:2]
    ext = jnp.concatenate([hist, xn], axis=1)
    cs = jnp.pad(jnp.cumsum(ext.astype(jnp.float32), axis=1), ((0, 0), (1, 0), (0, 0)))
    diffs = []
    for g, w in enumerate(C_WINDOWS):
        lo, hi = g * C_GROUP, (g + 1) * C_GROUP
        win_sum = cs[:, C_HIST + 1:C_HIST + 1 + t, lo:hi] - cs[:, C_HIST + 1 - w:C_HIST + 1 - w + t, lo:hi]
        cnt = jnp.minimum(pos + 1, w).astype(jnp.float32)[None, :, None]
        diffs.append(win_sum / cnt - xn[..., lo:hi].astype(jnp.float32))
    d = jnp.stack(diffs, axis=2).astype(xn.dtype)
    y = jnp.einsum('btgc,gce->btge', d, c_w).reshape(b, t, D_MODEL) * c_scale
    return y, ext[:, -C_HIST:]

def swiglu(h, w_in, w_out):
    gu = h @ w_in
    return (jax.nn.silu(gu[..., :D_FF]) * gu[..., D_FF:]) @ w_out

def setup_inputs(seed: int = 0) -> dict:
    key = jax.random.key(seed)
    ks = jax.random.split(key, 18)
    f32 = jnp.float32
    nrm = lambda k, shape, s: jax.random.normal(k, shape, f32) * s
    return {
        'x_prompt': nrm(ks[0], (BATCH, SEQ, D_MODEL), 1.0),
        'x_sample': nrm(ks[1], (DEC_BATCH, DEC_SEQ, D_MODEL), 1.0),
        'cache_b_k': nrm(ks[2], (N_EVEN, DEC_BATCH, B_WINDOW, B_KV_HEADS, B_HEAD_DIM), 1.0),
        'cache_b_v': nrm(ks[3], (N_EVEN, DEC_BATCH, B_WINDOW, B_KV_HEADS, B_HEAD_DIM), 1.0),
        'state_c_pool': nrm(ks[4], (N_ODD, DEC_BATCH, C_HIST, D_MODEL), 1.0),
        'norm_g': 1.0 + nrm(ks[5], (DEPTH, 4, D_MODEL), 0.05),
        'ab_w_in': nrm(ks[6], (N_EVEN, D_MODEL, AB_IN), D_MODEL ** -0.5),
        'a_ln_g': 1.0 + nrm(ks[7], (N_EVEN, A_WIDTH), 0.05),
        'a_ln_b': nrm(ks[8], (N_EVEN, A_WIDTH), 0.02),
        'a_ws': nrm(ks[9], (N_EVEN, A_HEADS, A_CHUNK, A_CHUNK), A_CHUNK ** -0.5),
        'a_bs': 1.0 + nrm(ks[10], (N_EVEN, A_HEADS, A_CHUNK), 0.05),
        'b_sinks': nrm(ks[11], (N_EVEN, B_Q_HEADS), 0.5),
        'ab_w_out': nrm(ks[12], (N_EVEN, AB_OUT, D_MODEL), AB_OUT ** -0.5),
        'c_w': nrm(ks[13], (N_ODD, C_GROUPS, C_GROUP, C_GROUP), C_GROUP ** -0.5),
        'c_scale': 1.0 + nrm(ks[14], (N_ODD, D_MODEL), 0.05),
        'ffn_w_in': nrm(ks[15], (DEPTH, D_MODEL, 2 * D_FF), D_MODEL ** -0.5),
        'ffn_w_out': nrm(ks[16], (DEPTH, D_FF, D_MODEL), D_FF ** -0.5),
    }

def reference(x_prompt, x_sample, cache_b_k, cache_b_v, state_c_pool, norm_g, ab_w_in, a_ln_g, a_ln_b,
              a_ws, a_bs, b_sinks, ab_w_out, c_w, c_scale, ffn_w_in, ffn_w_out):
    pos_p = jnp.arange(x_prompt.shape[1], dtype=jnp.int32)
    pos_s = PAST_LEN + jnp.arange(x_sample.shape[1], dtype=jnp.int32)
    hp, hs = x_prompt, x_sample
    bk_p, bv_p, cp_p, bk_s, bv_s, cp_s, av_s = [], [], [], [], [], [], []
    for layer in range(DEPTH):
        li = layer // 2
        g = norm_g[layer]
        xp = rms_norm(hp, g[0])
        xs = rms_norm(hs, g[0])
        if layer % 2 == 0:
            mp, kp, vp = ab_mixer_prompt(xp, pos_p, ab_w_in[li], a_ln_g[li], a_ln_b[li], a_ws[li], a_bs[li],
                                         b_sinks[li], ab_w_out[li])
            ms, kn, vn, avn = ab_mixer_sample(xs, pos_s, cache_b_k[li], cache_b_v[li], ab_w_in[li], a_ln_g[li],
                                              a_ln_b[li], a_ws[li], a_bs[li], b_sinks[li], ab_w_out[li])
            bk_p.append(kp)
            bv_p.append(vp)
            bk_s.append(kn)
            bv_s.append(vn)
            av_s.append(avn)
        else:
            hist0 = jnp.zeros((xp.shape[0], C_HIST, D_MODEL), xp.dtype)
            mp, cpn = pool_mixer(xp, hist0, pos_p, c_w[li], c_scale[li])
            ms, csn = pool_mixer(xs, state_c_pool[li], pos_s, c_w[li], c_scale[li])
            cp_p.append(cpn)
            cp_s.append(csn)
        hp = hp + rms_norm(mp, g[1])
        hs = hs + rms_norm(ms, g[1])
        hp = hp + rms_norm(swiglu(rms_norm(hp, g[2]), ffn_w_in[layer], ffn_w_out[layer]), g[3])
        hs = hs + rms_norm(swiglu(rms_norm(hs, g[2]), ffn_w_in[layer], ffn_w_out[layer]), g[3])
    return (hp, hs, jnp.stack(bk_p), jnp.stack(bv_p), jnp.stack(cp_p),
            jnp.stack(bk_s), jnp.stack(bv_s), jnp.stack(cp_s), jnp.stack(av_s))


_drawn_inputs = setup_inputs


def setup_inputs(seed=0):
    import zlib

    import numpy as np

    out = dict(_drawn_inputs(seed))
    spreads = {}
    factors = {'a_ln_b': 2.956, 'b_sinks': 8.0}
    for name, (base, spread) in spreads.items():
        noise = np.random.default_rng([zlib.crc32(name.encode()), seed]).standard_normal(out[name].shape)
        drawn = base * np.exp(spread * noise) if base else spread * noise
        out[name] = __import__('jax').numpy.asarray(drawn.astype(out[name].dtype))
    for name, factor in factors.items():
        out[name] = (out[name] * factor).astype(out[name].dtype)
    return out
```

```python
from contextlib import ExitStack

import concourse.bass as bass
import numpy as np
from concourse import mybir

F32 = mybir.dt.float32
F32R = mybir.dt.float32r
ACT = mybir.ActivationFunctionType
ALU = mybir.AluOpType
AX = mybir.AxisListType

P = 128
D = 1024
KC = D // P
SEQ, DEC, PAST = 512, 32, 1024
TOK = SEQ + DEC
HALF = TOK // 2
DFF = 2816
FC = DFF // P
CHUNK = 64
NCH = SEQ // CHUNK
HD = 64
AW = 512
AH = 4
NQ, NKV = 8, 2
ROPE, THETA = 16, 500000.0
WIN = 128
HIST = 15
POOLS = (2, 4, 8, 16)
EPS = 1e-6
MASKED = -1e30
SCALE = HD ** -0.5
TILES = [(t * P, P) for t in range(SEQ // P)] + [(SEQ, DEC)]
NT = len(TILES)
EXT = HIST + SEQ + HIST + DEC
EXP, EXS = HIST, 2 * HIST + SEQ
PIECES = ((0, 6), (6, 12), (12, 17), (17, 22))
MIXER_STORES = (5, 7)
OUT_BANKS = (2, 4, 6, 0)
GROUPS = (1, 0, 2, 3)
POOL_ORDER = (4, 5, 6, 7, 2, 3, 0, 1)

U_IN = 0
U_OUT = U_IN + 14
U_FI = (U_OUT + 8, U_OUT + 8 + 2 * FC + 4 * KC + 4)
U_FO = (U_FI[0] + 2 * FC, U_FI[1] + 2 * FC)
U_C = U_FO[0] + 4 * KC
U_END = U_FO[1] + 4 * KC
NRAW, NSPLIT = 2, 4
assert U_C + 4 == U_FI[1]
UNIT = 8 * P


def unit_columns(m):
    for base in U_FO:
        if base <= m < base + 4 * KC:
            a, b = PIECES[(m - base) % 4]
            return (b - a) * P
    return 4 * P if U_C <= m < U_C + 4 else UNIT


def unit_dmas(m):
    if U_IN + 6 <= m < U_IN + 10:
        return 2
    return 3 if U_OUT <= m < U_OUT + 8 else 1


def loaded(m):
    return 16 * sum(unit_dmas(j) for j in range(m % NRAW, m + 1, NRAW))


def shape_constants():
    pos = np.concatenate([np.arange(SEQ), PAST + np.arange(DEC)]).astype(np.float32)
    inv = np.float32(THETA) ** (-np.arange(ROPE // 2, dtype=np.float32) * np.float32(2.0) / np.float32(ROPE))
    ang = (pos[:, None] * inv.astype(np.float32)[None, :]).astype(np.float32)
    cos, sin = np.ones((P, TOK), np.float32), np.zeros((P, TOK), np.float32)
    for p in range(P):
        d = p % HD
        if d < ROPE:
            cos[p] = np.cos(ang[:, d % (ROPE // 2)])
            sin[p] = np.sin(ang[:, d % (ROPE // 2)]) * (-1.0 if d < ROPE // 2 else 1.0)
    inverse = np.stack([1.0 / np.minimum(np.arange(16) + 1, w) for w in POOLS]).astype(np.float32)
    return np.concatenate([np.eye(P, dtype=np.float32), cos, sin,
                           np.broadcast_to(inverse.reshape(1, -1), (P, 64))], axis=1)


def build(nc, x_prompt, x_sample, cache_k, cache_v, state, norm_g, ab_w_in, ln_g, ln_b, a_ws, a_bs, b_sinks,
          ab_w_out, c_w, c_scale, ffn_w_in, ffn_w_out, constants,
          y_p, y_s, bk_p, bv_p, cp_p, bk_s, bv_s, cp_s, av_s):
    with ExitStack() as ctx:
        def sb(name, shape, dt=F32, scope=ctx):
            return scope.enter_context(nc.sbuf_tensor(name, shape, dt))

        def sem(name):
            return ctx.enter_context(nc.semaphore(name))

        ps = ctx.enter_context(nc.psum_tensor("ps", [P, 8 * 512], F32))

        def flat(b, c0, n, p=P):
            return ps[0:p, b * 512 + c0:b * 512 + c0 + n]

        def pair(b):
            return ps[:, b * 512:(b + 2) * 512].rearrange("p (b n) -> p b n", b=2)[:, :, 0:HALF]

        def halves(ap):
            return ap.rearrange("p (b n) -> p b n", b=2)

        h = sb("h", [P, KC, TOK])
        xhi = sb("xhi", [P, KC, TOK], F32R)
        with ExitStack() as used:
            xlo = sb("xlo", [P, KC, TOK], F32R, used)
        z = sb("z", [P, KC, TOK])
        raw = sb("raw", [P, NRAW, UNIT])
        whi = sb("whi", [P, NSPLIT, UNIT], F32R)
        wlo = sb("wlo", [P, NSPLIT, UNIT], F32R)
        r_post = sb("r_post", [P, TOK])
        r_pre = sb("r_pre", [P, TOK])
        acc_post = sb("acc_post", [P, TOK])
        acc_pre = sb("acc_pre", [P, TOK])
        tmp = sb("tmp", [P, 2, TOK])
        tmp2 = sb("tmp2", [P, 2, TOK])
        ident = sb("ident", [P, P])
        gains = sb("gains", [P, 72])
        ssq = sb("ssq", [P, NT])
        rms = sb("rms", [P, NT])
        rstd = sb("rstd", [P, NT])
        eps = sb("eps", [P, 1])
        ones = sb("ones", [P, 1])
        warmed = sb("warmed", [P, 1])

        def gain(layer, j, k):
            c = (layer * 4 + j) * KC + k
            return gains[:, c:c + 1]

        def scale_c(k):
            return gains[:, 64 + k:65 + k]

        with ExitStack() as ab:
            ab_sb = lambda name, shape, dt=F32: sb(name, shape, dt, ab)
            yhi = ab_sb("yhi", [P, KC, TOK], F32R)
            ylo = ab_sb("ylo", [P, KC, TOK], F32R)
            u_raw = ab_sb("u_raw", [P, AH, TOK])
            gated = ab_sb("gated", [P, AH, TOK])
            va = ab_sb("va", [P, NT, AW])
            ln_gb = ab_sb("ln_gb", [P, 2, AW])
            bs_b = ab_sb("bs_b", [P, AH, P])
            cossin = ab_sb("cossin", [P, 2, TOK])
            q_r = ab_sb("q_r", [P, 4 * TOK])
            k_r = ab_sb("k_r", [P, TOK])
            v_t = ab_sb("v_t", [P, 4, P])
            v_even = ab_sb("v_even", [P, 4, P])
            v_s = ab_sb("v_s", [P, P])
            k_s = ab_sb("k_s", [P, P])
            wm_t = ab_sb("wm_t", [P, AH, P])
            s_sb = ab_sb("s_sb", [P, 2, 512])
            p_t = ab_sb("p_t", [P, 512])
            k_out = ab_sb("k_out", [P, 2, P])
            mask_s = ab_sb("mask_s", [P, P])
            sinks = ab_sb("sinks", [P, NQ])
            sink_p = ab_sb("sink_p", [P, 4])
            sink_s = ab_sb("sink_s", [P, 2])
            top = ab_sb("top", [P, 2, 4])
            peak = ab_sb("peak", [P, 2, 4])
            sunk = ab_sb("sunk", [P, 2, 4])
            den = ab_sb("den", [P, 2, 4])
            den2 = ab_sb("den2", [P, 2, 4])
            rden = ab_sb("rden", [P, 2, 4])
            stats = ab_sb("stats", [P, NT, 6])
            mean_var = ab_sb("mean_var", [P, NT, 2])
            ln_rms = ab_sb("ln_rms", [P, NT])
            ln_rstd = ab_sb("ln_rstd", [P, NT])
        with ExitStack() as first:
            x_tok = sb("x_tok", [P, NT, D], F32, first)
            gain_rows = sb("gain_rows", [72, P], F32, first)
            ws = sb("ws", [P, AH, P], F32, first)
            k_cache = sb("k_cache", [CHUNK, P], F32, first)
        with ExitStack() as ffn:
            mhi = sb("mhi", [P, FC, TOK], F32R, ffn)
            mlo = sb("mlo", [P, FC, TOK], F32R, ffn)
        with ExitStack() as pool_scope:
            ext = sb("ext", [P, KC, EXT], F32, pool_scope)
            win = [[sb(f"win{a}{b}", [P, 2, EXT], F32, pool_scope) for b in range(2)] for a in range(2)]
            dif = sb("dif", [P, 2, 2, TOK], F32, pool_scope)
            z_pool = sb("z_pool", [P, KC, TOK], F32, pool_scope)
            hist = sb("hist", [HIST, D], F32, pool_scope)
            pool_out = sb("pool_out", [HIST, 2, D], F32, pool_scope)
            early = sb("early", [P, 2, 16], F32, pool_scope)
            inverse = sb("inverse", [P, 4, 16], F32, pool_scope)
        with ExitStack() as end:
            y_tok = sb("y_tok", [P, NT, D], F32, end)

        w_loaded = [sem(f"w_loaded{i}") for i in range(NRAW)]
        w_hi, w_lo, w_used = sem("w_hi"), sem("w_lo"), sem("w_used")
        x_loaded = [sem(f"x_loaded{i}") for i in range(NT)]
        ident_loaded, gains_loaded, rope_loaded = sem("ident_loaded"), sem("gains_loaded"), sem("rope_loaded")
        ws_loaded, bs_loaded, ln_loaded = sem("ws_loaded"), sem("bs_loaded"), sem("ln_loaded")
        sinks_loaded, kc_loaded, vc_loaded = sem("sinks_loaded"), sem("kc_loaded"), sem("vc_loaded")
        hist_loaded, inverse_loaded = sem("hist_loaded"), sem("inverse_loaded")
        set_up, set_sample, set_stats, set_gaps = sem("set_up"), sem("set_sample"), sem("set_stats"), sem("set_gaps")
        gains_turned, gains_ready = sem("gains_turned"), sem("gains_ready")
        x_turned, h_first, x_squared = sem("x_turned"), sem("h_first"), sem("x_squared")
        ws_turned, wm_ready, kc_turned, kc_ready = sem("ws_turned"), sem("wm_ready"), sem("kc_turned"), sem("kc_ready")
        sum_ready, rms_ready, rstd_ready = sem("sum_ready"), sem("rms_ready"), sem("rstd_ready")
        rstd_spread, r_ready = sem("rstd_spread"), sem("r_ready")
        z_evacuated, acc_zeroed, acc_added = sem("z_evacuated"), sem("acc_zeroed"), sem("acc_added")
        z_scaled, h_added, h_squared, pre_added = sem("z_scaled"), sem("h_added"), sem("h_squared"), sem("pre_added")
        normed, x_hi, x_lo = sem("normed"), sem("x_hi"), sem("x_lo")
        va_gelu, va_stats, va_bn, ln_rms_ready = sem("va_gelu"), sem("va_stats"), sem("va_bn"), sem("ln_rms_ready")
        ln_rstd_ready, va_normed, va_scaled, va_ready = sem("ln_rstd_ready"), sem("va_normed"), sem("va_scaled"), sem("va_ready")
        v_evacuated, rope_swapped, rope_sined, rope_cosined = sem("v_evacuated"), sem("rope_swapped"), sem("rope_sined"), sem("rope_cosined")
        rope_done, k_s_ready, k_turned, k_out_ready = sem("rope_done"), sem("k_s_ready"), sem("k_turned"), sem("k_out_ready")
        gate_done, gate_biased, sinks_ready = sem("gate_done"), sem("gate_biased"), sem("sinks_ready")
        scored, s_masked, topped, peaked = sem("scored"), sem("s_masked"), sem("topped"), sem("peaked")
        shifted, sink_shifted, exp_done, summed = sem("shifted"), sem("sink_shifted"), sem("exp_done"), sem("summed")
        den_ready, rden_ready, p_ready = sem("den_ready"), sem("rden_ready"), sem("p_ready")
        p_turned, p_t_ready, pv_done, att_hi, att_lo = sem("p_turned"), sem("p_t_ready"), sem("pv_done"), sem("att_hi"), sem("att_lo")
        u_evacuated, u_gelu, ya_ready, ya_hi, ya_lo = sem("u_evacuated"), sem("u_gelu"), sem("ya_ready"), sem("ya_hi"), sem("ya_lo")
        gu_scaled, silu_done, m_ready, m_hi, m_lo = sem("gu_scaled"), sem("silu_done"), sem("m_ready"), sem("m_hi"), sem("m_lo")
        ext_zeroed, hist_turned, hist_ready, ext_ready = sem("ext_zeroed"), sem("hist_turned"), sem("hist_ready"), sem("ext_ready")
        ext_turned, pool_out_ready, win_dve, win_pool = sem("ext_turned"), sem("pool_out_ready"), sem("win_dve"), sem("win_pool")
        dif_early, dif_ready, win_read = sem("dif_early"), sem("dif_ready"), sem("win_read")
        pool_first = sem("pool_first")
        y_turned, y_ready_act, y_ready_dve = sem("y_turned"), sem("y_ready_act"), sem("y_ready_dve")
        y_stored, out_stored = sem("y_stored"), sem("out_stored")

        block = ctx.enter_context(nc.Block())

        @block.sync
        def _(sp):
            rows = ab_w_in[0].rearrange("(k p) n -> p k n", p=P)
            out_rows = ab_w_out[0]

            def raw_free(m):
                if m >= NRAW:
                    sp.wait_ge(w_lo, m - NRAW + 1)

            def tiles(m, n=UNIT):
                return raw[:, m % NRAW, 0:n]

            for t, (t0, n) in enumerate(TILES):
                src = x_prompt[0, t0:t0 + n, :] if t0 < SEQ else x_sample[0]
                sp.dma_start(x_tok[0:n, t, :], src).then_inc(x_loaded[t], 16)
            for j in range(4):
                m = U_IN + j
                raw_free(m)
                sp.dma_start(tiles(m).rearrange("p (k n) -> p k n", k=2), rows[:, 2 * j:2 * j + 2, AW:2 * AW])\
                    .then_inc(w_loaded[m % NRAW], 16)
            qo = 2 * AW
            ko, vo = qo + NQ * HD, qo + NQ * HD + NKV * HD
            for j, c in enumerate((vo, ko)):
                m = U_IN + 4 + j
                raw_free(m)
                sp.dma_start(tiles(m).rearrange("p (k n) -> p k n", k=KC), rows[:, :, c:c + P])\
                    .then_inc(w_loaded[m % NRAW], 16)
            for t in range(4):
                m = U_IN + 6 + t
                raw_free(m)
                for g in range(NKV):
                    c = qo + (4 * g + t) * HD
                    sp.dma_start(tiles(m).rearrange("p (k g n) -> p k g n", k=KC, g=NKV)[:, :, g, :],
                                 rows[:, :, c:c + HD]).then_inc(w_loaded[m % NRAW], 16)
            for t in range(4):
                m = U_IN + 10 + t
                raw_free(m)
                sp.dma_start(tiles(m).rearrange("p (k n) -> p k n", k=KC), rows[:, :, t * P:(t + 1) * P])\
                    .then_inc(w_loaded[m % NRAW], 16)
            for d in range(KC):
                m = U_OUT + d
                raw_free(m)
                dst = tiles(m).rearrange("p (k n) -> p k n", k=KC)
                cols = slice(d * P, (d + 1) * P)
                sp.dma_start(dst[:, 0:4, :], out_rows[0:AW, cols].rearrange("(k p) n -> p k n", p=P))\
                    .then_inc(w_loaded[m % NRAW], 16)
                for g in range(NKV):
                    r = AW + g * 4 * HD
                    sp.dma_start(dst[g * HD:(g + 1) * HD, 4:8, :],
                                 out_rows[r:r + 4 * HD, cols].rearrange("(t d) n -> d t n", t=4))\
                        .then_inc(w_loaded[m % NRAW], 16)

            def load_ffn(layer):
                w_in = ffn_w_in[layer].rearrange("(k p) n -> p k n", p=P)
                w_out = ffn_w_out[layer].rearrange("(c p) n -> p c n", p=P)
                base = U_FI[layer]
                with sp.Fori(0, FC // 2) as i:
                    for j in range(4):
                        m = base + j
                        sp.wait_ge(w_lo, i * 4 + (m - NRAW + 1))
                        col = i * (2 * P) + ((j // 2) * P + (j % 2) * DFF)
                        sp.dma_start(tiles(m).rearrange("p (k n) -> p k n", k=KC), w_in[:, :, bass.ds(col, P)])\
                            .then_inc(w_loaded[m % NRAW], 16)
                base = U_FO[layer]
                with sp.Fori(0, KC // 2) as i:
                    for j in range(8):
                        m = base + j
                        sp.wait_ge(w_lo, i * 8 + (m - NRAW + 1))
                        a, b = PIECES[j % 4]
                        col = i * (2 * P) + (j // 4) * P
                        sp.dma_start(tiles(m, (b - a) * P).rearrange("p (c n) -> p c n", n=P),
                                     w_out[:, a:b, bass.ds(col, P)]).then_inc(w_loaded[m % NRAW], 16)

            load_ffn(0)
            for j, g in enumerate(GROUPS):
                m = U_C + j
                raw_free(m)
                sp.dma_start(tiles(m, 4 * P).rearrange("p (k n) -> p k n", k=2),
                             c_w[0, g].rearrange("(k p) n -> p k n", p=P)).then_inc(w_loaded[m % NRAW], 16)
            load_ffn(1)
            for t, (t0, n) in enumerate(TILES):
                if t % 2 == 0:
                    sp.wait_ge(y_ready_act, t // 2 + 1)
                else:
                    sp.wait_ge(y_ready_dve, t // 2 + 1)
                dst = y_p[0, t0:t0 + n, :] if t0 < SEQ else y_s[0]
                sp.dma_start(dst, y_tok[0:n, t, :]).then_inc(y_stored, 16)
            sp.wait_ge(y_stored, 16 * NT)

        @block.tensor
        def _(pe):
            def product(out, wh, wl, xh, xl, first, last):
                pe.matmul(out, wh, xh, start=first, stop=False)
                pe.matmul(out, wh, xl, start=False, stop=False)
                return pe.matmul(out, wl, xh, start=False, stop=last)

            def both_halves(bank, m, tile, hi, lo, k, first, last):
                s = m % NSPLIT
                wh, wl = whi[:, s, tile * P:(tile + 1) * P], wlo[:, s, tile * P:(tile + 1) * P]
                for b in range(2):
                    c = slice(b * HALF, (b + 1) * HALF)
                    mm = product(flat(bank + b, 0, HALF), wh, wl, hi[:, k, c], lo[:, k, c], first, last)
                return mm

            def sum_squares(n, acc):
                for t in range(NT):
                    c = t * P if t < NT - 1 else TOK - P
                    mm = pe.matmul(flat(6, t, 1), acc[:, c:c + P], ones[:, :], start=True, stop=True)
                mm.then_inc(sum_ready, 1)

            def spread(n):
                pe.wait_ge(rstd_ready, n + 1)
                for t, (t0, w) in enumerate(TILES):
                    if n == 0:
                        lhs, rhs = rstd[0:w, t:t + 1].broadcast_to([w, P]), ident[0:w, 0:w]
                    else:
                        lhs, rhs = rstd[:, t:t + 1].broadcast_to([P, P]), ident[:, P - w:P]
                    mm = pe.matmul(flat(6, P + t0, w), lhs, rhs, start=True, stop=True)
                mm.then_inc(rstd_spread, 1)

            pe.wait_ge(ident_loaded, 16)
            pe.wait_ge(gains_loaded, 32)
            pe.transpose(flat(7, 0, 72), gain_rows[:, :], ident[0:72, 0:72]).then_inc(gains_turned, 1)
            for k in range(KC):
                if k >= 4:
                    pe.wait_ge(h_first, k - 3)
                if k == 3:
                    pe.wait_ge(gains_ready, 1)
                for t, (t0, n) in enumerate(TILES):
                    if k == 0:
                        pe.wait_ge(x_loaded[t], 16)
                    mm = pe.transpose(flat(2 * (k % 4), t0, n), x_tok[0:n, t, k * P:(k + 1) * P], ident[0:n, 0:n])
                mm.then_inc(x_turned, 1)
            pe.wait_ge(ws_loaded, 16)
            pe.wait_ge(h_first, 5)
            for a in range(AH):
                mm = pe.transpose(flat(0, a * P, P), ws[:, a, :], ident[:, :])
            mm.then_inc(ws_turned, 1)
            pe.wait_ge(kc_loaded, 16)
            pe.transpose(flat(1, 0, CHUNK), k_cache[:, :], ident[0:CHUNK, 0:CHUNK]).then_inc(kc_turned, 1)
            pe.wait_ge(h_first, KC)
            spread(0)

            pe.wait_ge(wm_ready, 1)
            pe.wait_ge(kc_ready, 1)
            for j in range(4):
                m = U_IN + j
                s = m % NSPLIT
                pe.wait_ge(w_lo, m + 1)
                pe.wait_ge(x_lo, 2 * j + 2)
                for t, (t0, n) in enumerate(TILES):
                    for c in range(2):
                        k = 2 * j + c
                        mm = product(flat(t, 0, AW, n), xhi[:, k, t0:t0 + n], xlo[:, k, t0:t0 + n],
                                     whi[:, s, c * AW:(c + 1) * AW], wlo[:, s, c * AW:(c + 1) * AW],
                                     k == 0, k == KC - 1)
                mm.then_inc(w_used, 1)
            m = U_IN + 4
            s = m % NSPLIT
            pe.wait_ge(w_lo, m + 1)
            for t, (t0, n) in enumerate(TILES):
                if t == NT - 1:
                    pe.wait_ge(va_gelu, NT)
                out = flat(5, t * P, P) if t < NT - 1 else flat(4, 0, P, n)
                for k in range(KC):
                    mm = product(out, xhi[:, k, t0:t0 + n], xlo[:, k, t0:t0 + n],
                                 whi[:, s, k * P:(k + 1) * P], wlo[:, s, k * P:(k + 1) * P], k == 0, k == KC - 1)
            mm.then_inc(w_used, 1)
            for r, bank in enumerate((6, 0, 2, 4, 6)):
                m = U_IN + 5 + r
                pe.wait_ge(w_lo, m + 1)
                if r == 3:
                    pe.wait_ge(v_evacuated, 4)
                if r == 4:
                    pe.wait_ge(rope_cosined, 1)
                for k in range(KC):
                    mm = both_halves(bank, m, k, xhi, xlo, k, k == 0, k == KC - 1)
                mm.then_inc(w_used, 1)
            pe.wait_ge(va_ready, NT)
            for a in range(AH):
                bank = 2 * (a % 2)
                if a < 2:
                    pe.wait_ge(rope_cosined, a + 2)
                else:
                    pe.wait_ge(gate_biased, a - 1)
                for t, (t0, n) in enumerate(TILES):
                    mm = pe.matmul(flat(bank, t0, n), va[0:n, t, a * P:(a + 1) * P], wm_t[0:n, a, 0:n],
                                   start=True, stop=True)
                mm.then_inc(gate_done, 1)
            pe.wait_ge(rope_cosined, 4)
            pe.wait_ge(rope_done, 1)
            pe.transpose(flat(5, 0, P), k_r[:, SEQ - P:SEQ], ident[:, :])
            pe.transpose(flat(5, P, P, DEC), k_r[:, SEQ:TOK], ident[:, :]).then_inc(k_turned, 1)

            def scores(c):
                bank = 2 + 2 * (c % 2)
                if c == 0:
                    pe.wait_ge(rope_done, 5)
                    pe.wait_ge(gate_biased, 4)
                if c == 1:
                    pe.wait_ge(k_out_ready, 1)
                if c >= 2:
                    pe.wait_ge(shifted, NKV * (c - 1))
                if c == NCH:
                    pe.wait_ge(k_s_ready, 1)
                    pe.wait_ge(kc_ready, 1)
                    for g in range(NKV):
                        r = slice(g * HD, (g + 1) * HD)
                        mm = pe.matmul(flat(bank + g, 0, P), q_r[r, 4 * SEQ:4 * TOK], k_s[r, :], start=True, stop=True)
                else:
                    for g in range(NKV):
                        r = slice(g * HD, (g + 1) * HD)
                        for j in range(2):
                            col = j * P
                            lhs = q_r[r, 4 * CHUNK * c + j * P:4 * CHUNK * c + (j + 1) * P]
                            if c % 2:
                                mm = pe.matmul(flat(bank + g, col, P), lhs, k_r[r, (c - 1) * CHUNK:(c + 1) * CHUNK],
                                               start=True, stop=True)
                                continue
                            mm = pe.matmul(flat(bank + g, col, CHUNK), lhs, k_r[r, c * CHUNK:(c + 1) * CHUNK],
                                           start=True, stop=True)
                            if c:
                                mm = pe.matmul(flat(bank + g, col + CHUNK, CHUNK), lhs, k_r[r, (c - 1) * CHUNK:c * CHUNK],
                                               start=True, stop=True)
                mm.then_inc(scored, 1)

            def turn_probs(c):
                if c == 0:
                    pe.wait_ge(rope_cosined, 5)
                else:
                    pe.wait_ge(p_t_ready, c)
                pe.wait_ge(p_ready, c + 1)
                w = CHUNK if c == 0 else P
                for j in range(2 if c == NCH else 4):
                    mm = pe.transpose(flat(6, j * P, P, w), s_sb[:, c % 2, j * P:j * P + w], ident[:, :])
                mm.then_inc(p_turned, 1)

            def weigh_values(c):
                pe.wait_ge(p_t_ready, c + 1)
                if c >= 1:
                    pe.wait_ge(att_lo, c)
                if c == 0:
                    pe.wait_ge(v_evacuated, 4)
                if c == NCH:
                    pe.wait_ge(vc_loaded, 16)
                    pe.wait_ge(set_gaps, 1)
                w = CHUNK if c == 0 else P
                for g in range(NKV):
                    cols = slice(g * HD, (g + 1) * HD)
                    v = v_s[:, cols] if c == NCH else v_t[:, c // 2, cols] if c % 2 else v_even[0:w, c // 2, cols]
                    n = P if c == NCH else 2 * P
                    mm = pe.matmul(ps[g * HD:(g + 1) * HD, 7 * 512:7 * 512 + n], v, p_t[0:w, g * n:(g + 1) * n],
                                   start=True, stop=True)
                mm.then_inc(pv_done, 1)

            def u_step(n):
                t, k = divmod(n, KC)
                m = U_IN + 10 + t
                if k == 0:
                    pe.wait_ge(w_lo, m + 1)
                    if t == 0:
                        pe.wait_ge(gate_biased, 3)
                    else:
                        pe.wait_ge(u_evacuated, t)
                mm = both_halves(0, m, k, xhi, xlo, k, k == 0, k == KC - 1)
                if k == KC - 1:
                    mm.then_inc(w_used, 1)

            for i in range(NCH + 3):
                if i <= NCH:
                    scores(i)
                for n in range(3 * i, min(3 * i + 3, 4 * KC)):
                    u_step(n)
                if 1 <= i <= NCH + 1:
                    turn_probs(i - 1)
                if i >= 2:
                    weigh_values(i - 2)

            def mixer_out(m, j, i, first):
                pe.wait_ge(w_lo, i * 4 + (m + 1))
                for n, k in enumerate((4, 5, 6, 7, 0, 1, 2, 3)):
                    if n == 0:
                        pe.wait_ge(att_lo, NCH + 1)
                    if k < 4:
                        pe.wait_ge(ya_lo, k + 1)
                    mm = both_halves(OUT_BANKS[j], m, k, yhi, ylo, k, n == 0, n == KC - 1)
                mm.then_inc(w_used, 1)

            for j in range(4):
                mixer_out(U_OUT + j, j, 0, True)
            for j in range(4):
                pe.wait_ge(z_evacuated, j + 1)
                mixer_out(U_OUT + 4 + j, j, 0, False)

            def ffn_layer(layer, n_post):
                base = U_FI[layer]
                xb = 8 * (2 * layer + 1)
                for k in range(KC):
                    pe.wait_ge(x_lo, xb + k + 1)
                    for j in range(3):
                        if k == 0:
                            pe.wait_ge(w_lo, base + j + 1)
                        mm = both_halves(2 * j, base + j, k, xhi, xlo, k, k == 0, k == KC - 1)
                        if k == KC - 1:
                            mm.then_inc(w_used, 1)
                pe.wait_ge(pre_added, 8 * (n_post // 2 + 1))
                sum_squares(n_post + 1, acc_pre)
                spread(n_post + 1)
                pe.wait_ge(w_lo, base + 4)
                pe.wait_ge(r_ready, n_post + 2)
                for k in range(KC):
                    mm = both_halves(6, base + 3, k, xhi, xlo, k, k == 0, k == KC - 1)
                mm.then_inc(w_used, 1)
                with pe.Fori(1, FC // 2) as i:
                    for j in range(4):
                        pe.wait_ge(w_lo, i * 4 + (base + j + 1))
                        if j % 2 == 0:
                            pe.wait_ge(gu_scaled, i * 2 + (FC * layer + j // 2 - 1))
                        for k in range(KC):
                            mm = both_halves(2 * j, base + j, k, xhi, xlo, k, k == 0, k == KC - 1)
                        mm.then_inc(w_used, 1)
                pe.wait_ge(gu_scaled, FC * (layer + 1))
                base = U_FO[layer]
                with pe.Fori(0, KC // 2) as i:
                    for d in range(2):
                        pe.wait_ge(z_evacuated, i * 2 + (8 * (2 * layer + 1) + d - 1))
                        for j, (a, b) in enumerate(PIECES):
                            m = base + 4 * d + j
                            pe.wait_ge(w_lo, i * 8 + (m + 1))
                            pe.wait_ge(m_lo, FC * layer + b)
                            for c in range(a, b):
                                mm = both_halves(2 * d, m, c - a, mhi, mlo, c, c == 0, c == FC - 1)
                            mm.then_inc(w_used, 1)
                pe.wait_ge(acc_added, 8 * (2 * layer + 2))
                sum_squares(n_post + 2, acc_post)
                spread(n_post + 2)

            pe.wait_ge(acc_added, 8)
            sum_squares(1, acc_post)
            spread(1)
            ffn_layer(0, 1)

            pe.wait_ge(hist_loaded, 16)
            for k in range(KC):
                mm = pe.transpose(flat(0, 16 * k, HIST), hist[:, k * P:(k + 1) * P], ident[0:HIST, 0:HIST])
            mm.then_inc(hist_turned, 1)
            pe.wait_ge(pre_added, 16)
            sum_squares(4, acc_pre)
            spread(4)
            pe.wait_ge(ext_ready, KC)
            for b, c in ((2, EXP + SEQ - HIST), (4, EXT - HIST)):
                for k in range(KC):
                    mm = pe.transpose(flat(b, k * P, P, HIST), ext[:, k, c:c + HIST], ident[:, :])
            mm.then_inc(ext_turned, 1)
            for e in range(2 * len(GROUPS)):
                j, o = divmod(e, 2)
                g = GROUPS[j]
                m = U_C + j
                s = m % NSPLIT
                if o == 0:
                    pe.wait_ge(w_lo, m + 1)
                    pe.wait_ge(x_lo, 16 + 2 * (j + 1))
                bank = (0, 6, 2, 4)[e % 4]
                if e == 0:
                    pe.wait_ge(hist_ready, 1)
                if e == 2:
                    pe.wait_ge(pool_out_ready, 1)
                if e >= 4:
                    pe.wait_ge(z_evacuated, 16 + e - 3)
                for b in range(2):
                    c = slice(b * HALF, (b + 1) * HALF)
                    for k in range(2):
                        w = slice(k * 2 * P + o * P, k * 2 * P + (o + 1) * P)
                        mm = product(flat(bank + b, 0, HALF), whi[:, s, w], wlo[:, s, w],
                                     xhi[:, 2 * g + k, c], xlo[:, 2 * g + k, c], k == 0, k == 1)
                if o:
                    mm.then_inc(w_used, 1)
                else:
                    mm.then_inc(pool_first, 1)
            pe.wait_ge(acc_added, 24)
            sum_squares(5, acc_post)
            spread(5)
            ffn_layer(1, 5)

            for k in range(KC):
                pe.wait_ge(h_added, 24 + k + 1)
                if k == 0:
                    pe.wait_ge(r_ready, 8)
                for t in range(NT - 1):
                    mm = pe.transpose(flat(2 * t, k * P, P), h[:, k, t * P:(t + 1) * P], ident[:, :])
                    if k == KC - 1:
                        mm.then_inc(y_turned, 1)
            pe.wait_ge(y_ready_act, 1)
            for k in range(KC):
                mm = pe.transpose(flat(0, k * P, P, DEC), h[:, k, SEQ:TOK], ident[:, :])
            mm.then_inc(y_turned, 1)

        @block.scalar
        def _(act):
            def hi_part(m, i=0, step=0):
                if step:
                    act.wait_ge(w_loaded[m % NRAW], i * (16 * step // NRAW) + loaded(m))
                    act.wait_ge(w_used, i * step + (m - NSPLIT + 1))
                else:
                    act.wait_ge(w_loaded[m % NRAW], loaded(m))
                    if m >= NSPLIT:
                        act.wait_ge(w_used, m - NSPLIT + 1)
                n = unit_columns(m)
                act.activation(whi[:, m % NSPLIT, 0:n], raw[:, m % NRAW, 0:n], ACT.Copy).then_inc(w_hi, 1)

            def root(n):
                if n == 0:
                    act.wait_ge(x_squared, NT)
                    src = ssq[:, :]
                else:
                    act.wait_ge(sum_ready, n)
                    src = flat(6, 0, NT)
                act.activation(rms[:, :], src, ACT.Sqrt, scale=1.0 / D, bias=eps[:, :]).then_inc(rms_ready, 1)

            def keep_spread(n, dst):
                act.wait_ge(rstd_spread, n + 1)
                act.activation(dst[:, :], flat(6, P, TOK), ACT.Copy).then_inc(r_ready, 1)

            def warm(func):
                act.activation(warmed[:, :], eps[:, :], func)

            act.dma_start(ident[:, :], constants[:, 0:P]).then_inc(ident_loaded, 16)
            act.dma_start(gain_rows[0:64, :], norm_g.rearrange("l j (k p) -> (l j k) p", p=P)).then_inc(gains_loaded, 16)
            act.dma_start(gain_rows[64:72, :], c_scale[0].rearrange("(k p) -> k p", p=P)).then_inc(gains_loaded, 16)
            act.dma_start(ws[:, :, :], a_ws[0].rearrange("h i j -> i h j")).then_inc(ws_loaded, 16)
            act.dma_start(k_cache[:, :], cache_k[0, 0, WIN - CHUNK:WIN].rearrange("t g d -> t (g d)")).then_inc(kc_loaded, 16)
            act.dma_start(v_s[CHUNK:P, :], cache_v[0, 0, WIN - CHUNK:WIN].rearrange("t g d -> t (g d)")).then_inc(vc_loaded, 16)
            act.dma_start(cossin[:, :, :], constants[:, P:P + 2 * TOK].rearrange("p (a n) -> p a n", a=2)).then_inc(rope_loaded, 16)
            act.dma_start(ln_gb[:, 0, :], ln_g[0].partition_broadcast(P)).then_inc(ln_loaded, 16)
            act.dma_start(ln_gb[:, 1, :], ln_b[0].partition_broadcast(P)).then_inc(ln_loaded, 16)
            act.dma_start(bs_b[:, :, :].rearrange("p h i -> p (h i)"),
                          a_bs[0].rearrange("h i -> (h i)").partition_broadcast(P)).then_inc(bs_loaded, 16)
            act.dma_start(sinks[:, :], b_sinks[0].partition_broadcast(P)).then_inc(sinks_loaded, 16)

            act.wait_ge(set_up, 1)
            act.wait_ge(gains_turned, 1)
            act.activation(gains[:, :], flat(7, 0, 72), ACT.Copy).then_inc(gains_ready, 1)
            for t, (t0, n) in enumerate(TILES):
                act.wait_ge(x_loaded[t], 16)
                if t:
                    act.wait_ge(x_squared, t)
                act.activation(u_raw[0:n, 0:2, 0:512], x_tok[0:n, t, :].rearrange("p (a b) -> p a b", a=2), ACT.Square,
                               accum_out=ssq[0:n, t:t + 1]).then_inc(x_squared, 1)
            root(0)
            hi_part(0)
            keep_spread(0, r_pre)

            def hi_of_normed(phase, k, g):
                act.wait_ge(normed, k + 1)
                act.activation(xhi[:, k, :], tmp[:, k % 2, :], ACT.Copy, scale=g).then_inc(x_hi, 1)

            for k in range(KC):
                hi_of_normed(0, k, gain(0, 0, k))
                if k in (0, 3, 5):
                    hi_part((1, None, None, 2, None, 3)[k])
            hi_part(4)
            act.wait_ge(w_used, 4)
            for t, (t0, n) in enumerate(TILES):
                act.activation(va[0:n, t, :], flat(t, 0, AW, n), ACT.Gelu_apprx_tanh).then_inc(va_gelu, 1)
            for m in (5, 6, 7):
                hi_part(m)
            act.wait_ge(va_bn, NT)
            act.activation(ln_rms[:, :], mean_var[:, :, 1], ACT.Sqrt, bias=eps[:, :]).then_inc(ln_rms_ready, 1)
            act.wait_ge(w_used, 5)
            bank5 = flat(5, 0, 512).rearrange("p (j n) -> p j n", j=4)
            act.activation(v_t[:, :, :], bank5, ACT.Copy).then_inc(v_evacuated, 1)
            act.activation(v_even[0:CHUNK, :, :], bank5[0:CHUNK], ACT.Copy).then_inc(v_evacuated, 1)
            act.activation(v_even[CHUNK:P, 1:4, :], bank5[CHUNK:P, 0:3, :], ACT.Copy).then_inc(v_evacuated, 1)
            act.activation(v_s[0:DEC, :], flat(4, 0, P, DEC), ACT.Copy).then_inc(v_evacuated, 1)
            for m in range(8, 14):
                hi_part(m)
            act.wait_ge(k_turned, 1)
            act.activation(k_out[:, 0, :], flat(5, 0, P), ACT.Copy)
            act.activation(k_out[0:DEC, 1, :], flat(5, P, P, DEC), ACT.Copy).then_inc(k_out_ready, 1)

            def exps(c):
                w = CHUNK if c == 0 else P
                n = 2 if c == NCH else 4
                s = s_sb[:, c % 2, 0:n * P].rearrange("p (c s) -> p c s", c=n)[:, :, 0:w]
                act.wait_ge(sink_shifted, c + 1)
                act.activation(den[:, c % 2, 0:n], sunk[:, c % 2, 0:n], ACT.Exp)
                act.activation(s, s, ACT.Exp).then_inc(exp_done, 1)

            def keep_turned(c):
                act.wait_ge(p_turned, c + 1)
                if c >= 1:
                    act.wait_ge(pv_done, c)
                w = CHUNK if c == 0 else P
                n = (2 if c == NCH else 4) * P
                act.activation(p_t[0:w, 0:n], flat(6, 0, n, w), ACT.Copy).then_inc(p_t_ready, 1)

            def attended(c):
                n = DEC if c == NCH else CHUNK
                return slice(c * CHUNK, c * CHUNK + n), flat(7, 0, 4 * n).rearrange("p (t q) -> p t q", t=4)

            def attended_hi(c):
                act.wait_ge(pv_done, c + 1)
                cols, src = attended(c)
                act.activation(yhi[:, 4:8, cols], src, ACT.Copy).then_inc(att_hi, 1)

            def evacuate_u(t, func):
                act.wait_ge(w_used, U_IN + 11 + t)
                mm = act.activation(halves(u_raw[:, t, :]), pair(0), func)
                mm.then_inc(u_evacuated, 1)

            for i in range(NCH + 3):
                if i <= NCH:
                    exps(i)
                if i == 2:
                    evacuate_u(0, ACT.Copy)
                    hi_part(14)
                if i == 5:
                    evacuate_u(1, ACT.Copy)
                    hi_part(15)
                if i == 7:
                    evacuate_u(2, ACT.Copy)
                    hi_part(16)
                if 1 <= i <= NCH + 1:
                    keep_turned(i - 1)
                if i >= 2:
                    attended_hi(i - 2)
                if i == NCH + 1:
                    act.wait_ge(u_evacuated, 3)
                    for t in range(3):
                        act.activation(u_raw[:, t, :], u_raw[:, t, :], ACT.Gelu_apprx_tanh).then_inc(u_gelu, 1)
            act.wait_ge(w_used, U_IN + 14)
            act.activation(halves(u_raw[:, 3, :]), pair(0), ACT.Gelu_apprx_tanh).then_inc(u_gelu, 1)
            hi_part(17)
            for t in range(AH):
                act.wait_ge(ya_ready, t + 1)
                act.activation(yhi[:, t, :], gated[:, t, :], ACT.Copy).then_inc(ya_hi, 1)

            def evacuate_z(s, n, chunk, i, step, bank, used, scale=1.0):
                act.wait_ge(w_used, i * (4 * step) + used) if step else act.wait_ge(w_used, used)
                act.activation(halves(z[:, bass.ds(i * step + chunk, 1), :].rearrange("p o n -> p (o n)"))
                               if step else halves(z[:, chunk, :]), pair(bank), ACT.Copy, scale=scale)
                if step:
                    act.wait_ge(acc_added, i * step + (8 * s + n - 1))
                elif 8 * s + n >= 2:
                    act.wait_ge(acc_added, 8 * s + n - 1)
                act.activation(halves(tmp2[:, n % 2, :]), pair(bank), ACT.Square, scale=scale).then_inc(z_evacuated, 1)

            for d in range(KC):
                evacuate_z(0, d, d, 0, 0, OUT_BANKS[d % 4], U_OUT + d + 1)
                if d < KC - 1:
                    hi_part(U_OUT + 4 + d)

            def residual(s, split, late):
                warm(ACT.Sqrt)
                root(2 * s + 1)
                keep_spread(2 * s + 1, r_post)
                for k in range(KC):
                    act.wait_ge(h_added, 8 * s + k + 1)
                    if split is not None:
                        act.activation(xhi[:, k, :], h[:, k, :], ACT.Copy, scale=split(k)).then_inc(x_hi, 1)
                    if k == 0:
                        act.activation(acc_pre[:, :], h[:, k, :], ACT.Square).then_inc(h_squared, 1)
                    else:
                        if k >= 3:
                            act.wait_ge(pre_added, 8 * s + k - 1)
                        act.activation(tmp2[:, k % 2, :], h[:, k, :], ACT.Square).then_inc(h_squared, 1)
                    if k == 4 and late is not None:
                        hi_part(late)

            def ffn_layer(layer, n_post):
                root(n_post + 1)
                keep_spread(n_post + 1, r_pre)
                warm(ACT.Silu)
                act.wait_ge(out_stored, 16 * MIXER_STORES[layer])
                base = U_FI[layer]

                def tiles_pair(i, following, i2, step2):
                    for f in range(2):
                        act.wait_ge(gu_scaled, i * 2 + (FC * layer + f + 1))
                        act.activation(tmp2[:, 0, :], tmp[:, 0, :], ACT.Silu).then_inc(silu_done, 1)
                        hi_part(following + 2 * f, i2, step2)
                        act.wait_ge(m_ready, i * 2 + (FC * layer + f + 1))
                        act.activation(mhi[:, bass.ds(i * 2 + f, 1), :].rearrange("p o n -> p (o n)"), tmp2[:, 1, :],
                                       ACT.Copy).then_inc(m_hi, 1)
                        hi_part(following + 2 * f + 1, i2, step2)

                with act.Fori(0, FC // 2 - 1) as i:
                    tiles_pair(i, base + 4, i, 4)
                tiles_pair(FC // 2 - 1, U_FO[layer], 0, 0)
                base = U_FO[layer]
                s = 2 * layer + 1

                def chunks_pair(i, last):
                    for d in range(2):
                        for j in range(4):
                            m = base + 4 * d + j + 4
                            if not last:
                                hi_part(m, i, 8)
                            elif 8 * (KC // 2 - 1) + m < U_END and not (d == 1 and j == 3):
                                hi_part(8 * (KC // 2 - 1) + m)
                        if last:
                            n = KC - 2 + d
                            evacuate_z(s, n, n, 0, 0, 2 * d, base + 4 * n + 4)
                        else:
                            evacuate_z_loop(s, d, i, 2 * d, base + 4 * d + 4)

                def evacuate_z_loop(s, d, i, bank, used):
                    act.wait_ge(w_used, i * 8 + used)
                    act.activation(halves(z[:, bass.ds(i * 2 + d, 1), :].rearrange("p o n -> p (o n)")), pair(bank), ACT.Copy)
                    act.wait_ge(acc_added, i * 2 + (8 * s + d - 1))
                    act.activation(halves(tmp2[:, d, :]), pair(bank), ACT.Square).then_inc(z_evacuated, 1)

                with act.Fori(0, KC // 2 - 1) as i:
                    chunks_pair(i, False)
                chunks_pair(KC // 2 - 1, True)

            residual(0, lambda k: gain(0, 2, k), U_OUT + 11)
            ffn_layer(0, 1)

            residual(1, None, U_C + 3)
            act.wait_ge(hist_turned, 1)
            act.activation(ext[:, :, EXS - HIST:EXS], flat(0, 0, P).rearrange("p (k n) -> p k n", k=KC)[:, :, 0:HIST],
                           ACT.Copy).then_inc(hist_ready, 1)
            root(4)
            keep_spread(4, r_pre)
            for n, k in enumerate(POOL_ORDER):
                act.wait_ge(normed, KC + n + 1)
                g = gain(1, 0, k)
                act.activation(ext[:, k, EXP:EXP + SEQ], tmp[:, n % 2, 0:SEQ], ACT.Copy, scale=g)
                act.activation(ext[:, k, EXS:EXT], tmp[:, n % 2, SEQ:TOK], ACT.Copy, scale=g).then_inc(ext_ready, 1)
            act.wait_ge(ext_turned, 1)
            act.activation(pool_out[:, 0, :], flat(2, 0, D, HIST), ACT.Copy)
            act.activation(pool_out[:, 1, :], flat(4, 0, D, HIST), ACT.Copy).then_inc(pool_out_ready, 1)
            for j, g in enumerate(GROUPS):
                act.wait_ge(dif_ready, j + 1)
                act.activation(xhi[:, 2 * g:2 * g + 2, :], dif[:, j % 2, :, :], ACT.Copy).then_inc(x_hi, 2)
            for e in range(2 * len(GROUPS)):
                j, o = divmod(e, 2)
                c = 2 * GROUPS[j] + o
                bank = (0, 6, 2, 4)[e % 4]
                if o == 0:
                    act.wait_ge(pool_first, j + 1)
                else:
                    act.wait_ge(w_used, U_C + j + 1)
                act.activation(halves(z_pool[:, c, :]), pair(bank), ACT.Copy, scale=scale_c(c))
                act.wait_ge(acc_added, 16 + e - 1)
                act.activation(halves(tmp2[:, e % 2, :]), pair(bank), ACT.Square, scale=scale_c(c)).then_inc(z_evacuated, 1)
                if o and j < 3:
                    hi_part(U_FI[1] + j)
            residual(2, lambda k: gain(1, 2, k), U_FI[1] + 3)
            ffn_layer(1, 5)
            warm(ACT.Sqrt)
            root(7)
            keep_spread(7, r_post)
            for t, (t0, n) in enumerate(TILES):
                if t % 2 == 0:
                    act.wait_ge(y_turned, t + 1)
                    act.activation(y_tok[0:n, t, :], flat(0 if t == NT - 1 else 2 * t, 0, D, n), ACT.Copy)\
                        .then_inc(y_ready_act, 1)

        @block.vector
        def _(dve):
            def lo_part(m, i=0, step=0):
                dve.wait_ge(w_hi, i * step + (m + 1) if step else m + 1)
                s, n = m % NSPLIT, unit_columns(m)
                dve.tensor_tensor(wlo[:, s, 0:n], raw[:, m % NRAW, 0:n], whi[:, s, 0:n].bitcast(F32), ALU.subtract)\
                    .then_inc(w_lo, 1)

            def invert(n):
                dve.wait_ge(rms_ready, n + 1)
                dve.reciprocal(rstd[:, :], rms[:, :]).then_inc(rstd_ready, 1)

            dve.memset(wm_t[CHUNK:P, :, 0:CHUNK], 0.0)
            dve.memset(v_s[DEC:CHUNK, :], 0.0).then_inc(set_gaps, 1)
            for k in range(KC):
                dve.wait_ge(x_turned, k + 1)
                dve.tensor_copy(h[:, k, :], flat(2 * (k % 4), 0, TOK)).then_inc(h_first, 1)
            invert(0)
            lo_part(0)
            dve.wait_ge(ws_turned, 1)
            turned = flat(0, 0, 512).rearrange("p (h i) -> p h i", h=AH)
            dve.tensor_copy(wm_t[0:CHUNK, :, :], turned[0:CHUNK])
            dve.tensor_copy(wm_t[CHUNK:P, :, CHUNK:P], turned[CHUNK:P, :, CHUNK:P]).then_inc(wm_ready, 1)
            dve.wait_ge(kc_turned, 1)
            dve.tensor_copy(k_s[:, CHUNK:P], flat(1, 0, CHUNK)).then_inc(kc_ready, 1)

            def normalise(n, k):
                dve.tensor_tensor(tmp[:, n % 2, :], h[:, k, :], r_pre[:, :], ALU.mult).then_inc(normed, 1)

            dve.wait_ge(r_ready, 1)
            for k in range(KC + 1):
                if k < KC:
                    if k >= 2:
                        dve.wait_ge(x_lo, k - 1)
                    normalise(k, k)
                if k >= 1:
                    dve.wait_ge(x_hi, k)
                    dve.scalar_tensor_tensor(xlo[:, k - 1, :], tmp[:, (k - 1) % 2, :], gain(0, 0, k - 1),
                                             xhi[:, k - 1, :].bitcast(F32), ALU.mult, ALU.subtract).then_inc(x_lo, 1)
                if k in (1, 4, 6):
                    lo_part({1: 1, 4: 2, 6: 3}[k])
            lo_part(4)
            dve.wait_ge(sinks_loaded, 16)
            dve.tensor_copy(sink_p[0:CHUNK, :], sinks[0:CHUNK, 0:NQ:2])
            dve.tensor_copy(sink_p[CHUNK:P, :], sinks[CHUNK:P, 1:NQ:2])
            for a in range(4):
                op = dve.tensor_copy(sink_s[a * DEC:(a + 1) * DEC, :], sinks[a * DEC:(a + 1) * DEC, a:NQ:4])
            op.then_inc(sinks_ready, 1)
            for t, (t0, n) in enumerate(TILES):
                dve.wait_ge(va_gelu, t + 1)
                dve.bn_stats(stats[0:n, t, :], va[0:n, t, :]).then_inc(va_stats, 1)
            dve.wait_ge(set_stats, 1)
            for t, (t0, n) in enumerate(TILES):
                dve.wait_ge(va_stats, t + 1)
                dve.bn_aggr(mean_var[0:n, t, :], stats[0:n, t, :]).then_inc(va_bn, 1)
            for m in (5, 6):
                lo_part(m)
            dve.wait_ge(ln_rms_ready, 1)
            dve.reciprocal(ln_rstd[:, :], ln_rms[:, :]).then_inc(ln_rstd_ready, 1)
            dve.wait_ge(ln_rstd_ready, 1)
            for t, (t0, n) in enumerate(TILES):
                dve.tensor_scalar(va[0:n, t, :], va[0:n, t, :], mean_var[0:n, t, 0:1], ln_rstd[0:n, t:t + 1],
                                  ALU.subtract, ALU.mult).then_inc(va_normed, 1)
            lo_part(7)

            half = ROPE // 2
            swap = [*range(half, ROPE), *range(half), *range(ROPE, 32)]

            def rope_parts(r):
                dve.wait_ge(w_used, U_IN + 6 + r)
                if r >= 2:
                    dve.wait_ge(rope_done, r - 1)
                elif r == 0:
                    dve.wait_ge(x_lo, KC)
                src = pair((6, 0, 2, 4, 6)[r])
                dve.stream_shuffle(halves(tmp[:, r % 2, :]), src, swap).then_inc(rope_swapped, 1)
                dve.tensor_tensor(halves(tmp2[:, r % 2, :]), src, halves(cossin[:, 0, :]), ALU.mult).then_inc(rope_cosined, 1)

            def rope_sum(r):
                dve.wait_ge(rope_sined, r + 1)
                dve.wait_ge(rope_cosined, r + 1)
                a, b = tmp[:, r % 2, :], tmp2[:, r % 2, :]
                if r == 0:
                    dve.tensor_tensor(k_r[:, :], a, b, ALU.add).then_inc(rope_done, 1)
                    return
                t = r - 1
                by_chunk = lambda ap: ap[:, 0:SEQ].rearrange("p (c q) -> p c q", c=NCH)
                dst = q_r[:, 0:4 * SEQ].rearrange("p (c t q) -> p c t q", c=NCH, t=4)[:, :, t, :]
                dve.tensor_tensor(dst, by_chunk(a), by_chunk(b), ALU.add)
                dve.tensor_tensor(q_r[:, 4 * SEQ + t * DEC:4 * SEQ + (t + 1) * DEC], a[:, SEQ:TOK], b[:, SEQ:TOK],
                                  ALU.add).then_inc(rope_done, 1)

            dve.wait_ge(rope_loaded, 16)
            for r in range(5):
                rope_parts(r)
                lo_part(8 + r)
                rope_sum(r)

            def bias_gate(a):
                dve.wait_ge(gate_done, a + 1)
                bank = 2 * (a % 2)
                dve.tensor_tensor(gated[:, a, 0:SEQ].rearrange("p (n i) -> p n i", i=P),
                                  flat(bank, 0, SEQ).rearrange("p (n i) -> p n i", i=P),
                                  bs_b[:, a:a + 1, :].broadcast_to([P, SEQ // P, P]), ALU.add)
                dve.tensor_tensor(gated[:, a, SEQ:TOK], flat(bank, SEQ, DEC), bs_b[:, a, 0:DEC], ALU.add)\
                    .then_inc(gate_biased, 1)

            dve.wait_ge(bs_loaded, 16)
            for a in range(AH):
                bias_gate(a)
            lo_part(13)

            def shift(c):
                n, b = (2, c % 2) if c == NCH else (4, c % 2)
                w = CHUNK if c == 0 else P
                sink = sink_s[:, :] if c == NCH else sink_p[:, :]
                npg = n // NKV
                dst = s_sb[:, b, 0:n * P].rearrange("p (c s) -> p c s", c=n)[:, :, 0:w]
                srcs = [flat(2 + 2 * (c % 2) + g, 0, npg * P).rearrange("p (c s) -> p c s", c=npg)[:, :, 0:w]
                        for g in range(NKV)]
                scale = SCALE
                dve.wait_ge(scored, c + 1)
                if c >= 2:
                    dve.wait_ge(p_turned, c - 1)
                if c == NCH:
                    for g in range(NKV):
                        dve.scalar_tensor_tensor(dst[:, g, :], srcs[g][:, 0, :], SCALE, mask_s[:, :],
                                                 ALU.mult, ALU.add).then_inc(s_masked, 1)
                    dve.wait_ge(s_masked, NKV)
                    srcs, scale = [dst[:, g:g + 1, :] for g in range(NKV)], 1.0
                for g in range(NKV):
                    dve.tensor_reduce(top[:, b, g * npg:(g + 1) * npg], srcs[g], AX.X, ALU.max).then_inc(topped, 1)
                dve.wait_ge(topped, NKV * (c + 1))
                dve.scalar_tensor_tensor(peak[:, b, 0:n], top[:, b, 0:n], scale, sink, ALU.mult, ALU.max).then_inc(peaked, 1)
                dve.wait_ge(peaked, c + 1)
                for g in range(NKV):
                    part = slice(g * npg, (g + 1) * npg)
                    dve.scalar_tensor_tensor(dst[:, part, :], srcs[g], scale,
                                             peak[:, b, part].unsqueeze(2).broadcast_to([P, npg, w]),
                                             ALU.mult, ALU.subtract).then_inc(shifted, 1)
                dve.tensor_tensor(sunk[:, b, 0:n], sink, peak[:, b, 0:n], ALU.subtract).then_inc(sink_shifted, 1)

            def denominator(c):
                n, b = (2, c % 2) if c == NCH else (4, c % 2)
                w = CHUNK if c == 0 else P
                p = s_sb[:, b, 0:n * P].rearrange("p (c s) -> p c s", c=n)[:, :, 0:w]
                dve.wait_ge(exp_done, c + 1)
                dve.tensor_reduce(den2[:, b, 0:n], p, AX.X, ALU.add).then_inc(summed, 1)
                dve.wait_ge(summed, c + 1)
                dve.tensor_tensor(den2[:, b, 0:n], den2[:, b, 0:n], den[:, b, 0:n], ALU.add).then_inc(den_ready, 1)
                dve.wait_ge(den_ready, c + 1)
                dve.reciprocal(rden[:, b, 0:n], den2[:, b, 0:n]).then_inc(rden_ready, 1)

            def attended_lo(c):
                n = DEC if c == NCH else CHUNK
                cols, src = slice(c * CHUNK, c * CHUNK + n), flat(7, 0, 4 * n).rearrange("p (t q) -> p t q", t=4)
                dve.wait_ge(att_hi, c + 1)
                dve.tensor_tensor(ylo[:, 4:8, cols], src, yhi[:, 4:8, cols].bitcast(F32), ALU.subtract).then_inc(att_lo, 1)

            dve.wait_ge(sinks_ready, 1)
            dve.wait_ge(set_sample, 1)
            for i in range(NCH + 3):
                if i <= NCH:
                    shift(i)
                if i == 2:
                    lo_part(14)
                if i == 5:
                    lo_part(15)
                if i == 7:
                    lo_part(16)
                if i <= NCH:
                    denominator(i)
                if i >= 2:
                    attended_lo(i - 2)
            lo_part(17)
            for t in range(AH):
                dve.wait_ge(ya_hi, t + 1)
                dve.tensor_tensor(ylo[:, t, :], gated[:, t, :], yhi[:, t, :].bitcast(F32), ALU.subtract).then_inc(ya_lo, 1)

            def add_squares(s, n, slot, i=0, step=0):
                if step:
                    dve.wait_ge(z_evacuated, i * step + (8 * s + n + 1))
                    dve.wait_ge(acc_added, i * step + (8 * s + n))
                else:
                    dve.wait_ge(z_evacuated, 8 * s + n + 1)
                    if 8 * s + n:
                        dve.wait_ge(acc_added, 8 * s + n)
                dve.tensor_tensor(acc_post[:, :], acc_post[:, :], tmp2[:, slot, :], ALU.add).then_inc(acc_added, 1)

            dve.wait_ge(acc_zeroed, 1)
            for d in range(KC):
                if d < KC - 1:
                    lo_part(U_OUT + 4 + d)
                add_squares(0, d, d % 2)

            def residual(s, layer, post, split, late):
                invert(2 * s + 1)
                dve.wait_ge(r_ready, 2 * s + 2)

                def lo(k):
                    dve.wait_ge(x_hi, split[0] + k + 1)
                    dve.scalar_tensor_tensor(xlo[:, k, :], h[:, k, :], split[1](k), xhi[:, k, :].bitcast(F32),
                                             ALU.mult, ALU.subtract).then_inc(x_lo, 1)

                for k in range(KC):
                    if 8 * s + k >= 2:
                        dve.wait_ge(h_added, 8 * s + k - 1)
                    dve.tensor_tensor(tmp[:, k % 2, :], (z_pool if s == 2 else z)[:, k, :], r_post[:, :], ALU.mult).then_inc(z_scaled, 1)
                    if k and split:
                        lo(k - 1)
                    dve.wait_ge(z_scaled, 8 * s + k + 1)
                    dve.scalar_tensor_tensor(h[:, k, :], tmp[:, k % 2, :], gain(layer, post, k), h[:, k, :],
                                             ALU.mult, ALU.add).then_inc(h_added, 1)
                    if k == 5 and late is not None:
                        lo_part(late)
                if split:
                    lo(KC - 1)

            def ffn_layer(layer, n_post):
                invert(n_post + 1)
                dve.wait_ge(r_ready, n_post + 2)
                dve.wait_ge(out_stored, 16 * MIXER_STORES[layer])
                base = U_FI[layer]
                fb = FC * layer

                def tiles_pair(i, following, i2, step2, looped):
                    for f in range(2):
                        at = (lambda v: i * 2 + (fb + f + v))
                        gate, up = pair(4 * f), pair(4 * f + 2)
                        r = halves(r_pre[:, :])
                        dve.wait_ge(w_used, i * 4 + (base + 2 * f + 2))
                        dve.wait_ge(m_lo, at(0))
                        dve.tensor_tensor(halves(tmp[:, 0, :]), gate, r, ALU.mult)
                        dve.tensor_tensor(halves(tmp[:, 1, :]), up, r, ALU.mult).then_inc(gu_scaled, 1)
                        lo_part(following + 2 * f, i2, step2)
                        dve.wait_ge(silu_done, at(1))
                        dve.tensor_tensor(tmp2[:, 1, :], tmp2[:, 0, :], tmp[:, 1, :], ALU.mult).then_inc(m_ready, 1)
                        dve.wait_ge(m_hi, at(1))
                        c = bass.ds(i * 2 + f, 1)
                        dve.tensor_tensor(mlo[:, c, :].rearrange("p o n -> p (o n)"), tmp2[:, 1, :],
                                          mhi[:, c, :].rearrange("p o n -> p (o n)").bitcast(F32), ALU.subtract)\
                            .then_inc(m_lo, 1)
                        lo_part(following + 2 * f + 1, i2, step2)

                with dve.Fori(0, FC // 2 - 1) as i:
                    tiles_pair(i, base + 4, i, 4, True)
                tiles_pair(FC // 2 - 1, U_FO[layer], 0, 0, False)
                base = U_FO[layer]
                s = 2 * layer + 1
                dve.wait_ge(acc_zeroed, s + 1)
                with dve.Fori(0, KC // 2 - 1) as i:
                    for d in range(2):
                        for j in range(4):
                            lo_part(base + 4 * d + j + 4, i, 8)
                        add_squares(s, d, d, i, 2)
                for d in range(2):
                    for j in range(4):
                        m = base + 8 * (KC // 2 - 1) + 4 * d + j + 4
                        if m < U_END and not (d == 1 and j == 3):
                            lo_part(m)
                    add_squares(s, KC - 2 + d, d)

            residual(0, 0, 1, (8, lambda k: gain(0, 2, k)), U_OUT + 11)
            ffn_layer(0, 1)
            residual(1, 0, 3, None, U_C + 3)

            invert(4)
            dve.wait_ge(r_ready, 5)
            for n, k in enumerate(POOL_ORDER):
                if n >= 2:
                    dve.wait_ge(ext_ready, n - 1)
                normalise(n, k)
            windows_dve = 0
            dve.wait_ge(hist_ready, 1)
            dve.wait_ge(ext_zeroed, 1)
            dve.wait_ge(inverse_loaded, 16)
            pool_count = 0
            for j, g in enumerate(GROUPS):
                w = POOLS[g]
                pairs = slice(2 * g, 2 * g + 2)
                if g < 2:
                    dve.wait_ge(ext_ready, max(POOL_ORDER.index(2 * g), POOL_ORDER.index(2 * g + 1)) + 1)
                    src, lead = ext[:, pairs, :], 1
                    for level in range(g + 1):
                        dst = win[0][level % 2][:, :, :]
                        if level:
                            dve.wait_ge(win_dve, windows_dve)
                        dve.tensor_tensor(dst[:, :, 2 * lead - 1:EXT], src[:, :, 2 * lead - 1:EXT],
                                          src[:, :, lead - 1:EXT - lead], ALU.add).then_inc(win_dve, 1)
                        windows_dve += 1
                        src, lead = dst, 2 * lead
                    dve.wait_ge(win_dve, windows_dve)
                    total = src
                else:
                    pool_count += g + 1
                    dve.wait_ge(win_pool, pool_count)
                    total = win[1][g % 2][:, :, :]
                if j >= 2:
                    dve.wait_ge(x_hi, 16 + 2 * (j - 1))
                out = dif[:, j % 2, :, :]
                dve.tensor_tensor(early[:, :, :], total[:, :, EXP:EXP + 16],
                                  inverse[:, g:g + 1, :].broadcast_to([P, 2, 16]), ALU.mult).then_inc(dif_early, 1)
                dve.scalar_tensor_tensor(out[:, :, 16:SEQ], total[:, :, EXP + 16:EXP + SEQ], 1.0 / w,
                                         ext[:, pairs, EXP + 16:EXP + SEQ], ALU.mult, ALU.subtract)
                dve.scalar_tensor_tensor(out[:, :, SEQ:TOK], total[:, :, EXS:EXT], 1.0 / w,
                                         ext[:, pairs, EXS:EXT], ALU.mult, ALU.subtract).then_inc(win_read, 1)
                dve.wait_ge(dif_early, j + 1)
                dve.tensor_tensor(out[:, :, 0:16], early[:, :, :], ext[:, pairs, EXP:EXP + 16], ALU.subtract)\
                    .then_inc(dif_ready, 1)
                dve.wait_ge(x_hi, 16 + 2 * (j + 1))
                dve.wait_ge(dif_ready, j + 1)
                dve.tensor_tensor(xlo[:, pairs, :], out, xhi[:, pairs, :].bitcast(F32), ALU.subtract).then_inc(x_lo, 2)
            dve.wait_ge(acc_zeroed, 3)
            for e in range(2 * len(GROUPS)):
                add_squares(2, e, e % 2)
                if e % 2 and e // 2 < 3:
                    lo_part(U_FI[1] + e // 2)
            residual(2, 1, 1, (24, lambda k: gain(1, 2, k)), U_FI[1] + 3)
            ffn_layer(1, 5)
            residual(3, 1, 3, None, None)
            for t in (1, 3):
                dve.wait_ge(y_turned, t + 1)
                dve.tensor_copy(y_tok[:, t, :], flat(2 * t, 0, D)).then_inc(y_ready_dve, 1)

        @block.gpsimd
        def _(pool):
            pool.memset(eps[:, :], EPS)
            pool.memset(ssq[:, :], 1.0)
            pool.memset(ones[:, :], 1.0).then_inc(set_up, 1)
            pool.memset(k_s[:, DEC:CHUNK], 0.0)
            pool.memset(mask_s[:, 0:DEC], 0.0)
            pool.memset(mask_s[:, CHUNK:P], 0.0)
            pool.memset(mask_s[:, DEC:CHUNK], MASKED).then_inc(set_sample, 1)
            pool.memset(mean_var[:, :, :], 1.0).then_inc(set_stats, 1)
            pool.memset(acc_post[:, :], 0.0).then_inc(acc_zeroed, 1)
            pool.wait_ge(ln_loaded, 32)
            for t, (t0, n) in enumerate(TILES):
                pool.wait_ge(va_normed, t + 1)
                pool.tensor_tensor(va[0:n, t, :], va[0:n, t, :], ln_gb[0:n, 0, :], ALU.mult).then_inc(va_scaled, 1)
            for t, (t0, n) in enumerate(TILES):
                pool.wait_ge(va_scaled, t + 1)
                pool.tensor_tensor(va[0:n, t, :], va[0:n, t, :], ln_gb[0:n, 1, :], ALU.add).then_inc(va_ready, 1)
            pool.wait_ge(va_ready, NT)
            pool.dma_start(av_s[0, 0].rearrange("t h c -> t (h c)"), va[0:DEC, NT - 1, :]).then_inc(out_stored, 16)
            pool.wait_ge(v_evacuated, 4)
            pool.dma_start(bv_p[0, 0].rearrange("t g d -> t (g d)"), v_t[:, 3, :]).then_inc(out_stored, 16)
            pool.dma_start(bv_s[0, 0].rearrange("t g d -> t (g d)"), v_s[0:DEC, :]).then_inc(out_stored, 16)
            for r in range(5):
                pool.wait_ge(rope_swapped, r + 1)
                pool.tensor_tensor(tmp[:, r % 2, :], tmp[:, r % 2, :], cossin[:, 1, :], ALU.mult).then_inc(rope_sined, 1)
                if r == 1:
                    pool.wait_ge(rope_done, 1)
                    pool.tensor_copy(k_s[:, 0:DEC], k_r[:, SEQ:TOK]).then_inc(k_s_ready, 1)
            pool.wait_ge(k_out_ready, 1)
            pool.dma_start(bk_p[0, 0].rearrange("t g d -> t (g d)"), k_out[:, 0, :]).then_inc(out_stored, 16)
            pool.dma_start(bk_s[0, 0].rearrange("t g d -> t (g d)"), k_out[0:DEC, 1, :]).then_inc(out_stored, 16)
            for c in range(NCH + 1):
                n, b = (2, c % 2) if c == NCH else (4, c % 2)
                w = CHUNK if c == 0 else P
                p = s_sb[:, b, 0:n * P].rearrange("p (c s) -> p c s", c=n)[:, :, 0:w]
                pool.wait_ge(rden_ready, c + 1)
                pool.tensor_tensor(p, p, rden[:, b, 0:n].unsqueeze(2).broadcast_to([P, n, w]), ALU.mult).then_inc(p_ready, 1)
            for t in range(AH):
                pool.wait_ge(u_gelu, t + 1)
                pool.wait_ge(gate_biased, t + 1)
                pool.tensor_tensor(gated[:, t, :], gated[:, t, :], u_raw[:, t, :], ALU.mult).then_inc(ya_ready, 1)

            def add_squares(s):
                pool.wait_ge(h_squared, 8 * s + 1)
                pool.sem_inc(pre_added, 1)
                for k in range(1, KC):
                    pool.wait_ge(h_squared, 8 * s + k + 1)
                    pool.wait_ge(pre_added, 8 * s + k)
                    pool.tensor_tensor(acc_pre[:, :], acc_pre[:, :], tmp2[:, k % 2, :], ALU.add).then_inc(pre_added, 1)

            def zero_sum(n):
                pool.wait_ge(sum_ready, n)
                pool.memset(acc_post[:, :], 0.0).then_inc(acc_zeroed, 1)

            add_squares(0)
            zero_sum(1)
            pool.wait_ge(w_used, U_FO[0] + 4 * KC)
            pool.dma_start(hist[:, :], state[0, 0]).then_inc(hist_loaded, 16)
            pool.dma_start(inverse[:, :, :].rearrange("p g n -> p (g n)"), constants[:, P + 2 * TOK:]).then_inc(inverse_loaded, 16)
            pool.memset(ext[:, :, 0:HIST], 0.0).then_inc(ext_zeroed, 1)
            zero_sum(3)
            add_squares(1)
            done = 0
            pool.wait_ge(hist_ready, 1)
            pool.wait_ge(ext_zeroed, 1)
            for g in (2, 3):
                pool.wait_ge(ext_ready, max(POOL_ORDER.index(2 * g), POOL_ORDER.index(2 * g + 1)) + 1)
                src, lead = ext[:, 2 * g:2 * g + 2, :], 1
                for level in range(g + 1):
                    dst = win[1][level % 2][:, :, :]
                    if level:
                        pool.wait_ge(win_pool, done)
                    if g == 3 and level == 0:
                        pool.wait_ge(win_read, GROUPS.index(2) + 1)
                    pool.tensor_tensor(dst[:, :, 2 * lead - 1:EXT], src[:, :, 2 * lead - 1:EXT],
                                       src[:, :, lead - 1:EXT - lead], ALU.add).then_inc(win_pool, 1)
                    done += 1
                    src, lead = dst, 2 * lead
            pool.wait_ge(pool_out_ready, 1)
            pool.dma_start(cp_p[0, 0], pool_out[:, 0, :]).then_inc(out_stored, 16)
            pool.dma_start(cp_s[0, 0], pool_out[:, 1, :]).then_inc(out_stored, 16)
            pool.wait_ge(out_stored, 16 * MIXER_STORES[1])
            add_squares(2)
            zero_sum(5)


_INS = ["x_prompt", "x_sample", "cache_b_k", "cache_b_v", "state_c_pool", "norm_g", "ab_w_in", "a_ln_g", "a_ln_b",
        "a_ws", "a_bs", "b_sinks", "ab_w_out", "c_w", "c_scale", "ffn_w_in", "ffn_w_out"]
_OUTS = [(1, SEQ, D), (1, DEC, D), (1, 1, WIN, NKV, HD), (1, 1, WIN, NKV, HD), (1, 1, HIST, D),
         (1, 1, DEC, NKV, HD), (1, 1, DEC, NKV, HD), (1, 1, HIST, D), (1, 1, DEC, AH, P)]


def kernel(**inputs):
    import numpy as _np
    import concourse.bacc as _bacc
    from concourse import mybir as _mybir
    from concourse.bass_utils import run_bass_kernel_spmd as _run

    nc = _bacc.Bacc("TRN2", target_bir_lowering=False, num_devices=1)
    arrays, args = {}, []
    named = [(name, _np.ascontiguousarray(inputs[name])) for name in _INS] + [("constants", shape_constants())]
    for name, a in named:
        arrays[f"in_{name}_dram"] = a
        args.append(nc.dram_tensor(f"in_{name}_dram", a.shape, _mybir.dt.from_np(a.dtype), kind="ExternalInput").ap())
    for i, shape in enumerate(_OUTS):
        args.append(nc.dram_tensor(f"out_{i}_dram", shape, _mybir.dt.float32, kind="ExternalOutput").ap())
    build(nc, *args)
    r = _run(nc, [arrays], core_ids=[0])
    return tuple(r.results[0][f"out_{i}_dram"] for i in range(len(_OUTS)))
```

```python
from contextlib import ExitStack

import concourse.bass as bass
import numpy as np
from concourse import mybir

F32 = mybir.dt.float32
F32R = mybir.dt.float32r
ACT = mybir.ActivationFunctionType
ALU = mybir.AluOpType
AX = mybir.AxisListType

P = 128
D = 1024
KC = D // P
SEQ, DEC, PAST = 512, 32, 1024
TOK = SEQ + DEC
HALF = TOK // 2
DFF = 2816
FC = DFF // P
CHUNK = 64
NCH = SEQ // CHUNK
HD = 64
AW = 512
AH = 4
NQ, NKV = 8, 2
ROPE, THETA = 16, 500000.0
WIN = 128
HIST = 15
POOLS = (2, 4, 8, 16)
EPS = 1e-6
MASKED = -1e30
SCALE = HD ** -0.5
TILES = [(t * P, P) for t in range(SEQ // P)] + [(SEQ, DEC)]
NT = len(TILES)
STEP = P - HIST
POOL_TILES = [(t * STEP, min(P, TOK - t * STEP)) for t in range(-(-SEQ // STEP))]
POOL_OUT = [(t0 + (HIST if t0 else 0), t0 + n) for t0, n in POOL_TILES]
TAIL, TAIL_SEQ = POOL_TILES[-1][1], SEQ - POOL_TILES[-1][0]
TAIL_OUT = TOK - POOL_OUT[-1][0]
POOL_AT = 512 - POOL_OUT[-1][0]
assert len(POOL_TILES) == NT and TAIL + HIST <= P
PIECES = ((0, 6), (6, 12), (12, 17), (17, 22))
MIXER_STORES = (5, 7)
OUT_BANKS = (2, 4, 6, 0)
GROUPS = (0, 1, 2, 3)

U_IN = 0
U_OUT = U_IN + 14
U_FI = (U_OUT + 8, U_OUT + 8 + 2 * FC + 4 * KC + 4)
U_FO = (U_FI[0] + 2 * FC, U_FI[1] + 2 * FC)
U_C = U_FO[0] + 4 * KC
U_END = U_FO[1] + 4 * KC
NRAW, NSPLIT = 2, 4
assert U_C + 4 == U_FI[1]
UNIT = 8 * P


def unit_columns(m):
    for base in U_FO:
        if base <= m < base + 4 * KC:
            a, b = PIECES[(m - base) % 4]
            return (b - a) * P
    return 4 * P if U_C <= m < U_C + 4 else UNIT


def unit_dmas(m):
    if U_IN + 6 <= m < U_IN + 10:
        return 2
    return 3 if U_OUT <= m < U_OUT + 8 else 1


def loaded(m):
    return 16 * sum(unit_dmas(j) for j in range(m % NRAW, m + 1, NRAW))


def shape_constants():
    pos = np.concatenate([np.arange(SEQ), PAST + np.arange(DEC)]).astype(np.float32)
    inv = np.float32(THETA) ** (-np.arange(ROPE // 2, dtype=np.float32) * np.float32(2.0) / np.float32(ROPE))
    ang = (pos[:, None] * inv.astype(np.float32)[None, :]).astype(np.float32)
    cos, sin = np.ones((P, TOK), np.float32), np.zeros((P, TOK), np.float32)
    for p in range(P):
        d = p % HD
        if d < ROPE:
            cos[p] = np.cos(ang[:, d % (ROPE // 2)])
            sin[p] = np.sin(ang[:, d % (ROPE // 2)]) * (-1.0 if d < ROPE // 2 else 1.0)
    return np.concatenate([np.eye(P, dtype=np.float32), cos, sin, pooling_matrices()], axis=1)


def pooling_matrices():
    i, j = np.arange(P)[None, :], np.arange(P)[:, None]
    row_at = np.concatenate([np.arange(TAIL_SEQ), np.arange(TAIL - TAIL_SEQ), np.arange(-HIST, 0)])[:, None]
    row_stream = (np.arange(TAIL + HIST) >= TAIL_SEQ)[:, None]
    col_at, col_stream = row_at[HIST:TAIL].T, row_stream[HIST:TAIL].T
    first, later, last = [], [], []
    for w in POOLS:
        inside = (j <= i) & (j > i - w)
        first.append(inside / np.minimum(i + 1, w) - (i == j))
        later.append((inside / w - (i == j))[:, HIST:])
        tail = np.zeros((P, TAIL_OUT))
        tail[:TAIL + HIST] = (row_stream == col_stream) * (((row_at <= col_at) & (row_at > col_at - w)) / w
                                                          - (row_at == col_at))
        last.append(tail)
    return np.concatenate(first + later + last, axis=1).astype(np.float32)


def build(nc, x_prompt, x_sample, cache_k, cache_v, state, norm_g, ab_w_in, ln_g, ln_b, a_ws, a_bs, b_sinks,
          ab_w_out, c_w, c_scale, ffn_w_in, ffn_w_out, constants,
          y_p, y_s, bk_p, bv_p, cp_p, bk_s, bv_s, cp_s, av_s):
    with ExitStack() as ctx:
        def sb(name, shape, dt=F32, scope=ctx):
            return scope.enter_context(nc.sbuf_tensor(name, shape, dt))

        def sem(name):
            return ctx.enter_context(nc.semaphore(name))

        ps = ctx.enter_context(nc.psum_tensor("ps", [P, 8 * 512], F32))

        def flat(b, c0, n, p=P):
            return ps[0:p, b * 512 + c0:b * 512 + c0 + n]

        def pair(b):
            return ps[:, b * 512:(b + 2) * 512].rearrange("p (b n) -> p b n", b=2)[:, :, 0:HALF]

        def halves(ap):
            return ap.rearrange("p (b n) -> p b n", b=2)

        h = sb("h", [P, KC, TOK])
        xhi = sb("xhi", [P, KC, TOK], F32R)
        with ExitStack() as used:
            xlo = sb("xlo", [P, KC, TOK], F32R, used)
        z = sb("z", [P, KC, TOK])
        raw = sb("raw", [P, NRAW, UNIT])
        whi = sb("whi", [P, NSPLIT, UNIT], F32R)
        wlo = sb("wlo", [P, NSPLIT, UNIT], F32R)
        r_post = sb("r_post", [P, TOK])
        r_pre = sb("r_pre", [P, TOK])
        acc_post = sb("acc_post", [P, TOK])
        acc_pre = sb("acc_pre", [P, TOK])
        tmp = sb("tmp", [P, 2, TOK])
        tmp2 = sb("tmp2", [P, 2, TOK])
        ident = sb("ident", [P, P])
        gains = sb("gains", [P, 72])
        ssq = sb("ssq", [P, NT])
        rms = sb("rms", [P, NT])
        rstd = sb("rstd", [P, NT])
        eps = sb("eps", [P, 1])
        ones = sb("ones", [P, 1])
        warmed = sb("warmed", [P, 1])

        def gain(layer, j, k):
            c = (layer * 4 + j) * KC + k
            return gains[:, c:c + 1]

        def scale_c(k):
            return gains[:, 64 + k:65 + k]

        with ExitStack() as ab:
            ab_sb = lambda name, shape, dt=F32: sb(name, shape, dt, ab)
            yhi = ab_sb("yhi", [P, KC, TOK], F32R)
            ylo = ab_sb("ylo", [P, KC, TOK], F32R)
            u_raw = ab_sb("u_raw", [P, AH, TOK])
            gated = ab_sb("gated", [P, AH, TOK])
            va = ab_sb("va", [P, NT, AW])
            ln_gb = ab_sb("ln_gb", [P, 2, AW])
            bs_b = ab_sb("bs_b", [P, AH, P])
            cossin = ab_sb("cossin", [P, 2, TOK])
            q_r = ab_sb("q_r", [P, 4 * TOK])
            k_r = ab_sb("k_r", [P, TOK])
            v_t = ab_sb("v_t", [P, 4, P])
            v_even = ab_sb("v_even", [P, 4, P])
            v_s = ab_sb("v_s", [P, P])
            k_s = ab_sb("k_s", [P, P])
            wm_t = ab_sb("wm_t", [P, AH, P])
            s_sb = ab_sb("s_sb", [P, 2, 512])
            p_t = ab_sb("p_t", [P, 512])
            k_out = ab_sb("k_out", [P, 2, P])
            mask_s = ab_sb("mask_s", [P, P])
            sinks = ab_sb("sinks", [P, NQ])
            sink_p = ab_sb("sink_p", [P, 4])
            sink_s = ab_sb("sink_s", [P, 2])
            top = ab_sb("top", [P, 2, 4])
            peak = ab_sb("peak", [P, 2, 4])
            sunk = ab_sb("sunk", [P, 2, 4])
            den = ab_sb("den", [P, 2, 4])
            den2 = ab_sb("den2", [P, 2, 4])
            rden = ab_sb("rden", [P, 2, 4])
            stats = ab_sb("stats", [P, NT, 6])
            mean_var = ab_sb("mean_var", [P, NT, 2])
            ln_rms = ab_sb("ln_rms", [P, NT])
            ln_rstd = ab_sb("ln_rstd", [P, NT])
        with ExitStack() as first:
            x_tok = sb("x_tok", [P, NT, D], F32, first)
            gain_rows = sb("gain_rows", [72, P], F32, first)
            ws = sb("ws", [P, AH, P], F32, first)
            k_cache = sb("k_cache", [CHUNK, P], F32, first)
        with ExitStack() as ffn:
            mhi = sb("mhi", [P, FC, TOK], F32R, ffn)
            mlo = sb("mlo", [P, FC, TOK], F32R, ffn)
        with ExitStack() as pool_scope:
            h_tok = sb("h_tok", [P, NT, D], F32, pool_scope)
            z_pool = sb("z_pool", [P, KC, TOK], F32, pool_scope)
            pool_out = sb("pool_out", [P, D], F32, pool_scope)
            gain_diag = sb("gain_diag", [P, KC, P], F32, pool_scope)
            band_first = sb("band_first", [P, 4, P], F32, pool_scope)
            band_later = sb("band_later", [P, 4, STEP], F32, pool_scope)
            band_last = sb("band_last", [P, 4, TAIL_OUT], F32, pool_scope)
            band_r = [sb(f"band_r{t}", [P, 4, b - a], F32, pool_scope) for t, (a, b) in enumerate(POOL_OUT)]
        with ExitStack() as end:
            y_tok = sb("y_tok", [P, NT, D], F32, end)

        w_loaded = [sem(f"w_loaded{i}") for i in range(NRAW)]
        w_hi, w_lo, w_used = sem("w_hi"), sem("w_lo"), sem("w_used")
        x_loaded = [sem(f"x_loaded{i}") for i in range(NT)]
        ident_loaded, gains_loaded, rope_loaded = sem("ident_loaded"), sem("gains_loaded"), sem("rope_loaded")
        ws_loaded, bs_loaded, ln_loaded = sem("ws_loaded"), sem("bs_loaded"), sem("ln_loaded")
        sinks_loaded, kc_loaded, vc_loaded = sem("sinks_loaded"), sem("kc_loaded"), sem("vc_loaded")
        hist_loaded, band_loaded = sem("hist_loaded"), sem("band_loaded")
        set_up, set_sample, set_stats, set_gaps = sem("set_up"), sem("set_sample"), sem("set_stats"), sem("set_gaps")
        gains_turned, gains_ready = sem("gains_turned"), sem("gains_ready")
        x_turned, h_first, x_squared = sem("x_turned"), sem("h_first"), sem("x_squared")
        ws_turned, wm_ready, kc_turned, kc_ready = sem("ws_turned"), sem("wm_ready"), sem("kc_turned"), sem("kc_ready")
        sum_ready, rms_ready, rstd_ready = sem("sum_ready"), sem("rms_ready"), sem("rstd_ready")
        rstd_spread, r_ready = sem("rstd_spread"), sem("r_ready")
        z_evacuated, acc_zeroed, acc_added = sem("z_evacuated"), sem("acc_zeroed"), sem("acc_added")
        z_scaled, h_added, h_squared, pre_added = sem("z_scaled"), sem("h_added"), sem("h_squared"), sem("pre_added")
        x_hi, x_lo = sem("x_hi"), sem("x_lo")
        va_gelu, va_stats, va_bn, ln_rms_ready = sem("va_gelu"), sem("va_stats"), sem("va_bn"), sem("ln_rms_ready")
        ln_rstd_ready, va_normed, va_scaled, va_ready = sem("ln_rstd_ready"), sem("va_normed"), sem("va_scaled"), sem("va_ready")
        v_evacuated, rope_swapped, rope_sined, rope_cosined = sem("v_evacuated"), sem("rope_swapped"), sem("rope_sined"), sem("rope_cosined")
        rope_done, k_s_ready, k_turned, k_out_ready = sem("rope_done"), sem("k_s_ready"), sem("k_turned"), sem("k_out_ready")
        gate_done, gate_biased, sinks_ready = sem("gate_done"), sem("gate_biased"), sem("sinks_ready")
        scored, s_masked, topped, peaked = sem("scored"), sem("s_masked"), sem("topped"), sem("peaked")
        shifted, sink_shifted, exp_done, summed = sem("shifted"), sem("sink_shifted"), sem("exp_done"), sem("summed")
        den_ready, rden_ready, p_ready = sem("den_ready"), sem("rden_ready"), sem("p_ready")
        p_turned, p_t_ready, pv_done, att_hi, att_lo = sem("p_turned"), sem("p_t_ready"), sem("pv_done"), sem("att_hi"), sem("att_lo")
        u_evacuated, u_gelu, ya_ready, ya_hi, ya_lo = sem("u_evacuated"), sem("u_gelu"), sem("ya_ready"), sem("ya_hi"), sem("ya_lo")
        v_ready, rope_scaled = sem("v_ready"), sem("rope_scaled")
        gu_scaled, silu_done, m_ready, m_hi, m_lo = sem("gu_scaled"), sem("silu_done"), sem("m_ready"), sem("m_hi"), sem("m_lo")
        diag_ready, h_turned, h_tok_ready = sem("diag_ready"), sem("h_turned"), sem("h_tok_ready")
        band_dve, band_act, pooled, pool_out_ready = sem("band_dve"), sem("band_act"), sem("pooled"), sem("pool_out_ready")
        pool_first = sem("pool_first")
        y_turned, y_ready_act, y_ready_dve = sem("y_turned"), sem("y_ready_act"), sem("y_ready_dve")
        y_stored, out_stored = sem("y_stored"), sem("out_stored")

        def spreads(n):
            return n + 1 if n < 4 else n

        block = ctx.enter_context(nc.Block())

        @block.sync
        def _(sp):
            rows = ab_w_in[0].rearrange("(k p) n -> p k n", p=P)
            out_rows = ab_w_out[0]

            def raw_free(m):
                if m >= NRAW:
                    sp.wait_ge(w_lo, m - NRAW + 1)

            def tiles(m, n=UNIT):
                return raw[:, m % NRAW, 0:n]

            for t, (t0, n) in enumerate(TILES):
                src = x_prompt[0, t0:t0 + n, :] if t0 < SEQ else x_sample[0]
                sp.dma_start(x_tok[0:n, t, :], src).then_inc(x_loaded[t], 16)
            for j in range(4):
                m = U_IN + j
                raw_free(m)
                sp.dma_start(tiles(m).rearrange("p (k n) -> p k n", k=2), rows[:, 2 * j:2 * j + 2, AW:2 * AW])\
                    .then_inc(w_loaded[m % NRAW], 16)
            qo = 2 * AW
            ko, vo = qo + NQ * HD, qo + NQ * HD + NKV * HD
            for j, c in enumerate((vo, ko)):
                m = U_IN + 4 + j
                raw_free(m)
                sp.dma_start(tiles(m).rearrange("p (k n) -> p k n", k=KC), rows[:, :, c:c + P])\
                    .then_inc(w_loaded[m % NRAW], 16)
            for t in range(4):
                m = U_IN + 6 + t
                raw_free(m)
                for g in range(NKV):
                    c = qo + (4 * g + t) * HD
                    sp.dma_start(tiles(m).rearrange("p (k g n) -> p k g n", k=KC, g=NKV)[:, :, g, :],
                                 rows[:, :, c:c + HD]).then_inc(w_loaded[m % NRAW], 16)
            for t in range(4):
                m = U_IN + 10 + t
                raw_free(m)
                sp.dma_start(tiles(m).rearrange("p (k n) -> p k n", k=KC), rows[:, :, t * P:(t + 1) * P])\
                    .then_inc(w_loaded[m % NRAW], 16)
            for d in range(KC):
                m = U_OUT + d
                raw_free(m)
                dst = tiles(m).rearrange("p (k n) -> p k n", k=KC)
                cols = slice(d * P, (d + 1) * P)
                sp.dma_start(dst[:, 0:4, :], out_rows[0:AW, cols].rearrange("(k p) n -> p k n", p=P))\
                    .then_inc(w_loaded[m % NRAW], 16)
                for g in range(NKV):
                    r = AW + g * 4 * HD
                    sp.dma_start(dst[g * HD:(g + 1) * HD, 4:8, :],
                                 out_rows[r:r + 4 * HD, cols].rearrange("(t d) n -> d t n", t=4))\
                        .then_inc(w_loaded[m % NRAW], 16)

            def load_ffn(layer):
                w_in = ffn_w_in[layer].rearrange("(k p) n -> p k n", p=P)
                w_out = ffn_w_out[layer].rearrange("(c p) n -> p c n", p=P)
                base = U_FI[layer]
                with sp.Fori(0, FC // 2) as i:
                    for j in range(4):
                        m = base + j
                        sp.wait_ge(w_lo, i * 4 + (m - NRAW + 1))
                        col = i * (2 * P) + ((j // 2) * P + (j % 2) * DFF)
                        sp.dma_start(tiles(m).rearrange("p (k n) -> p k n", k=KC), w_in[:, :, bass.ds(col, P)])\
                            .then_inc(w_loaded[m % NRAW], 16)
                base = U_FO[layer]
                with sp.Fori(0, KC // 2) as i:
                    for j in range(8):
                        m = base + j
                        sp.wait_ge(w_lo, i * 8 + (m - NRAW + 1))
                        a, b = PIECES[j % 4]
                        col = i * (2 * P) + (j // 4) * P
                        sp.dma_start(tiles(m, (b - a) * P).rearrange("p (c n) -> p c n", n=P),
                                     w_out[:, a:b, bass.ds(col, P)]).then_inc(w_loaded[m % NRAW], 16)

            load_ffn(0)
            for j, g in enumerate(GROUPS):
                m = U_C + j
                raw_free(m)
                sp.dma_start(tiles(m, 4 * P).rearrange("p (k n) -> p k n", k=2),
                             c_w[0, g].rearrange("(k p) n -> p k n", p=P)).then_inc(w_loaded[m % NRAW], 16)
            load_ffn(1)
            for t, (t0, n) in enumerate(TILES):
                if t % 2 == 0:
                    sp.wait_ge(y_ready_act, t // 2 + 1)
                else:
                    sp.wait_ge(y_ready_dve, t // 2 + 1)
                dst = y_p[0, t0:t0 + n, :] if t0 < SEQ else y_s[0]
                sp.dma_start(dst, y_tok[0:n, t, :]).then_inc(y_stored, 16)
            sp.wait_ge(y_stored, 16 * NT)

        @block.tensor
        def _(pe):
            def product(out, wh, wl, xh, xl, first, last):
                pe.matmul(out, wh, xh, start=first, stop=False)
                pe.matmul(out, wh, xl, start=False, stop=False)
                return pe.matmul(out, wl, xh, start=False, stop=last)

            def both_halves(bank, m, tile, hi, lo, k, first, last):
                s = m % NSPLIT
                wh, wl = whi[:, s, tile * P:(tile + 1) * P], wlo[:, s, tile * P:(tile + 1) * P]
                for b in range(2):
                    c = slice(b * HALF, (b + 1) * HALF)
                    mm = product(flat(bank + b, 0, HALF), wh, wl, hi[:, k, c], lo[:, k, c], first, last)
                return mm

            def sum_squares(n, acc):
                for t in range(NT):
                    c, w = POOL_TILES[t] if n == 4 else (t * P if t < NT - 1 else TOK - P, P)
                    mm = pe.matmul(flat(6, t, 1, w), acc[:, c:c + w], ones[:, :], start=True, stop=True)
                mm.then_inc(sum_ready, 1)

            def spread(n):
                pe.wait_ge(rstd_ready, n + 1)
                for t, (t0, w) in enumerate(TILES):
                    if n == 0:
                        lhs, rhs = rstd[0:w, t:t + 1].broadcast_to([w, P]), ident[0:w, 0:w]
                    else:
                        lhs, rhs = rstd[:, t:t + 1].broadcast_to([P, P]), ident[:, P - w:P]
                    mm = pe.matmul(flat(6, P + t0, w), lhs, rhs, start=True, stop=True)
                mm.then_inc(rstd_spread, 1)

            pe.wait_ge(ident_loaded, 16)
            pe.wait_ge(gains_loaded, 32)
            pe.transpose(flat(7, 0, 72), gain_rows[:, :], ident[0:72, 0:72]).then_inc(gains_turned, 1)
            for k in range(KC):
                if k >= 4:
                    pe.wait_ge(h_first, k - 3)
                if k == 3:
                    pe.wait_ge(gains_ready, 1)
                for t, (t0, n) in enumerate(TILES):
                    if k == 0:
                        pe.wait_ge(x_loaded[t], 16)
                    mm = pe.transpose(flat(2 * (k % 4), t0, n), x_tok[0:n, t, k * P:(k + 1) * P], ident[0:n, 0:n])
                mm.then_inc(x_turned, 1)

            pe.wait_ge(h_first, 7)
            for j in range(4):
                m = U_IN + j
                s = m % NSPLIT
                pe.wait_ge(w_lo, m + 1)
                pe.wait_ge(x_lo, 2 * j + 2)
                for t, (t0, n) in enumerate(TILES):
                    for c in range(2):
                        k = 2 * j + c
                        mm = product(flat(t, 0, AW, n), xhi[:, k, t0:t0 + n], xlo[:, k, t0:t0 + n],
                                     whi[:, s, c * AW:(c + 1) * AW], wlo[:, s, c * AW:(c + 1) * AW],
                                     k == 0, k == KC - 1)
                mm.then_inc(w_used, 1)
            pe.wait_ge(h_first, KC)
            spread(0)
            m = U_IN + 4
            s = m % NSPLIT
            pe.wait_ge(w_lo, m + 1)
            for t, (t0, n) in enumerate(TILES):
                if t == NT - 1:
                    pe.wait_ge(va_gelu, NT)
                out = flat(5, t * P, P) if t < NT - 1 else flat(4, 0, P, n)
                for k in range(KC):
                    mm = product(out, xhi[:, k, t0:t0 + n], xlo[:, k, t0:t0 + n],
                                 whi[:, s, k * P:(k + 1) * P], wlo[:, s, k * P:(k + 1) * P], k == 0, k == KC - 1)
            mm.then_inc(w_used, 1)
            for r, bank in enumerate((6, 0, 2, 4, 6)):
                m = U_IN + 5 + r
                pe.wait_ge(w_lo, m + 1)
                if r == 0:
                    pe.wait_ge(r_ready, 1)
                if r == 2:
                    pe.wait_ge(v_evacuated, 2)
                    pe.wait_ge(ws_loaded, 16)
                    for a in range(AH):
                        mm = pe.transpose(flat(4, a * P, P), ws[:, a, :], ident[:, :])
                    mm.then_inc(ws_turned, 1)
                    pe.wait_ge(kc_loaded, 16)
                    pe.transpose(flat(5, 0, CHUNK), k_cache[:, :], ident[0:CHUNK, 0:CHUNK]).then_inc(kc_turned, 1)
                if r == 3:
                    pe.wait_ge(wm_ready, 1)
                    pe.wait_ge(kc_ready, 1)
                if r == 4:
                    pe.wait_ge(rope_cosined, 1)
                for k in range(KC):
                    mm = both_halves(bank, m, k, xhi, xlo, k, k == 0, k == KC - 1)
                mm.then_inc(w_used, 1)
            pe.wait_ge(va_ready, NT)
            for a in range(AH):
                bank = 2 * (a % 2)
                if a < 2:
                    pe.wait_ge(rope_cosined, a + 2)
                else:
                    pe.wait_ge(gate_biased, a - 1)
                for t, (t0, n) in enumerate(TILES):
                    mm = pe.matmul(flat(bank, t0, n), va[0:n, t, a * P:(a + 1) * P], wm_t[0:n, a, 0:n],
                                   start=True, stop=True)
                mm.then_inc(gate_done, 1)
            pe.wait_ge(rope_cosined, 4)
            pe.wait_ge(rope_done, 1)
            pe.transpose(flat(5, 0, P), k_r[:, SEQ - P:SEQ], ident[:, :])
            pe.transpose(flat(5, P, P, DEC), k_r[:, SEQ:TOK], ident[:, :]).then_inc(k_turned, 1)

            def scores(c):
                bank = 2 + 2 * (c % 2)
                if c == 0:
                    pe.wait_ge(rope_done, 5)
                    pe.wait_ge(gate_biased, 4)
                if c == 1:
                    pe.wait_ge(k_out_ready, 1)
                if c >= 2:
                    pe.wait_ge(shifted, NKV * (c - 1))
                if c == NCH:
                    pe.wait_ge(k_s_ready, 1)
                    pe.wait_ge(kc_ready, 1)
                    for g in range(NKV):
                        r = slice(g * HD, (g + 1) * HD)
                        mm = pe.matmul(flat(bank + g, 0, P), q_r[r, 4 * SEQ:4 * TOK], k_s[r, :], start=True, stop=True)
                else:
                    for g in range(NKV):
                        r = slice(g * HD, (g + 1) * HD)
                        for j in range(2):
                            col = j * P
                            lhs = q_r[r, 4 * CHUNK * c + j * P:4 * CHUNK * c + (j + 1) * P]
                            if c % 2:
                                mm = pe.matmul(flat(bank + g, col, P), lhs, k_r[r, (c - 1) * CHUNK:(c + 1) * CHUNK],
                                               start=True, stop=True)
                                continue
                            mm = pe.matmul(flat(bank + g, col, CHUNK), lhs, k_r[r, c * CHUNK:(c + 1) * CHUNK],
                                           start=True, stop=True)
                            if c:
                                mm = pe.matmul(flat(bank + g, col + CHUNK, CHUNK), lhs, k_r[r, (c - 1) * CHUNK:c * CHUNK],
                                               start=True, stop=True)
                mm.then_inc(scored, 1)

            def turn_probs(c):
                if c == 0:
                    pe.wait_ge(rope_cosined, 5)
                else:
                    pe.wait_ge(p_t_ready, c)
                pe.wait_ge(p_ready, c + 1)
                w = CHUNK if c == 0 else P
                for j in range(2 if c == NCH else 4):
                    mm = pe.transpose(flat(6, j * P, P, w), s_sb[:, c % 2, j * P:j * P + w], ident[:, :])
                mm.then_inc(p_turned, 1)

            def weigh_values(c):
                pe.wait_ge(p_t_ready, c + 1)
                if c >= 1:
                    pe.wait_ge(att_lo, c)
                if c == 0:
                    pe.wait_ge(v_ready, 2)
                    pe.wait_ge(v_evacuated, 2)
                if c == NCH:
                    pe.wait_ge(vc_loaded, 16)
                    pe.wait_ge(set_gaps, 1)
                w = CHUNK if c == 0 else P
                for g in range(NKV):
                    cols = slice(g * HD, (g + 1) * HD)
                    v = v_s[:, cols] if c == NCH else v_t[:, c // 2, cols] if c % 2 else v_even[0:w, c // 2, cols]
                    n = P if c == NCH else 2 * P
                    mm = pe.matmul(ps[g * HD:(g + 1) * HD, 7 * 512:7 * 512 + n], v, p_t[0:w, g * n:(g + 1) * n],
                                   start=True, stop=True)
                mm.then_inc(pv_done, 1)

            def u_step(n):
                t, k = divmod(n, KC)
                m = U_IN + 10 + t
                if k == 0:
                    pe.wait_ge(w_lo, m + 1)
                    if t == 0:
                        pe.wait_ge(gate_biased, 3)
                    else:
                        pe.wait_ge(u_evacuated, t)
                mm = both_halves(0, m, k, xhi, xlo, k, k == 0, k == KC - 1)
                if k == KC - 1:
                    mm.then_inc(w_used, 1)

            for i in range(NCH + 3):
                if i <= NCH:
                    scores(i)
                for n in range(3 * i, min(3 * i + 3, 4 * KC)):
                    u_step(n)
                if 1 <= i <= NCH + 1:
                    turn_probs(i - 1)
                if i >= 2:
                    weigh_values(i - 2)

            def mixer_out(m, j, i, first):
                pe.wait_ge(w_lo, i * 4 + (m + 1))
                for n, k in enumerate((4, 5, 6, 7, 0, 1, 2, 3)):
                    if n == 0:
                        pe.wait_ge(att_lo, NCH + 1)
                    if k < 4:
                        pe.wait_ge(ya_lo, k + 1)
                    mm = both_halves(OUT_BANKS[j], m, k, yhi, ylo, k, n == 0, n == KC - 1)
                mm.then_inc(w_used, 1)

            for j in range(4):
                mixer_out(U_OUT + j, j, 0, True)
            for j in range(4):
                pe.wait_ge(z_evacuated, j + 1)
                mixer_out(U_OUT + 4 + j, j, 0, False)

            def ffn_layer(layer, n_post):
                base = U_FI[layer]
                xb = 8 * (2 * layer + 1)
                for k in range(KC):
                    pe.wait_ge(x_lo, xb + k + 1)
                    for j in range(3):
                        if k == 0:
                            pe.wait_ge(w_lo, base + j + 1)
                        mm = both_halves(2 * j, base + j, k, xhi, xlo, k, k == 0, k == KC - 1)
                        if k == KC - 1:
                            mm.then_inc(w_used, 1)
                pe.wait_ge(pre_added, 8 * (n_post // 2 + 1))
                sum_squares(n_post + 1, acc_pre)
                spread(n_post + 1)
                pe.wait_ge(w_lo, base + 4)
                pe.wait_ge(r_ready, spreads(n_post + 1))
                for k in range(KC):
                    mm = both_halves(6, base + 3, k, xhi, xlo, k, k == 0, k == KC - 1)
                mm.then_inc(w_used, 1)
                with pe.Fori(1, FC // 2) as i:
                    for j in range(4):
                        pe.wait_ge(w_lo, i * 4 + (base + j + 1))
                        if j % 2 == 0:
                            pe.wait_ge(gu_scaled, i * 2 + (FC * layer + j // 2 - 1))
                        for k in range(KC):
                            mm = both_halves(2 * j, base + j, k, xhi, xlo, k, k == 0, k == KC - 1)
                        mm.then_inc(w_used, 1)
                pe.wait_ge(gu_scaled, FC * (layer + 1))
                base = U_FO[layer]
                with pe.Fori(0, KC // 2) as i:
                    for d in range(2):
                        pe.wait_ge(z_evacuated, i * 2 + (8 * (2 * layer + 1) + d - 1))
                        for j, (a, b) in enumerate(PIECES):
                            m = base + 4 * d + j
                            pe.wait_ge(w_lo, i * 8 + (m + 1))
                            pe.wait_ge(m_lo, FC * layer + b)
                            for c in range(a, b):
                                mm = both_halves(2 * d, m, c - a, mhi, mlo, c, c == 0, c == FC - 1)
                            mm.then_inc(w_used, 1)
                pe.wait_ge(acc_added, 8 * (2 * layer + 2))
                sum_squares(n_post + 2, acc_post)
                spread(n_post + 2)

            pe.wait_ge(acc_added, 8)
            sum_squares(1, acc_post)
            spread(1)
            ffn_layer(0, 1)

            for k in range(KC):
                pe.wait_ge(h_added, 8 + k + 1)
                if k == 0:
                    pe.wait_ge(diag_ready, 1)
                if k >= 3:
                    pe.wait_ge(h_tok_ready, k - 2)
                for t, (c, w) in enumerate(POOL_TILES):
                    mm = pe.matmul(flat(2 * (k % 3), t * P, P, w), h[:, k, c:c + w], gain_diag[:, k, :],
                                   start=True, stop=True)
                mm.then_inc(h_turned, 1)
            pe.wait_ge(pre_added, 16)
            sum_squares(4, acc_pre)

            def pool_chunk(n):
                g = GROUPS[n // 2]
                c = 2 * g + n % 2
                bank = 2 * (n % 2)
                cols = slice(c * P, (c + 1) * P)
                if n == 0:
                    pe.wait_ge(h_tok_ready, KC)
                    pe.wait_ge(hist_loaded, 16)
                    pe.wait_ge(band_loaded, 64)
                    pe.wait_ge(band_dve, 1)
                    pe.wait_ge(band_act, 1)
                if n >= 2:
                    pe.wait_ge(x_lo, 16 + n - 1)
                for t, (a, b) in enumerate(POOL_OUT):
                    w = P if t < NT - 1 else TAIL + HIST
                    mm = pe.matmul(flat(bank, POOL_AT + a, b - a), h_tok[0:w, t, cols], band_r[t][0:w, g, :],
                                   start=True, stop=True)
                mm.then_inc(pooled, 1)

            def pool_product(e):
                j, o = divmod(e, 2)
                g = GROUPS[j]
                m = U_C + j
                s = m % NSPLIT
                if o == 0:
                    pe.wait_ge(w_lo, m + 1)
                    pe.wait_ge(x_lo, 16 + 2 * (j + 1))
                bank = 4 + 2 * o
                if e >= 2:
                    pe.wait_ge(z_evacuated, 16 + e - 1)
                for b in range(2):
                    c = slice(b * HALF, (b + 1) * HALF)
                    for k in range(2):
                        w = slice(k * 2 * P + o * P, k * 2 * P + (o + 1) * P)
                        mm = product(flat(bank + b, 0, HALF), whi[:, s, w], wlo[:, s, w],
                                     xhi[:, 2 * g + k, c], xlo[:, 2 * g + k, c], k == 0, k == 1)
                if o:
                    mm.then_inc(w_used, 1)
                else:
                    mm.then_inc(pool_first, 1)

            for j in range(len(GROUPS) + 1):
                for o in range(2):
                    if j < len(GROUPS):
                        pool_chunk(2 * j + o)
                for o in range(2):
                    if j:
                        pool_product(2 * (j - 1) + o)
            pe.wait_ge(acc_added, 24)
            sum_squares(5, acc_post)
            spread(5)
            ffn_layer(1, 5)

            for k in range(KC):
                pe.wait_ge(h_added, 24 + k + 1)
                if k == 0:
                    pe.wait_ge(r_ready, spreads(7))
                for t in range(NT - 1):
                    mm = pe.transpose(flat(2 * t, k * P, P), h[:, k, t * P:(t + 1) * P], ident[:, :])
                    if k == KC - 1:
                        mm.then_inc(y_turned, 1)
            pe.wait_ge(y_ready_act, 1)
            for k in range(KC):
                mm = pe.transpose(flat(0, k * P, P, DEC), h[:, k, SEQ:TOK], ident[:, :])
            mm.then_inc(y_turned, 1)

        @block.scalar
        def _(act):
            def hi_part(m, i=0, step=0):
                if step:
                    act.wait_ge(w_loaded[m % NRAW], i * (16 * step // NRAW) + loaded(m))
                    act.wait_ge(w_used, i * step + (m - NSPLIT + 1))
                else:
                    act.wait_ge(w_loaded[m % NRAW], loaded(m))
                    if m >= NSPLIT:
                        act.wait_ge(w_used, m - NSPLIT + 1)
                n = unit_columns(m)
                act.activation(whi[:, m % NSPLIT, 0:n], raw[:, m % NRAW, 0:n], ACT.Copy).then_inc(w_hi, 1)

            def root(n):
                if n == 0:
                    act.wait_ge(x_squared, NT)
                    src = ssq[:, :]
                else:
                    act.wait_ge(sum_ready, n)
                    src = flat(6, 0, NT)
                if n == 4:
                    act.activation(rms[0:TAIL, NT - 1:NT], flat(6, NT - 1, 1, TAIL), ACT.Sqrt, scale=1.0 / D,
                                   bias=eps[0:TAIL, :])
                    act.activation(rms[:, 0:NT - 1], flat(6, 0, NT - 1), ACT.Sqrt, scale=1.0 / D, bias=eps[:, :])\
                        .then_inc(rms_ready, 1)
                    return
                act.activation(rms[:, :], src, ACT.Sqrt, scale=1.0 / D, bias=eps[:, :]).then_inc(rms_ready, 1)

            def keep_spread(n, dst):
                act.wait_ge(rstd_spread, spreads(n))
                act.activation(dst[:, :], flat(6, P, TOK), ACT.Copy).then_inc(r_ready, 1)

            def warm(func):
                act.activation(warmed[:, :], eps[:, :], func)

            act.dma_start(ident[:, :], constants[:, 0:P]).then_inc(ident_loaded, 16)
            act.dma_start(gain_rows[0:64, :], norm_g.rearrange("l j (k p) -> (l j k) p", p=P)).then_inc(gains_loaded, 16)
            act.dma_start(gain_rows[64:72, :], c_scale[0].rearrange("(k p) -> k p", p=P)).then_inc(gains_loaded, 16)
            act.dma_start(ws[:, :, :], a_ws[0].rearrange("h i j -> i h j")).then_inc(ws_loaded, 16)
            act.dma_start(k_cache[:, :], cache_k[0, 0, WIN - CHUNK:WIN].rearrange("t g d -> t (g d)")).then_inc(kc_loaded, 16)
            act.dma_start(v_s[CHUNK:P, :], cache_v[0, 0, WIN - CHUNK:WIN].rearrange("t g d -> t (g d)")).then_inc(vc_loaded, 16)
            act.dma_start(cossin[:, :, :], constants[:, P:P + 2 * TOK].rearrange("p (a n) -> p a n", a=2)).then_inc(rope_loaded, 16)
            act.dma_start(ln_gb[:, 0, :], ln_g[0].partition_broadcast(P)).then_inc(ln_loaded, 16)
            act.dma_start(ln_gb[:, 1, :], ln_b[0].partition_broadcast(P)).then_inc(ln_loaded, 16)
            act.dma_start(bs_b[:, :, :].rearrange("p h i -> p (h i)"),
                          a_bs[0].rearrange("h i -> (h i)").partition_broadcast(P)).then_inc(bs_loaded, 16)
            act.dma_start(sinks[:, :], b_sinks[0].partition_broadcast(P)).then_inc(sinks_loaded, 16)

            act.wait_ge(set_up, 1)
            act.wait_ge(gains_turned, 1)
            act.activation(gains[:, :], flat(7, 0, 72), ACT.Copy).then_inc(gains_ready, 1)
            act.wait_ge(gains_ready, 1)
            for k in range(KC):
                if k in (2, 5):
                    hi_part(k // 3)
                act.wait_ge(h_first, k + 1)
                act.activation(xhi[:, k, :], h[:, k, :], ACT.Copy, scale=gain(0, 0, k)).then_inc(x_hi, 1)
            for t, (t0, n) in enumerate(TILES):
                act.wait_ge(x_loaded[t], 16)
                if t:
                    act.wait_ge(x_squared, t)
                act.activation(u_raw[0:n, 0:2, 0:512], x_tok[0:n, t, :].rearrange("p (a b) -> p a b", a=2), ACT.Square,
                               accum_out=ssq[0:n, t:t + 1]).then_inc(x_squared, 1)
                if t in (0, 3):
                    hi_part(2 + t // 3)
            root(0)
            hi_part(4)
            act.wait_ge(rstd_ready, 1)
            act.wait_ge(w_used, 4)
            for t, (t0, n) in enumerate(TILES):
                act.activation(va[0:n, t, :], flat(t, 0, AW, n), ACT.Gelu_apprx_tanh, scale=rstd[0:n, t:t + 1])\
                    .then_inc(va_gelu, 1)
            keep_spread(0, r_pre)
            for m in (5, 6, 7):
                hi_part(m)
            act.wait_ge(va_bn, NT)
            act.activation(ln_rms[:, :], mean_var[:, :, 1], ACT.Sqrt, bias=eps[:, :]).then_inc(ln_rms_ready, 1)
            act.wait_ge(v_evacuated, 1)
            act.activation(v_even[0:CHUNK, :, :], v_t[0:CHUNK, :, :], ACT.Copy).then_inc(v_ready, 1)
            act.activation(v_even[CHUNK:P, 1:4, :], v_t[CHUNK:P, 0:3, :], ACT.Copy).then_inc(v_ready, 1)
            for m in range(8, 14):
                hi_part(m)
            act.wait_ge(k_turned, 1)
            act.activation(k_out[:, 0, :], flat(5, 0, P), ACT.Copy)
            act.activation(k_out[0:DEC, 1, :], flat(5, P, P, DEC), ACT.Copy).then_inc(k_out_ready, 1)

            def exps(c):
                w = CHUNK if c == 0 else P
                n = 2 if c == NCH else 4
                s = s_sb[:, c % 2, 0:n * P].rearrange("p (c s) -> p c s", c=n)[:, :, 0:w]
                act.wait_ge(sink_shifted, c + 1)
                act.activation(den[:, c % 2, 0:n], sunk[:, c % 2, 0:n], ACT.Exp)
                act.activation(s, s, ACT.Exp).then_inc(exp_done, 1)

            def keep_turned(c):
                act.wait_ge(p_turned, c + 1)
                if c >= 1:
                    act.wait_ge(pv_done, c)
                w = CHUNK if c == 0 else P
                n = (2 if c == NCH else 4) * P
                act.activation(p_t[0:w, 0:n], flat(6, 0, n, w), ACT.Copy).then_inc(p_t_ready, 1)

            def attended(c):
                n = DEC if c == NCH else CHUNK
                return slice(c * CHUNK, c * CHUNK + n), flat(7, 0, 4 * n).rearrange("p (t q) -> p t q", t=4)

            def attended_hi(c):
                act.wait_ge(pv_done, c + 1)
                cols, src = attended(c)
                act.activation(yhi[:, 4:8, cols], src, ACT.Copy).then_inc(att_hi, 1)

            for i in range(NCH + 3):
                if i <= NCH:
                    exps(i)
                if i == 2:
                    hi_part(14)
                if i == 5:
                    hi_part(15)
                if i == 7:
                    hi_part(16)
                if 1 <= i <= NCH + 1:
                    keep_turned(i - 1)
                if i >= 2:
                    attended_hi(i - 2)
                if i == NCH + 1:
                    for t in range(3):
                        act.wait_ge(u_evacuated, t + 1)
                        act.activation(u_raw[:, t, :], u_raw[:, t, :], ACT.Gelu_apprx_tanh).then_inc(u_gelu, 1)
            act.wait_ge(u_evacuated, 4)
            act.activation(u_raw[:, 3, :], u_raw[:, 3, :], ACT.Gelu_apprx_tanh).then_inc(u_gelu, 1)
            hi_part(17)
            for t in range(AH):
                act.wait_ge(ya_ready, t + 1)
                act.activation(yhi[:, t, :], gated[:, t, :], ACT.Copy).then_inc(ya_hi, 1)

            def evacuate_z(s, n, chunk, i, step, bank, used, scale=1.0):
                act.wait_ge(w_used, i * (4 * step) + used) if step else act.wait_ge(w_used, used)
                act.activation(halves(z[:, bass.ds(i * step + chunk, 1), :].rearrange("p o n -> p (o n)"))
                               if step else halves(z[:, chunk, :]), pair(bank), ACT.Copy, scale=scale)
                if step:
                    act.wait_ge(acc_added, i * step + (8 * s + n - 1))
                elif 8 * s + n >= 2:
                    act.wait_ge(acc_added, 8 * s + n - 1)
                act.activation(halves(tmp2[:, n % 2, :]), pair(bank), ACT.Square, scale=scale).then_inc(z_evacuated, 1)

            for d in range(KC):
                evacuate_z(0, d, d, 0, 0, OUT_BANKS[d % 4], U_OUT + d + 1)
                if d < KC - 1:
                    hi_part(U_OUT + 4 + d)

            def residual(s, split, late, follow=None):
                warm(ACT.Sqrt)
                root(2 * s + 1)
                keep_spread(2 * s + 1, r_post)
                for k in range(KC):
                    act.wait_ge(h_added, 8 * s + k + 1)
                    if split is not None:
                        act.activation(xhi[:, k, :], h[:, k, :], ACT.Copy, scale=split(k)).then_inc(x_hi, 1)
                    if k == 0:
                        act.activation(acc_pre[:, :], h[:, k, :], ACT.Square).then_inc(h_squared, 1)
                    else:
                        if k >= 3:
                            act.wait_ge(pre_added, 8 * s + k - 1)
                        act.activation(tmp2[:, k % 2, :], h[:, k, :], ACT.Square).then_inc(h_squared, 1)
                    if follow and k:
                        follow(k - 1)
                    if k == 4 and late is not None:
                        hi_part(late)
                if follow:
                    follow(KC - 1)

            def ffn_layer(layer, n_post):
                root(n_post + 1)
                keep_spread(n_post + 1, r_pre)
                warm(ACT.Silu)
                act.wait_ge(out_stored, 16 * MIXER_STORES[layer])
                base = U_FI[layer]

                def tiles_pair(i, following, i2, step2):
                    for f in range(2):
                        act.wait_ge(gu_scaled, i * 2 + (FC * layer + f + 1))
                        act.activation(tmp2[:, 0, :], tmp[:, 0, :], ACT.Silu).then_inc(silu_done, 1)
                        hi_part(following + 2 * f, i2, step2)
                        act.wait_ge(m_ready, i * 2 + (FC * layer + f + 1))
                        act.activation(mhi[:, bass.ds(i * 2 + f, 1), :].rearrange("p o n -> p (o n)"), tmp2[:, 1, :],
                                       ACT.Copy).then_inc(m_hi, 1)
                        hi_part(following + 2 * f + 1, i2, step2)

                with act.Fori(0, FC // 2 - 1) as i:
                    tiles_pair(i, base + 4, i, 4)
                tiles_pair(FC // 2 - 1, U_FO[layer], 0, 0)
                base = U_FO[layer]
                s = 2 * layer + 1

                def chunks_pair(i, last):
                    for d in range(2):
                        for j in range(4):
                            m = base + 4 * d + j + 4
                            if not last:
                                hi_part(m, i, 8)
                            elif 8 * (KC // 2 - 1) + m < U_END and not (d == 1 and j == 3):
                                hi_part(8 * (KC // 2 - 1) + m)
                        if last:
                            n = KC - 2 + d
                            evacuate_z(s, n, n, 0, 0, 2 * d, base + 4 * n + 4)
                        else:
                            evacuate_z_loop(s, d, i, 2 * d, base + 4 * d + 4)

                def evacuate_z_loop(s, d, i, bank, used):
                    act.wait_ge(w_used, i * 8 + used)
                    act.activation(halves(z[:, bass.ds(i * 2 + d, 1), :].rearrange("p o n -> p (o n)")), pair(bank), ACT.Copy)
                    act.wait_ge(acc_added, i * 2 + (8 * s + d - 1))
                    act.activation(halves(tmp2[:, d, :]), pair(bank), ACT.Square).then_inc(z_evacuated, 1)

                with act.Fori(0, KC // 2 - 1) as i:
                    chunks_pair(i, False)
                chunks_pair(KC // 2 - 1, True)

            residual(0, lambda k: gain(0, 2, k), U_OUT + 11)
            ffn_layer(0, 1)

            def keep_turned_h(k):
                act.wait_ge(h_turned, k + 1)
                c = slice(k * P, (k + 1) * P)
                act.activation(h_tok[0:TAIL, NT - 1, c], flat(2 * (k % 3) + 1, 0, P, TAIL), ACT.Copy)
                act.activation(h_tok[:, 0:NT - 1, c], flat(2 * (k % 3), 0, 512).rearrange("p (t n) -> p t n", n=P),
                               ACT.Copy).then_inc(h_tok_ready, 1)

            residual(1, None, U_C + 3, keep_turned_h)
            root(4)
            act.wait_ge(band_loaded, 64)
            act.wait_ge(rstd_ready, 5)
            for t in (2, 3):
                op = act.activation(band_r[t][:, :, :], band_later[:, :, :], ACT.Copy, scale=rstd[:, t:t + 1])
            op.then_inc(band_act, 1)

            def pool_evacuate(e):
                j, o = divmod(e, 2)
                c = 2 * GROUPS[j] + o
                bank = 4 + 2 * o
                if o == 0:
                    act.wait_ge(pool_first, j + 1)
                else:
                    act.wait_ge(w_used, U_C + j + 1)
                act.activation(halves(z_pool[:, c, :]), pair(bank), ACT.Copy, scale=scale_c(c))
                act.wait_ge(acc_added, 16 + e - 1)
                act.activation(halves(tmp2[:, e % 2, :]), pair(bank), ACT.Square, scale=scale_c(c)).then_inc(z_evacuated, 1)
                if o and j < 3:
                    hi_part(U_FI[1] + j)

            for j in range(len(GROUPS) + 1):
                for o in range(2):
                    if j < len(GROUPS):
                        n = 2 * j + o
                        act.wait_ge(pooled, n + 1)
                        act.activation(xhi[:, 2 * GROUPS[j] + o, :], flat(2 * o, POOL_AT, TOK), ACT.Copy).then_inc(x_hi, 1)
                for o in range(2):
                    if j:
                        pool_evacuate(2 * (j - 1) + o)
            residual(2, lambda k: gain(1, 2, k), U_FI[1] + 3)
            ffn_layer(1, 5)
            warm(ACT.Sqrt)
            root(7)
            keep_spread(7, r_post)
            for t, (t0, n) in enumerate(TILES):
                if t % 2 == 0:
                    act.wait_ge(y_turned, t + 1)
                    act.activation(y_tok[0:n, t, :], flat(0 if t == NT - 1 else 2 * t, 0, D, n), ACT.Copy)\
                        .then_inc(y_ready_act, 1)

        @block.vector
        def _(dve):
            def lo_part(m, i=0, step=0):
                dve.wait_ge(w_hi, i * step + (m + 1) if step else m + 1)
                s, n = m % NSPLIT, unit_columns(m)
                dve.tensor_tensor(wlo[:, s, 0:n], raw[:, m % NRAW, 0:n], whi[:, s, 0:n].bitcast(F32), ALU.subtract)\
                    .then_inc(w_lo, 1)

            def invert(n):
                dve.wait_ge(rms_ready, n + 1)
                if n == 5:
                    dve.wait_ge(pool_out_ready, 1)
                if n == 4:
                    dve.reciprocal(rstd[0:TAIL, NT - 1:NT], rms[0:TAIL, NT - 1:NT])
                    dve.reciprocal(rstd[:, 0:NT - 1], rms[:, 0:NT - 1]).then_inc(rstd_ready, 1)
                    return
                dve.reciprocal(rstd[:, :], rms[:, :]).then_inc(rstd_ready, 1)

            dve.memset(wm_t[CHUNK:P, :, 0:CHUNK], 0.0)
            dve.memset(v_s[DEC:CHUNK, :], 0.0).then_inc(set_gaps, 1)
            for k in range(KC + 1):
                if k < KC:
                    dve.wait_ge(x_turned, k + 1)
                    dve.tensor_copy(h[:, k, :], flat(2 * (k % 4), 0, TOK)).then_inc(h_first, 1)
                if k >= 1:
                    dve.wait_ge(x_hi, k)
                    dve.scalar_tensor_tensor(xlo[:, k - 1, :], h[:, k - 1, :], gain(0, 0, k - 1),
                                             xhi[:, k - 1, :].bitcast(F32), ALU.mult, ALU.subtract).then_inc(x_lo, 1)
                if k in (2, 5):
                    lo_part(k // 3)
            lo_part(2)
            lo_part(3)
            invert(0)

            lo_part(4)
            dve.wait_ge(sinks_loaded, 16)
            dve.tensor_copy(sink_p[0:CHUNK, :], sinks[0:CHUNK, 0:NQ:2])
            dve.tensor_copy(sink_p[CHUNK:P, :], sinks[CHUNK:P, 1:NQ:2])
            for a in range(4):
                op = dve.tensor_copy(sink_s[a * DEC:(a + 1) * DEC, :], sinks[a * DEC:(a + 1) * DEC, a:NQ:4])
            op.then_inc(sinks_ready, 1)
            for t, (t0, n) in enumerate(TILES):
                dve.wait_ge(va_gelu, t + 1)
                dve.bn_stats(stats[0:n, t, :], va[0:n, t, :]).then_inc(va_stats, 1)
            dve.wait_ge(set_stats, 1)
            for t, (t0, n) in enumerate(TILES):
                dve.wait_ge(va_stats, t + 1)
                dve.bn_aggr(mean_var[0:n, t, :], stats[0:n, t, :]).then_inc(va_bn, 1)
            lo_part(5)
            dve.wait_ge(w_used, 5)
            dve.tensor_tensor(v_t[:, :, :], flat(5, 0, 512).rearrange("p (j n) -> p j n", j=4),
                              rstd[:, 0:4].unsqueeze(2).broadcast_to([P, 4, P]), ALU.mult).then_inc(v_evacuated, 1)
            dve.tensor_scalar(v_s[0:DEC, :], flat(4, 0, P, DEC), rstd[0:DEC, 4:5], None, ALU.mult).then_inc(v_evacuated, 1)
            lo_part(6)
            dve.wait_ge(ln_rms_ready, 1)
            dve.reciprocal(ln_rstd[:, :], ln_rms[:, :]).then_inc(ln_rstd_ready, 1)
            dve.wait_ge(ln_rstd_ready, 1)
            for t, (t0, n) in enumerate(TILES):
                dve.tensor_scalar(va[0:n, t, :], va[0:n, t, :], mean_var[0:n, t, 0:1], ln_rstd[0:n, t:t + 1],
                                  ALU.subtract, ALU.mult).then_inc(va_normed, 1)
            lo_part(7)

            half = ROPE // 2
            swap = [*range(half, ROPE), *range(half), *range(ROPE, 32)]

            def rope_parts(r):
                dve.wait_ge(w_used, U_IN + 6 + r)
                if r >= 2:
                    dve.wait_ge(rope_done, r - 1)
                elif r == 0:
                    dve.wait_ge(x_lo, KC)
                src = pair((6, 0, 2, 4, 6)[r])
                dve.stream_shuffle(halves(tmp[:, r % 2, :]), src, swap).then_inc(rope_swapped, 1)
                dve.tensor_tensor(halves(tmp2[:, r % 2, :]), src, halves(cossin[:, 0, :]), ALU.mult).then_inc(rope_cosined, 1)
                dve.wait_ge(rope_swapped, r + 1)
                dve.tensor_tensor(tmp[:, r % 2, :], tmp[:, r % 2, :], cossin[:, 1, :], ALU.mult).then_inc(rope_sined, 1)

            def rope_sum(r):
                dve.wait_ge(rope_sined, r + 1)
                dve.wait_ge(rope_cosined, r + 1)
                a, b = tmp[:, r % 2, :], tmp2[:, r % 2, :]
                if r == 0:
                    dve.tensor_tensor(k_r[:, :], a, b, ALU.add).then_inc(rope_done, 1)
                    return
                t = r - 1
                by_chunk = lambda ap: ap[:, 0:SEQ].rearrange("p (c q) -> p c q", c=NCH)
                dst = q_r[:, 0:4 * SEQ].rearrange("p (c t q) -> p c t q", c=NCH, t=4)[:, :, t, :]
                dve.tensor_tensor(dst, by_chunk(a), by_chunk(b), ALU.add)
                dve.tensor_tensor(q_r[:, 4 * SEQ + t * DEC:4 * SEQ + (t + 1) * DEC], a[:, SEQ:TOK], b[:, SEQ:TOK],
                                  ALU.add).then_inc(rope_done, 1)

            dve.wait_ge(rope_loaded, 16)
            dve.wait_ge(r_ready, 1)
            for a in range(2):
                dve.tensor_tensor(cossin[:, a, :], cossin[:, a, :], r_pre[:, :], ALU.mult).then_inc(rope_scaled, 1)
            dve.wait_ge(rope_scaled, 2)
            for r in range(5):
                if r == 2:
                    dve.wait_ge(ws_turned, 1)
                    turned = flat(4, 0, 512).rearrange("p (h i) -> p h i", h=AH)
                    dve.tensor_copy(wm_t[0:CHUNK, :, :], turned[0:CHUNK])
                    dve.tensor_copy(wm_t[CHUNK:P, :, CHUNK:P], turned[CHUNK:P, :, CHUNK:P]).then_inc(wm_ready, 1)
                    dve.wait_ge(kc_turned, 1)
                    dve.tensor_copy(k_s[:, CHUNK:P], flat(5, 0, CHUNK)).then_inc(kc_ready, 1)
                rope_parts(r)
                lo_part(8 + r)
                rope_sum(r)

            def bias_gate(a):
                dve.wait_ge(gate_done, a + 1)
                bank = 2 * (a % 2)
                dve.tensor_tensor(gated[:, a, 0:SEQ].rearrange("p (n i) -> p n i", i=P),
                                  flat(bank, 0, SEQ).rearrange("p (n i) -> p n i", i=P),
                                  bs_b[:, a:a + 1, :].broadcast_to([P, SEQ // P, P]), ALU.add)
                dve.tensor_tensor(gated[:, a, SEQ:TOK], flat(bank, SEQ, DEC), bs_b[:, a, 0:DEC], ALU.add)\
                    .then_inc(gate_biased, 1)

            dve.wait_ge(bs_loaded, 16)
            for a in range(AH):
                bias_gate(a)
            lo_part(13)

            def shift(c):
                n, b = (2, c % 2) if c == NCH else (4, c % 2)
                w = CHUNK if c == 0 else P
                sink = sink_s[:, :] if c == NCH else sink_p[:, :]
                npg = n // NKV
                dst = s_sb[:, b, 0:n * P].rearrange("p (c s) -> p c s", c=n)[:, :, 0:w]
                srcs = [flat(2 + 2 * (c % 2) + g, 0, npg * P).rearrange("p (c s) -> p c s", c=npg)[:, :, 0:w]
                        for g in range(NKV)]
                scale = SCALE
                dve.wait_ge(scored, c + 1)
                if c >= 2:
                    dve.wait_ge(p_turned, c - 1)
                if c == NCH:
                    for g in range(NKV):
                        dve.scalar_tensor_tensor(dst[:, g, :], srcs[g][:, 0, :], SCALE, mask_s[:, :],
                                                 ALU.mult, ALU.add).then_inc(s_masked, 1)
                    dve.wait_ge(s_masked, NKV)
                    srcs, scale = [dst[:, g:g + 1, :] for g in range(NKV)], 1.0
                for g in range(NKV):
                    dve.tensor_reduce(top[:, b, g * npg:(g + 1) * npg], srcs[g], AX.X, ALU.max).then_inc(topped, 1)
                dve.wait_ge(topped, NKV * (c + 1))
                dve.scalar_tensor_tensor(peak[:, b, 0:n], top[:, b, 0:n], scale, sink, ALU.mult, ALU.max).then_inc(peaked, 1)
                dve.wait_ge(peaked, c + 1)
                for g in range(NKV):
                    part = slice(g * npg, (g + 1) * npg)
                    dve.scalar_tensor_tensor(dst[:, part, :], srcs[g], scale,
                                             peak[:, b, part].unsqueeze(2).broadcast_to([P, npg, w]),
                                             ALU.mult, ALU.subtract).then_inc(shifted, 1)
                dve.tensor_tensor(sunk[:, b, 0:n], sink, peak[:, b, 0:n], ALU.subtract).then_inc(sink_shifted, 1)

            def denominator(c):
                n, b = (2, c % 2) if c == NCH else (4, c % 2)
                w = CHUNK if c == 0 else P
                p = s_sb[:, b, 0:n * P].rearrange("p (c s) -> p c s", c=n)[:, :, 0:w]
                dve.wait_ge(exp_done, c + 1)
                dve.tensor_reduce(den2[:, b, 0:n], p, AX.X, ALU.add).then_inc(summed, 1)
                dve.wait_ge(summed, c + 1)
                dve.tensor_tensor(den2[:, b, 0:n], den2[:, b, 0:n], den[:, b, 0:n], ALU.add).then_inc(den_ready, 1)
                dve.wait_ge(den_ready, c + 1)
                dve.reciprocal(rden[:, b, 0:n], den2[:, b, 0:n]).then_inc(rden_ready, 1)

            def attended_lo(c):
                n = DEC if c == NCH else CHUNK
                cols, src = slice(c * CHUNK, c * CHUNK + n), flat(7, 0, 4 * n).rearrange("p (t q) -> p t q", t=4)
                dve.wait_ge(att_hi, c + 1)
                dve.tensor_tensor(ylo[:, 4:8, cols], src, yhi[:, 4:8, cols].bitcast(F32), ALU.subtract).then_inc(att_lo, 1)

            def evacuate_u(t):
                dve.wait_ge(w_used, U_IN + 11 + t)
                dve.tensor_tensor(halves(u_raw[:, t, :]), pair(0), halves(r_pre[:, :]), ALU.mult).then_inc(u_evacuated, 1)

            dve.wait_ge(sinks_ready, 1)
            dve.wait_ge(set_sample, 1)
            for i in range(NCH + 3):
                if i <= NCH:
                    shift(i)
                if i in (2, 5, 7):
                    t = (2, 5, 7).index(i)
                    evacuate_u(t)
                    lo_part(14 + t)
                if i <= NCH:
                    denominator(i)
                if i >= 2:
                    attended_lo(i - 2)
            evacuate_u(3)
            lo_part(17)
            for t in range(AH):
                dve.wait_ge(ya_hi, t + 1)
                dve.tensor_tensor(ylo[:, t, :], gated[:, t, :], yhi[:, t, :].bitcast(F32), ALU.subtract).then_inc(ya_lo, 1)

            def add_squares(s, n, slot, i=0, step=0):
                if step:
                    dve.wait_ge(z_evacuated, i * step + (8 * s + n + 1))
                    dve.wait_ge(acc_added, i * step + (8 * s + n))
                else:
                    dve.wait_ge(z_evacuated, 8 * s + n + 1)
                    if 8 * s + n:
                        dve.wait_ge(acc_added, 8 * s + n)
                dve.tensor_tensor(acc_post[:, :], acc_post[:, :], tmp2[:, slot, :], ALU.add).then_inc(acc_added, 1)

            dve.wait_ge(acc_zeroed, 1)
            for d in range(KC):
                if d < KC - 1:
                    lo_part(U_OUT + 4 + d)
                add_squares(0, d, d % 2)

            def residual(s, layer, post, split, late):
                invert(2 * s + 1)
                dve.wait_ge(r_ready, spreads(2 * s + 1))

                def lo(k):
                    dve.wait_ge(x_hi, split[0] + k + 1)
                    dve.scalar_tensor_tensor(xlo[:, k, :], h[:, k, :], split[1](k), xhi[:, k, :].bitcast(F32),
                                             ALU.mult, ALU.subtract).then_inc(x_lo, 1)

                for k in range(KC):
                    if 8 * s + k >= 2:
                        dve.wait_ge(h_added, 8 * s + k - 1)
                    dve.tensor_tensor(tmp[:, k % 2, :], (z_pool if s == 2 else z)[:, k, :], r_post[:, :], ALU.mult).then_inc(z_scaled, 1)
                    if k and split:
                        lo(k - 1)
                    dve.wait_ge(z_scaled, 8 * s + k + 1)
                    dve.scalar_tensor_tensor(h[:, k, :], tmp[:, k % 2, :], gain(layer, post, k), h[:, k, :],
                                             ALU.mult, ALU.add).then_inc(h_added, 1)
                    if k == 5 and late is not None:
                        lo_part(late)
                if split:
                    lo(KC - 1)

            def ffn_layer(layer, n_post):
                invert(n_post + 1)
                dve.wait_ge(r_ready, spreads(n_post + 1))
                dve.wait_ge(out_stored, 16 * MIXER_STORES[layer])
                base = U_FI[layer]
                fb = FC * layer

                def tiles_pair(i, following, i2, step2, looped):
                    for f in range(2):
                        at = (lambda v: i * 2 + (fb + f + v))
                        gate, up = pair(4 * f), pair(4 * f + 2)
                        r = halves(r_pre[:, :])
                        dve.wait_ge(w_used, i * 4 + (base + 2 * f + 2))
                        dve.wait_ge(m_lo, at(0))
                        dve.tensor_tensor(halves(tmp[:, 0, :]), gate, r, ALU.mult)
                        dve.tensor_tensor(halves(tmp[:, 1, :]), up, r, ALU.mult).then_inc(gu_scaled, 1)
                        lo_part(following + 2 * f, i2, step2)
                        dve.wait_ge(silu_done, at(1))
                        dve.tensor_tensor(tmp2[:, 1, :], tmp2[:, 0, :], tmp[:, 1, :], ALU.mult).then_inc(m_ready, 1)
                        dve.wait_ge(m_hi, at(1))
                        c = bass.ds(i * 2 + f, 1)
                        dve.tensor_tensor(mlo[:, c, :].rearrange("p o n -> p (o n)"), tmp2[:, 1, :],
                                          mhi[:, c, :].rearrange("p o n -> p (o n)").bitcast(F32), ALU.subtract)\
                            .then_inc(m_lo, 1)
                        lo_part(following + 2 * f + 1, i2, step2)

                with dve.Fori(0, FC // 2 - 1) as i:
                    tiles_pair(i, base + 4, i, 4, True)
                tiles_pair(FC // 2 - 1, U_FO[layer], 0, 0, False)
                base = U_FO[layer]
                s = 2 * layer + 1
                dve.wait_ge(acc_zeroed, s + 1)
                with dve.Fori(0, KC // 2 - 1) as i:
                    for d in range(2):
                        for j in range(4):
                            lo_part(base + 4 * d + j + 4, i, 8)
                        add_squares(s, d, d, i, 2)
                for d in range(2):
                    for j in range(4):
                        m = base + 8 * (KC // 2 - 1) + 4 * d + j + 4
                        if m < U_END and not (d == 1 and j == 3):
                            lo_part(m)
                    add_squares(s, KC - 2 + d, d)

            residual(0, 0, 1, (8, lambda k: gain(0, 2, k)), U_OUT + 11)
            ffn_layer(0, 1)
            residual(1, 0, 3, None, U_C + 3)

            invert(4)
            dve.wait_ge(band_loaded, 64)
            dve.wait_ge(rstd_ready, 5)
            dve.tensor_scalar(band_r[0][:, :, :], band_first[:, :, :], rstd[:, 0:1], None, ALU.mult)
            dve.tensor_scalar(band_r[NT - 1][0:TAIL, :, :], band_last[0:TAIL, :, :], rstd[0:TAIL, NT - 1:NT], None, ALU.mult)
            dve.tensor_scalar(band_r[1][:, :, :], band_later[:, :, :], rstd[:, 1:2], None, ALU.mult).then_inc(band_dve, 1)
            dve.wait_ge(acc_zeroed, 3)
            for j in range(len(GROUPS) + 1):
                for o in range(2):
                    if j < len(GROUPS):
                        c = 2 * GROUPS[j] + o
                        dve.wait_ge(x_hi, 16 + 2 * j + o + 1)
                        dve.tensor_tensor(xlo[:, c, :], flat(2 * o, POOL_AT, TOK), xhi[:, c, :].bitcast(F32), ALU.subtract)\
                            .then_inc(x_lo, 1)
                for o in range(2):
                    if j:
                        add_squares(2, 2 * (j - 1) + o, o)
                if 1 <= j <= 3:
                    lo_part(U_FI[1] + j - 1)
            residual(2, 1, 1, (24, lambda k: gain(1, 2, k)), U_FI[1] + 3)
            ffn_layer(1, 5)
            residual(3, 1, 3, None, None)
            for t in (1, 3):
                dve.wait_ge(y_turned, t + 1)
                dve.tensor_copy(y_tok[:, t, :], flat(2 * t, 0, D)).then_inc(y_ready_dve, 1)

        @block.gpsimd
        def _(pool):
            pool.memset(eps[:, :], EPS)
            pool.memset(ssq[:, :], 1.0)
            pool.memset(ones[:, :], 1.0).then_inc(set_up, 1)
            pool.memset(k_s[:, DEC:CHUNK], 0.0)
            pool.memset(mask_s[:, 0:DEC], 0.0)
            pool.memset(mask_s[:, CHUNK:P], 0.0)
            pool.memset(mask_s[:, DEC:CHUNK], MASKED).then_inc(set_sample, 1)
            pool.memset(mean_var[:, :, :], 1.0).then_inc(set_stats, 1)
            pool.memset(acc_post[:, :], 0.0).then_inc(acc_zeroed, 1)
            pool.wait_ge(ln_loaded, 32)
            for t, (t0, n) in enumerate(TILES):
                pool.wait_ge(va_normed, t + 1)
                pool.tensor_tensor(va[0:n, t, :], va[0:n, t, :], ln_gb[0:n, 0, :], ALU.mult).then_inc(va_scaled, 1)
            for t, (t0, n) in enumerate(TILES):
                pool.wait_ge(va_scaled, t + 1)
                pool.tensor_tensor(va[0:n, t, :], va[0:n, t, :], ln_gb[0:n, 1, :], ALU.add).then_inc(va_ready, 1)
            pool.wait_ge(va_ready, NT)
            pool.dma_start(av_s[0, 0].rearrange("t h c -> t (h c)"), va[0:DEC, NT - 1, :]).then_inc(out_stored, 16)
            pool.wait_ge(v_evacuated, 2)
            pool.dma_start(bv_p[0, 0].rearrange("t g d -> t (g d)"), v_t[:, 3, :]).then_inc(out_stored, 16)
            pool.dma_start(bv_s[0, 0].rearrange("t g d -> t (g d)"), v_s[0:DEC, :]).then_inc(out_stored, 16)
            pool.wait_ge(rope_done, 1)
            pool.tensor_copy(k_s[:, 0:DEC], k_r[:, SEQ:TOK]).then_inc(k_s_ready, 1)
            pool.wait_ge(k_out_ready, 1)
            pool.dma_start(bk_p[0, 0].rearrange("t g d -> t (g d)"), k_out[:, 0, :]).then_inc(out_stored, 16)
            pool.dma_start(bk_s[0, 0].rearrange("t g d -> t (g d)"), k_out[0:DEC, 1, :]).then_inc(out_stored, 16)
            for c in range(NCH + 1):
                n, b = (2, c % 2) if c == NCH else (4, c % 2)
                w = CHUNK if c == 0 else P
                p = s_sb[:, b, 0:n * P].rearrange("p (c s) -> p c s", c=n)[:, :, 0:w]
                pool.wait_ge(rden_ready, c + 1)
                pool.tensor_tensor(p, p, rden[:, b, 0:n].unsqueeze(2).broadcast_to([P, n, w]), ALU.mult).then_inc(p_ready, 1)
            for t in range(AH):
                pool.wait_ge(u_gelu, t + 1)
                pool.wait_ge(gate_biased, t + 1)
                pool.tensor_tensor(gated[:, t, :], gated[:, t, :], u_raw[:, t, :], ALU.mult).then_inc(ya_ready, 1)

            def add_squares(s):
                pool.wait_ge(h_squared, 8 * s + 1)
                pool.sem_inc(pre_added, 1)
                for k in range(1, KC):
                    pool.wait_ge(h_squared, 8 * s + k + 1)
                    pool.wait_ge(pre_added, 8 * s + k)
                    pool.tensor_tensor(acc_pre[:, :], acc_pre[:, :], tmp2[:, k % 2, :], ALU.add).then_inc(pre_added, 1)

            def zero_sum(n):
                pool.wait_ge(sum_ready, n)
                pool.memset(acc_post[:, :], 0.0).then_inc(acc_zeroed, 1)

            add_squares(0)
            zero_sum(1)
            pool.wait_ge(w_used, U_FO[0] + 4 * KC)
            c = (4 + 0) * KC
            pool.tensor_tensor(gain_diag[:, :, :], ident[:, :].unsqueeze(1).broadcast_to([P, KC, P]),
                               gains[:, c:c + KC].unsqueeze(2).broadcast_to([P, KC, P]), ALU.mult).then_inc(diag_ready, 1)
            pool.dma_start(h_tok[TAIL:TAIL + HIST, NT - 1, :], state[0, 0]).then_inc(hist_loaded, 16)
            c = P + 2 * TOK
            for dst in (band_first, band_later, band_last):
                n = 4 * dst.shape[2]
                pool.dma_start(dst[:, :, :].rearrange("p g n -> p (g n)"), constants[:, c:c + n]).then_inc(band_loaded, 16)
                c += n
            pool.dma_start(band_r[NT - 1][TAIL:TAIL + HIST, :, :].rearrange("p g n -> p (g n)"),
                           constants[TAIL:TAIL + HIST, c - n:c]).then_inc(band_loaded, 16)
            zero_sum(3)
            add_squares(1)
            pool.wait_ge(h_tok_ready, KC)
            pool.wait_ge(rstd_ready, 5)
            pool.tensor_scalar(pool_out[0:TAIL, :], h_tok[0:TAIL, NT - 1, :], rstd[0:TAIL, NT - 1:NT], None, ALU.mult)\
                .then_inc(pool_out_ready, 1)
            pool.wait_ge(pool_out_ready, 1)
            pool.dma_start(cp_p[0, 0], pool_out[TAIL_SEQ - HIST:TAIL_SEQ, :]).then_inc(out_stored, 16)
            pool.dma_start(cp_s[0, 0], pool_out[TAIL - HIST:TAIL, :]).then_inc(out_stored, 16)
            pool.wait_ge(out_stored, 16 * MIXER_STORES[1])
            add_squares(2)
            zero_sum(5)


_INS = ["x_prompt", "x_sample", "cache_b_k", "cache_b_v", "state_c_pool", "norm_g", "ab_w_in", "a_ln_g", "a_ln_b",
        "a_ws", "a_bs", "b_sinks", "ab_w_out", "c_w", "c_scale", "ffn_w_in", "ffn_w_out"]
_OUTS = [(1, SEQ, D), (1, DEC, D), (1, 1, WIN, NKV, HD), (1, 1, WIN, NKV, HD), (1, 1, HIST, D),
         (1, 1, DEC, NKV, HD), (1, 1, DEC, NKV, HD), (1, 1, HIST, D), (1, 1, DEC, AH, P)]


def kernel(**inputs):
    import numpy as _np
    import concourse.bacc as _bacc
    from concourse import mybir as _mybir
    from concourse.bass_utils import run_bass_kernel_spmd as _run

    nc = _bacc.Bacc("TRN2", target_bir_lowering=False, num_devices=1)
    arrays, args = {}, []
    named = [(name, _np.ascontiguousarray(inputs[name])) for name in _INS] + [("constants", shape_constants())]
    for name, a in named:
        arrays[f"in_{name}_dram"] = a
        args.append(nc.dram_tensor(f"in_{name}_dram", a.shape, _mybir.dt.from_np(a.dtype), kind="ExternalInput").ap())
    for i, shape in enumerate(_OUTS):
        args.append(nc.dram_tensor(f"out_{i}_dram", shape, _mybir.dt.float32, kind="ExternalOutput").ap())
    build(nc, *args)
    r = _run(nc, [arrays], core_ids=[0])
    return tuple(r.results[0][f"out_{i}_dram"] for i in range(len(_OUTS)))
```

```python
from contextlib import ExitStack

import concourse.bass as bass
import numpy as np
from concourse import mybir

F32 = mybir.dt.float32
F32R = mybir.dt.float32r
ACT = mybir.ActivationFunctionType
ALU = mybir.AluOpType
AX = mybir.AxisListType

P = 128
D = 1024
KC = D // P
SEQ, DEC, PAST = 512, 32, 1024
TOK = SEQ + DEC
HALF = TOK // 2
DFF = 2816
FC = DFF // P
CHUNK = 64
NCH = SEQ // CHUNK
HD = 64
AW = 512
AH = 4
NQ, NKV = 8, 2
ROPE, THETA = 16, 500000.0
WIN = 128
HIST = 15
POOLS = (2, 4, 8, 16)
EPS = 1e-6
MASKED = -1e30
SCALE = HD ** -0.5
TILES = [(t * P, P) for t in range(SEQ // P)] + [(SEQ, DEC)]
NT = len(TILES)
STEP = P - HIST
POOL_TILES = [(t * STEP, min(P, TOK - t * STEP)) for t in range(-(-SEQ // STEP))]
POOL_OUT = [(t0 + (HIST if t0 else 0), t0 + n) for t0, n in POOL_TILES]
TAIL, TAIL_SEQ = POOL_TILES[-1][1], SEQ - POOL_TILES[-1][0]
TAIL_OUT = TOK - POOL_OUT[-1][0]
POOL_AT = 512 - POOL_OUT[-1][0]
assert len(POOL_TILES) == NT and TAIL + HIST <= P
PIECES = ((0, 6), (6, 12), (12, 17), (17, 22))
MIXER_STORES = (5, 7)
U_STEPS = (3, 3, 2, 3, 3, 2, 3, 3, 2, 4, 4)
U_THROUGH = (2, 5, 8)
GATE_BANKS = (0, 2, 4, 0)
OUT_STEPS = [(d, None) for d in range(4)] + [(d, b) for b in range(2) for d in range(4, KC)]
OUT_BANKS = (2, 4, 0)
NORM_POST = (1, 4, 7, 10)
Z_BEFORE = (0, len(OUT_STEPS), len(OUT_STEPS) + KC + 1, len(OUT_STEPS) + 3 * KC + 1)
H_BEFORE = (0, 2 * KC, 4 * KC, 6 * KC)
SHARED = (0, 2, 3)
SCALED_DVE_BEFORE, SCALED_POOL_BEFORE = (0, KC, 3 * KC, 4 * KC), (0, None, KC, 2 * KC)
X_FFN, X_POOL = (KC, 4 * KC), 3 * KC
POOL_BANKS = ((4, 5), (0, 1, 2, 3))
SUM_AT, SPREAD_AT = (0, 0), (3, 3)

U_IN = 0
U_OUT = U_IN + 14
U_FI = (U_OUT + KC, U_OUT + KC + 2 * FC + 4 * KC + 2)
U_FO = (U_FI[0] + 2 * FC, U_FI[1] + 2 * FC)
U_C = U_FO[0] + 4 * KC
U_END = U_FO[1] + 4 * KC
NRAW, NSPLIT = 2, 4
assert U_C + 2 == U_FI[1]
UNIT = 8 * P


def unit_columns(m):
    for base in U_FO:
        if base <= m < base + 4 * KC:
            a, b = PIECES[(m - base) % 4]
            return (b - a) * P
    return UNIT


def unit_dmas(m):
    if U_IN + 6 <= m < U_IN + 10:
        return 2
    return 3 if U_OUT <= m < U_FI[0] else 1


def loaded(m):
    return 16 * sum(unit_dmas(j) for j in range(m % NRAW, m + 1, NRAW))


def shape_constants():
    pos = np.concatenate([np.arange(SEQ), PAST + np.arange(DEC)]).astype(np.float32)
    inv = np.float32(THETA) ** (-np.arange(ROPE // 2, dtype=np.float32) * np.float32(2.0) / np.float32(ROPE))
    ang = (pos[:, None] * inv.astype(np.float32)[None, :]).astype(np.float32)
    cos, sin = np.ones((P, TOK), np.float32), np.zeros((P, TOK), np.float32)
    for p in range(P):
        d = p % HD
        if d < ROPE:
            cos[p] = np.cos(ang[:, d % (ROPE // 2)])
            sin[p] = np.sin(ang[:, d % (ROPE // 2)]) * (-1.0 if d < ROPE // 2 else 1.0)
    return np.concatenate([np.eye(P, dtype=np.float32), cos, sin, pooling_matrices()], axis=1)


def pooling_matrices():
    i, j = np.arange(P)[None, :], np.arange(P)[:, None]
    row_at = np.concatenate([np.arange(TAIL_SEQ), np.arange(TAIL - TAIL_SEQ), np.arange(-HIST, 0)])[:, None]
    row_stream = (np.arange(TAIL + HIST) >= TAIL_SEQ)[:, None]
    col_at, col_stream = row_at[HIST:TAIL].T, row_stream[HIST:TAIL].T
    first, later, last = [], [], []
    for w in POOLS:
        inside = (j <= i) & (j > i - w)
        first.append(inside / np.minimum(i + 1, w) - (i == j))
        later.append((inside / w - (i == j))[:, HIST:])
        tail = np.zeros((P, TAIL_OUT))
        tail[:TAIL + HIST] = (row_stream == col_stream) * (((row_at <= col_at) & (row_at > col_at - w)) / w
                                                          - (row_at == col_at))
        last.append(tail)
    return np.concatenate(first + later + last, axis=1).astype(np.float32)


def build(nc, x_prompt, x_sample, cache_k, cache_v, state, norm_g, ab_w_in, ln_g, ln_b, a_ws, a_bs, b_sinks,
          ab_w_out, c_w, c_scale, ffn_w_in, ffn_w_out, constants,
          y_p, y_s, bk_p, bv_p, cp_p, bk_s, bv_s, cp_s, av_s):
    with ExitStack() as ctx:
        def sb(name, shape, dt=F32, scope=ctx):
            return scope.enter_context(nc.sbuf_tensor(name, shape, dt))

        def sem(name):
            return ctx.enter_context(nc.semaphore(name))

        ps = ctx.enter_context(nc.psum_tensor("ps", [P, 8 * 512], F32))

        def flat(b, c0, n, p=P):
            return ps[0:p, b * 512 + c0:b * 512 + c0 + n]

        def pair(b):
            return ps[:, b * 512:(b + 2) * 512].rearrange("p (b n) -> p b n", b=2)[:, :, 0:HALF]

        def frames(b):
            return slice(b * HALF, (b + 1) * HALF)

        def quarter(k):
            return tmp[:, k % 2, frames(k // 2 % 2)]

        def halves(ap):
            return ap.rearrange("p (b n) -> p b n", b=2)

        h = sb("h", [P, KC, TOK])
        xhi = sb("xhi", [P, KC, TOK], F32R)
        with ExitStack() as used:
            xlo = sb("xlo", [P, KC, TOK], F32R, used)
        z = sb("z", [P, KC, TOK])
        raw = sb("raw", [P, NRAW, UNIT])
        whi = sb("whi", [P, NSPLIT, UNIT], F32R)
        wlo = sb("wlo", [P, NSPLIT, UNIT], F32R)
        r_post = sb("r_post", [P, TOK])
        r_pre = sb("r_pre", [P, TOK])
        acc_post = sb("acc_post", [P, TOK])
        acc_pre = sb("acc_pre", [P, TOK])
        tmp = sb("tmp", [P, 2, TOK])
        tmp2 = sb("tmp2", [P, 2, TOK])
        ident = sb("ident", [P, P])
        gains = sb("gains", [P, 72])
        ssq = sb("ssq", [P, NT])
        rms = sb("rms", [P, 6])
        rstd = sb("rstd", [P, 6])
        eps = sb("eps", [P, 1])
        ones = sb("ones", [P, 1])
        warmed = sb("warmed", [P, 1])

        def gain(layer, j, k):
            c = (layer * 4 + j) * KC + k
            return gains[:, c:c + 1]

        def scale_c(k):
            return gains[:, 64 + k:65 + k]

        with ExitStack() as ab:
            ab_sb = lambda name, shape, dt=F32: sb(name, shape, dt, ab)
            yhi = ab_sb("yhi", [P, KC, TOK], F32R)
            ylo = ab_sb("ylo", [P, KC, TOK], F32R)
            u_raw = ab_sb("u_raw", [P, AH, TOK])
            gated = ab_sb("gated", [P, AH, TOK])
            va = ab_sb("va", [P, NT, AW])
            ln_gb = ab_sb("ln_gb", [P, 2, AW])
            bs_b = ab_sb("bs_b", [P, AH, P])
            cossin = ab_sb("cossin", [P, 2, TOK])
            q_r = ab_sb("q_r", [P, 4 * TOK])
            k_r = ab_sb("k_r", [P, TOK])
            v_t = ab_sb("v_t", [P, 4, P])
            v_even = ab_sb("v_even", [P, 4, P])
            v_s = ab_sb("v_s", [P, P])
            k_s = ab_sb("k_s", [P, P])
            wm_t = ab_sb("wm_t", [P, AH, P])
            s_sb = ab_sb("s_sb", [P, 2, 512])
            p_t = ab_sb("p_t", [P, 512])
            k_out = ab_sb("k_out", [P, 2, P])
            mask_s = ab_sb("mask_s", [P, P])
            sinks = ab_sb("sinks", [P, NQ])
            sink_p = ab_sb("sink_p", [P, 4])
            sink_s = ab_sb("sink_s", [P, 2])
            top = ab_sb("top", [P, 2, 4])
            peak = ab_sb("peak", [P, 2, 4])
            sunk = ab_sb("sunk", [P, 2, 4])
            den = ab_sb("den", [P, 2, 4])
            den2 = ab_sb("den2", [P, 2, 4])
            rden = ab_sb("rden", [P, 2, 4])
            stats = ab_sb("stats", [P, NT, 6])
            mean_var = ab_sb("mean_var", [P, NT, 2])
            ln_rms = ab_sb("ln_rms", [P, NT])
            ln_rstd = ab_sb("ln_rstd", [P, NT])
        with ExitStack() as first:
            x_tok = sb("x_tok", [P, NT, D], F32, first)
            gain_rows = sb("gain_rows", [72, P], F32, first)
            ws = sb("ws", [P, AH, P], F32, first)
            k_cache = sb("k_cache", [CHUNK, P], F32, first)
        with ExitStack() as ffn:
            mhi = sb("mhi", [P, FC, TOK], F32R, ffn)
            mlo = sb("mlo", [P, FC, TOK], F32R, ffn)
        with ExitStack() as pool_scope:
            h_tok = sb("h_tok", [P, NT, D], F32, pool_scope)
            z_pool = sb("z_pool", [P, KC, TOK], F32, pool_scope)
            pool_out = sb("pool_out", [P, D], F32, pool_scope)
            gain_diag = sb("gain_diag", [P, KC, P], F32, pool_scope)
            band_first = sb("band_first", [P, 4, P], F32, pool_scope)
            band_later = sb("band_later", [P, 4, STEP], F32, pool_scope)
            band_last = sb("band_last", [P, 4, TAIL_OUT], F32, pool_scope)
            band_r = [sb(f"band_r{t}", [P, 4, b - a], F32, pool_scope) for t, (a, b) in enumerate(POOL_OUT)]
        with ExitStack() as end:
            y_tok = sb("y_tok", [P, NT, D], F32, end)

        w_loaded = [sem(f"w_loaded{i}") for i in range(NRAW)]
        w_hi, w_lo, w_used = sem("w_hi"), sem("w_lo"), sem("w_used")
        x_loaded = [sem(f"x_loaded{i}") for i in range(NT)]
        ident_loaded, gains_loaded, rope_loaded = sem("ident_loaded"), sem("gains_loaded"), sem("rope_loaded")
        ws_loaded, bs_loaded, ln_loaded = sem("ws_loaded"), sem("bs_loaded"), sem("ln_loaded")
        sinks_loaded, kc_loaded, vc_loaded = sem("sinks_loaded"), sem("kc_loaded"), sem("vc_loaded")
        hist_loaded, band_loaded = sem("hist_loaded"), sem("band_loaded")
        set_up, set_sample, set_stats, set_gaps = sem("set_up"), sem("set_sample"), sem("set_stats"), sem("set_gaps")
        gains_turned, gains_ready = sem("gains_turned"), sem("gains_ready")
        x_turned, x_squared = sem("x_turned"), sem("x_squared")
        h_first_even, h_first_odd = sem("h_first_even"), sem("h_first_odd")
        ws_turned, wm_ready, kc_turned, kc_ready = sem("ws_turned"), sem("wm_ready"), sem("kc_turned"), sem("kc_ready")
        sum_ready, rms_ready, rstd_ready = sem("sum_ready"), sem("rms_ready"), sem("rstd_ready")
        rstd_spread, r_ready = sem("rstd_spread"), sem("r_ready")
        z_evacuated, acc_zeroed, acc_added = sem("z_evacuated"), sem("acc_zeroed"), sem("acc_added")
        half_scaled_dve, half_scaled_pool = sem("half_scaled_dve"), sem("half_scaled_pool")
        h_added, h_squared, pre_added = sem("h_added"), sem("h_squared"), sem("pre_added")
        x_hi, x_lo = sem("x_hi"), sem("x_lo")
        va_gelu, va_stats, va_bn, ln_rms_ready = sem("va_gelu"), sem("va_stats"), sem("va_bn"), sem("ln_rms_ready")
        ln_rstd_ready, va_normed, va_scaled, va_ready = sem("ln_rstd_ready"), sem("va_normed"), sem("va_scaled"), sem("va_ready")
        v_evacuated, rope_swapped, rope_sined, rope_cosined = sem("v_evacuated"), sem("rope_swapped"), sem("rope_sined"), sem("rope_cosined")
        rope_done, k_s_ready, k_turned, k_out_ready = sem("rope_done"), sem("k_s_ready"), sem("k_turned"), sem("k_out_ready")
        gate_done, gate_biased, sinks_ready = sem("gate_done"), sem("gate_biased"), sem("sinks_ready")
        scored, s_masked, topped, peaked = sem("scored"), sem("s_masked"), sem("topped"), sem("peaked")
        shifted, sink_shifted, exp_done, summed = sem("shifted"), sem("sink_shifted"), sem("exp_done"), sem("summed")
        den_ready, rden_ready, p_ready = sem("den_ready"), sem("rden_ready"), sem("p_ready")
        p_turned, p_t_ready, pv_done, att_hi, att_lo = sem("p_turned"), sem("p_t_ready"), sem("pv_done"), sem("att_hi"), sem("att_lo")
        u_evacuated, u_gelu, ya_ready, ya_hi, ya_lo = sem("u_evacuated"), sem("u_gelu"), sem("ya_ready"), sem("ya_hi"), sem("ya_lo")
        ya_last, v_copied, v_turned, v_ready, rope_scaled = sem("ya_last"), sem("v_copied"), sem("v_turned"), sem("v_ready"), sem("rope_scaled")
        gu_scaled, silu_done, m_ready, m_hi, m_lo = sem("gu_scaled"), sem("silu_done"), sem("m_ready"), sem("m_hi"), sem("m_lo")
        diag_ready, h_turned, h_tok_ready = sem("diag_ready"), sem("h_turned"), sem("h_tok_ready")
        band_dve, band_act, pooled, pool_out_ready = sem("band_dve"), sem("band_act"), sem("pooled"), sem("pool_out_ready")
        pool_done, out_half_done, ffn_half_done = sem("pool_done"), sem("out_half_done"), sem("ffn_half_done")
        z_squared = sem("z_squared")
        y_turned, y_ready_act, y_ready_dve = sem("y_turned"), sem("y_ready_act"), sem("y_ready_dve")
        y_stored, out_stored = sem("y_stored"), sem("out_stored")

        def spreads(n):
            return n + 1 if n < 6 else n

        def h_first_wait(engine, k):
            engine.wait_ge(h_first_odd if k % 2 else h_first_even, k // 2 + 1)

        block = ctx.enter_context(nc.Block())

        @block.sync
        def _(sp):
            rows = ab_w_in[0].rearrange("(k p) n -> p k n", p=P)
            out_rows = ab_w_out[0]

            def raw_free(m):
                if m >= NRAW:
                    sp.wait_ge(w_lo, m - NRAW + 1)

            def tiles(m, n=UNIT):
                return raw[:, m % NRAW, 0:n]

            for t, (t0, n) in enumerate(TILES):
                src = x_prompt[0, t0:t0 + n, :] if t0 < SEQ else x_sample[0]
                sp.dma_start(x_tok[0:n, t, :], src).then_inc(x_loaded[t], 16)
            for j in range(4):
                m = U_IN + j
                raw_free(m)
                sp.dma_start(tiles(m).rearrange("p (k n) -> p k n", k=2), rows[:, 2 * j:2 * j + 2, AW:2 * AW])\
                    .then_inc(w_loaded[m % NRAW], 16)
            qo = 2 * AW
            ko, vo = qo + NQ * HD, qo + NQ * HD + NKV * HD
            for j, c in enumerate((vo, ko)):
                m = U_IN + 4 + j
                raw_free(m)
                sp.dma_start(tiles(m).rearrange("p (k n) -> p k n", k=KC), rows[:, :, c:c + P])\
                    .then_inc(w_loaded[m % NRAW], 16)
            for t in range(4):
                m = U_IN + 6 + t
                raw_free(m)
                for g in range(NKV):
                    c = qo + (4 * g + t) * HD
                    sp.dma_start(tiles(m).rearrange("p (k g n) -> p k g n", k=KC, g=NKV)[:, :, g, :],
                                 rows[:, :, c:c + HD]).then_inc(w_loaded[m % NRAW], 16)
            for t in range(4):
                m = U_IN + 10 + t
                raw_free(m)
                sp.dma_start(tiles(m).rearrange("p (k n) -> p k n", k=KC), rows[:, :, t * P:(t + 1) * P])\
                    .then_inc(w_loaded[m % NRAW], 16)
            for d in range(KC):
                m = U_OUT + d
                raw_free(m)
                dst = tiles(m).rearrange("p (k n) -> p k n", k=KC)
                cols = slice(d * P, (d + 1) * P)
                sp.dma_start(dst[:, 0:4, :], out_rows[0:AW, cols].rearrange("(k p) n -> p k n", p=P))\
                    .then_inc(w_loaded[m % NRAW], 16)
                for g in range(NKV):
                    r = AW + g * 4 * HD
                    sp.dma_start(dst[g * HD:(g + 1) * HD, 4:8, :],
                                 out_rows[r:r + 4 * HD, cols].rearrange("(t d) n -> d t n", t=4))\
                        .then_inc(w_loaded[m % NRAW], 16)

            def load_ffn(layer):
                w_in = ffn_w_in[layer].rearrange("(k p) n -> p k n", p=P)
                w_out = ffn_w_out[layer].rearrange("(c p) n -> p c n", p=P)
                base = U_FI[layer]
                with sp.Fori(0, FC // 2) as i:
                    for j in range(4):
                        m = base + j
                        sp.wait_ge(w_lo, i * 4 + (m - NRAW + 1))
                        col = i * (2 * P) + ((j // 2) * P + (j % 2) * DFF)
                        sp.dma_start(tiles(m).rearrange("p (k n) -> p k n", k=KC), w_in[:, :, bass.ds(col, P)])\
                            .then_inc(w_loaded[m % NRAW], 16)
                base = U_FO[layer]
                with sp.Fori(0, KC // 2) as i:
                    for j in range(8):
                        m = base + j
                        sp.wait_ge(w_lo, i * 8 + (m - NRAW + 1))
                        a, b = PIECES[j % 4]
                        col = i * (2 * P) + (j // 4) * P
                        sp.dma_start(tiles(m, (b - a) * P).rearrange("p (c n) -> p c n", n=P),
                                     w_out[:, a:b, bass.ds(col, P)]).then_inc(w_loaded[m % NRAW], 16)

            load_ffn(0)
            for j in range(2):
                m = U_C + j
                raw_free(m)
                sp.dma_start(tiles(m).rearrange("p (k n) -> p k n", k=4),
                             c_w[0, 2 * j:2 * j + 2].rearrange("g m n -> (g m) n").rearrange("(k p) n -> p k n", p=P))\
                    .then_inc(w_loaded[m % NRAW], 16)
            sp.wait_ge(w_used, U_FO[0] + 4 * KC)
            sp.dma_start(h_tok[TAIL:TAIL + HIST, NT - 1, :], state[0, 0]).then_inc(hist_loaded, 16)
            c = P + 2 * TOK
            for dst in (band_first, band_later, band_last):
                n = 4 * dst.shape[2]
                sp.dma_start(dst[:, :, :].rearrange("p g n -> p (g n)"), constants[:, c:c + n]).then_inc(band_loaded, 16)
                c += n
            sp.dma_start(band_r[NT - 1][TAIL:TAIL + HIST, :, :].rearrange("p g n -> p (g n)"),
                           constants[TAIL:TAIL + HIST, c - n:c]).then_inc(band_loaded, 16)
            load_ffn(1)
            for t, (t0, n) in enumerate(TILES):
                sp.wait_ge(y_ready_act, min(t, 2) + 1 if t < NT - 1 else NT - 1)
                if t == 3:
                    sp.wait_ge(y_ready_dve, 1)
                dst = y_p[0, t0:t0 + n, :] if t0 < SEQ else y_s[0]
                sp.dma_start(dst, y_tok[0:n, t, :]).then_inc(y_stored, 16)
            sp.wait_ge(y_stored, 16 * NT)

        @block.tensor
        def _(pe):
            def product(out, wh, wl, xh, xl, first, last):
                pe.matmul(out, wh, xh, start=first, stop=False)
                pe.matmul(out, wh, xl, start=False, stop=False)
                return pe.matmul(out, wl, xh, start=False, stop=last)

            def one_half(bank, b, m, tile, hi, lo, k, first, last):
                s = m % NSPLIT
                wh, wl = whi[:, s, tile * P:(tile + 1) * P], wlo[:, s, tile * P:(tile + 1) * P]
                return product(flat(bank + b, 0, HALF), wh, wl, hi[:, k, frames(b)], lo[:, k, frames(b)], first, last)

            def both_halves(bank, m, tile, hi, lo, k, first, last):
                for b in range(2):
                    mm = one_half(bank, b, m, tile, hi, lo, k, first, last)
                return mm

            def sum_squares_half(n, b):
                for t, c in enumerate((0, P, HALF - P)):
                    c += b * HALF
                    mm = pe.matmul(flat(6, 3 * b + t, 1), acc_post[:, c:c + P], ones[:, :], start=True, stop=True)
                mm.then_inc(sum_ready, 1)

            def spread_half(n, b):
                pe.wait_ge(rstd_ready, n + 1)
                for t, w in enumerate((P, P, HALF - 2 * P)):
                    lhs, rhs = rstd[:, 3 * b + t:3 * b + t + 1].broadcast_to([P, P]), ident[:, P - w:P]
                    mm = pe.matmul(flat(6, P + t * P, w), lhs, rhs, start=True, stop=True)
                mm.then_inc(rstd_spread, 1)

            def sum_squares(n, acc):
                for t in range(NT):
                    c, w = POOL_TILES[t] if n == 6 else (t * P if t < NT - 1 else TOK - P, P)
                    mm = pe.matmul(flat(6, t, 1, w), acc[:, c:c + w], ones[:, :], start=True, stop=True)
                mm.then_inc(sum_ready, 1)

            def spread(n):
                pe.wait_ge(rstd_ready, n + 1)
                for t, (t0, w) in enumerate(TILES):
                    if n == 0:
                        lhs, rhs = rstd[0:w, t:t + 1].broadcast_to([w, P]), ident[0:w, 0:w]
                    else:
                        lhs, rhs = rstd[:, t:t + 1].broadcast_to([P, P]), ident[:, P - w:P]
                    mm = pe.matmul(flat(6, P + t0, w), lhs, rhs, start=True, stop=True)
                mm.then_inc(rstd_spread, 1)

            pe.wait_ge(ident_loaded, 16)
            pe.wait_ge(gains_loaded, 32)
            pe.transpose(flat(7, 0, 72), gain_rows[:, :], ident[0:72, 0:72]).then_inc(gains_turned, 1)
            for k in range(KC):
                if k >= 4:
                    h_first_wait(pe, k - 4)
                if k == 3:
                    pe.wait_ge(gains_ready, 1)
                for t, (t0, n) in enumerate(TILES):
                    if k == 0:
                        pe.wait_ge(x_loaded[t], 16)
                    mm = pe.transpose(flat(2 * (k % 4), t0, n), x_tok[0:n, t, k * P:(k + 1) * P], ident[0:n, 0:n])
                mm.then_inc(x_turned, 1)

            h_first_wait(pe, 5)
            h_first_wait(pe, 6)
            for j in range(4):
                m = U_IN + j
                s = m % NSPLIT
                pe.wait_ge(w_lo, m + 1)
                pe.wait_ge(x_lo, 2 * j + 2)
                for t, (t0, n) in enumerate(TILES):
                    for c in range(2):
                        k = 2 * j + c
                        mm = product(flat(t, 0, AW, n), xhi[:, k, t0:t0 + n], xlo[:, k, t0:t0 + n],
                                     whi[:, s, c * AW:(c + 1) * AW], wlo[:, s, c * AW:(c + 1) * AW],
                                     k == 0, k == KC - 1)
                mm.then_inc(w_used, 1)
            h_first_wait(pe, 7)
            spread(0)
            m = U_IN + 4
            pe.wait_ge(w_lo, m + 1)
            for b in range(2):
                if b:
                    pe.wait_ge(va_gelu, 1)
                for k in range(KC):
                    mm = one_half((5, -1)[b], b, m, k, xhi, xlo, k, k == 0, k == KC - 1)
            mm.then_inc(w_used, 1)
            def gate(a):
                if a < 3:
                    pe.wait_ge(rope_cosined, a + 2)
                else:
                    pe.wait_ge(gate_biased, 1)
                for t, (t0, n) in enumerate(TILES):
                    mm = pe.matmul(flat(GATE_BANKS[a], t0, n), va[0:n, t, a * P:(a + 1) * P], wm_t[0:n, a, 0:n],
                                   start=True, stop=True)
                mm.then_inc(gate_done, 1)

            for r, bank in enumerate((6, 0, 2, 4, 6)):
                m = U_IN + 5 + r
                pe.wait_ge(w_lo, m + 1)
                if r == 0:
                    pe.wait_ge(r_ready, 1)
                if r == 1:
                    pe.wait_ge(v_copied, 2)
                    pe.wait_ge(va_gelu, NT)
                    for t, (t0, n) in enumerate(TILES):
                        out = flat(5, t * P, P) if t < NT - 1 else flat(4, 0, P, n)
                        mm = pe.transpose(out, gated[:, AH - 1, t0:t0 + n], ident[:, :])
                    mm.then_inc(v_turned, 1)
                if r == 2:
                    pe.wait_ge(v_evacuated, 2)
                    pe.wait_ge(ws_loaded, 16)
                    for a in range(AH):
                        mm = pe.transpose(flat(4, a * P, P), ws[:, a, :], ident[:, :])
                    mm.then_inc(ws_turned, 1)
                    pe.wait_ge(kc_loaded, 16)
                    pe.transpose(flat(5, 0, CHUNK), k_cache[:, :], ident[0:CHUNK, 0:CHUNK]).then_inc(kc_turned, 1)
                if r == 3:
                    pe.wait_ge(rope_cosined, 1)
                    pe.wait_ge(rope_done, 1)
                    pe.transpose(flat(6, 0, P), k_r[:, SEQ - P:SEQ], ident[:, :])
                    pe.transpose(flat(6, P, P, DEC), k_r[:, SEQ:TOK], ident[:, :]).then_inc(k_turned, 1)
                    pe.wait_ge(wm_ready, 1)
                    pe.wait_ge(kc_ready, 1)
                if r == 4:
                    pe.wait_ge(rope_cosined, 1)
                    pe.wait_ge(k_out_ready, 1)
                for k in range(KC):
                    mm = both_halves(bank, m, k, xhi, xlo, k, k == 0, k == KC - 1)
                mm.then_inc(w_used, 1)
                if r == 3:
                    pe.wait_ge(va_ready, NT)
                    gate(0)
                    gate(1)
            gate(2)
            gate(3)

            def scores(c):
                bank = 2 + 2 * (c % 2)
                if c == 0:
                    pe.wait_ge(rope_done, 5)
                    pe.wait_ge(gate_biased, 2)
                if c == 1:
                    pe.wait_ge(gate_biased, 3)
                if c >= 2:
                    pe.wait_ge(shifted, NKV * (c - 1))
                if c == NCH:
                    pe.wait_ge(k_s_ready, 1)
                    pe.wait_ge(kc_ready, 1)
                    for g in range(NKV):
                        r = slice(g * HD, (g + 1) * HD)
                        mm = pe.matmul(flat(bank + g, 0, P), q_r[r, 4 * SEQ:4 * TOK], k_s[r, :], start=True, stop=True)
                else:
                    for g in range(NKV):
                        r = slice(g * HD, (g + 1) * HD)
                        for j in range(2):
                            col = j * P
                            lhs = q_r[r, 4 * CHUNK * c + j * P:4 * CHUNK * c + (j + 1) * P]
                            if c % 2:
                                mm = pe.matmul(flat(bank + g, col, P), lhs, k_r[r, (c - 1) * CHUNK:(c + 1) * CHUNK],
                                               start=True, stop=True)
                                continue
                            mm = pe.matmul(flat(bank + g, col, CHUNK), lhs, k_r[r, c * CHUNK:(c + 1) * CHUNK],
                                           start=True, stop=True)
                            if c:
                                mm = pe.matmul(flat(bank + g, col + CHUNK, CHUNK), lhs, k_r[r, (c - 1) * CHUNK:c * CHUNK],
                                               start=True, stop=True)
                mm.then_inc(scored, 1)

            def turn_probs(c):
                if c == 0:
                    pe.wait_ge(rope_cosined, 5)
                else:
                    pe.wait_ge(p_t_ready, c)
                pe.wait_ge(p_ready, c + 1)
                w = CHUNK if c == 0 else P
                for j in range(2 if c == NCH else 4):
                    mm = pe.transpose(flat(6, j * P, P, w), s_sb[:, c % 2, j * P:j * P + w], ident[:, :])
                mm.then_inc(p_turned, 1)

            def weigh_values(c):
                pe.wait_ge(p_t_ready, c + 1)
                if c >= 1:
                    pe.wait_ge(att_lo, c)
                if c == 0:
                    pe.wait_ge(v_ready, 2)
                    pe.wait_ge(v_evacuated, 2)
                if c == NCH:
                    pe.wait_ge(vc_loaded, 16)
                    pe.wait_ge(set_gaps, 1)
                w = CHUNK if c == 0 else P
                for g in range(NKV):
                    cols = slice(g * HD, (g + 1) * HD)
                    v = v_s[:, cols] if c == NCH else v_t[:, c // 2, cols] if c % 2 else v_even[0:w, c // 2, cols]
                    n = P if c == NCH else 2 * P
                    mm = pe.matmul(ps[g * HD:(g + 1) * HD, 7 * 512:7 * 512 + n], v, p_t[0:w, g * n:(g + 1) * n],
                                   start=True, stop=True)
                mm.then_inc(pv_done, 1)

            def u_step(n):
                t, k = divmod(n, KC)
                m = U_IN + 10 + t
                if k == 0:
                    pe.wait_ge(w_lo, m + 1)
                    if t == 0:
                        pe.wait_ge(gate_biased, 4)
                    else:
                        pe.wait_ge(u_evacuated, t)
                mm = both_halves(0, m, k, xhi, xlo, k, k == 0, k == KC - 1)
                if k == KC - 1:
                    mm.then_inc(w_used, 1)

            for i in range(NCH + 3):
                if i <= NCH:
                    scores(i)
                if i == NCH + 2:
                    weigh_values(NCH)
                for n in range(sum(U_STEPS[:i]), sum(U_STEPS[:i + 1])):
                    u_step(n)
                if 1 <= i <= NCH + 1:
                    turn_probs(i - 1)
                if 2 <= i < NCH + 2:
                    weigh_values(i - 2)

            def out_rows(e, ks, first, last):
                d, b = OUT_STEPS[e]
                if b is None:
                    for k in ks:
                        mm = both_halves(OUT_BANKS[e % 3], U_OUT + d, k, yhi, ylo, k, k == first, k == last)
                else:
                    for k in ks:
                        mm = one_half(OUT_BANKS[e % 3], b, U_OUT + d, k, yhi, ylo, k, k == first, k == last)
                return mm

            for e, (d, b) in enumerate(OUT_STEPS):
                if e == 0:
                    for early in range(2):
                        pe.wait_ge(w_lo, U_OUT + early + 1)
                        if early == 0:
                            pe.wait_ge(att_lo, NCH + 1)
                        out_rows(early, range(4, KC), 4, None)
                    for k in range(4):
                        pe.wait_ge(ya_lo, k + 1)
                        mm = out_rows(0, range(k, k + 1), None, 3)
                elif e == 1:
                    mm = out_rows(1, range(4), None, 3)
                else:
                    pe.wait_ge(w_lo, U_OUT + d + 1)
                    if e >= 3:
                        pe.wait_ge(z_evacuated, e - 2)
                    mm = out_rows(e, range(KC), 0, KC - 1)
                mm.then_inc(out_half_done if b == 0 else w_used, 1)
                if e == 8:
                    pe.wait_ge(acc_added, 8)
                    sum_squares_half(1, 0)
                if e == 9:
                    spread_half(1, 0)

            def ffn_layer(layer, n_post):
                base = U_FI[layer]
                for b in range(2):
                    for k in range(KC):
                        pe.wait_ge(x_lo, X_FFN[layer] + KC * b + k + 1)
                        for j in range(3):
                            if b == 0 and k == 0:
                                pe.wait_ge(w_lo, base + j + 1)
                            mm = one_half(2 * j, b, base + j, k, xhi, xlo, k, k == 0, k == KC - 1)
                            if b == 1 and k == KC - 1:
                                mm.then_inc(w_used, 1)
                        if b == 0 and k == SUM_AT[layer]:
                            pe.wait_ge(acc_added, Z_BEFORE[2 * layer + 1])
                            pe.wait_ge(r_ready, spreads(n_post - 1))
                            sum_squares_half(n_post, 1)
                        if b == 0 and k == SPREAD_AT[layer]:
                            spread_half(n_post, 1)
                pe.wait_ge(pre_added, H_BEFORE[2 * layer + 1])
                sum_squares(n_post + 1, acc_pre)
                spread(n_post + 1)
                pe.wait_ge(w_lo, base + 4)
                pe.wait_ge(r_ready, spreads(n_post + 1))
                for k in range(KC):
                    mm = both_halves(6, base + 3, k, xhi, xlo, k, k == 0, k == KC - 1)
                mm.then_inc(w_used, 1)
                with pe.Fori(1, FC // 2) as i:
                    for j in range(4):
                        pe.wait_ge(w_lo, i * 4 + (base + j + 1))
                        if j % 2 == 0:
                            pe.wait_ge(gu_scaled, i * 2 + (FC * layer + j // 2 - 1))
                        for k in range(KC):
                            mm = both_halves(2 * j, base + j, k, xhi, xlo, k, k == 0, k == KC - 1)
                        mm.then_inc(w_used, 1)
                pe.wait_ge(gu_scaled, FC * (layer + 1))
                base = U_FO[layer]
                z_before = Z_BEFORE[2 * layer + 1]
                with pe.Fori(0, KC // 2 - 1) as i:
                    for d in range(2):
                        pe.wait_ge(z_evacuated, i * 2 + (z_before + d - 1))
                        for j, (a, b) in enumerate(PIECES):
                            m = base + 4 * d + j
                            pe.wait_ge(w_lo, i * 8 + (m + 1))
                            pe.wait_ge(m_lo, FC * layer + b)
                            for c in range(a, b):
                                mm = both_halves(2 * d, m, c - a, mhi, mlo, c, c == 0, c == FC - 1)
                            mm.then_inc(w_used, 1)
                pe.wait_ge(z_evacuated, z_before + KC - 3)
                for j, (a, b) in enumerate(PIECES):
                    m = base + 4 * (KC - 2) + j
                    pe.wait_ge(w_lo, m + 1)
                    for c in range(a, b):
                        mm = both_halves(0, m, c - a, mhi, mlo, c, c == 0, c == FC - 1)
                    mm.then_inc(w_used, 1)
                pe.wait_ge(z_evacuated, z_before + KC - 2)
                for half in range(2):
                    for j, (a, b) in enumerate(PIECES):
                        m = base + 4 * (KC - 1) + j
                        if half == 0:
                            pe.wait_ge(w_lo, m + 1)
                        for c in range(a, b):
                            mm = one_half(2, half, m, c - a, mhi, mlo, c, c == 0, c == FC - 1)
                        if half == 1:
                            mm.then_inc(w_used, 1)
                        elif j == 3:
                            mm.then_inc(ffn_half_done, 1)
                        if half == 1 and j == 0:
                            pe.wait_ge(acc_added, z_before + KC)
                            sum_squares_half(n_post + 2, 0)
                        if half == 1 and j == 2:
                            spread_half(n_post + 2, 0)
                pe.wait_ge(acc_added, z_before + KC + 1)
                pe.wait_ge(r_ready, spreads(n_post + 2))
                sum_squares_half(n_post + 3, 1)

            ffn_layer(0, 2)

            for b in range(2):
                for k in range(KC):
                    n = KC * b + k
                    pe.wait_ge(h_added, H_BEFORE[1] + n + 1)
                    if n == 0:
                        pe.wait_ge(diag_ready, 1)
                    if k >= 3:
                        pe.wait_ge(h_tok_ready, n - 2)
                    for t in ((0, 1), (2, 3, 4))[b]:
                        c, w = POOL_TILES[t]
                        mm = pe.matmul(flat(2 * (k % 3) + b, (t - 2 * b) * P, P, w), h[:, k, c:c + w], gain_diag[:, k, :],
                                       start=True, stop=True)
                    mm.then_inc(h_turned, 1)
                    if b == 0 and k == 3:
                        spread_half(5, 1)
            pe.wait_ge(pre_added, H_BEFORE[2])
            sum_squares(6, acc_pre)

            def pool_chunk(n):
                g = n // 2
                bank = 2 * (n % 2)
                cols = slice(n * P, (n + 1) * P)
                if n == 0:
                    pe.wait_ge(h_tok_ready, 2 * KC)
                    pe.wait_ge(hist_loaded, 16)
                    pe.wait_ge(band_loaded, 64)
                    pe.wait_ge(band_dve, 1)
                    pe.wait_ge(band_act, 1)
                if n >= 2:
                    pe.wait_ge(x_lo, X_POOL + n - 1)
                for t, (a, b) in enumerate(POOL_OUT):
                    w = P if t < NT - 1 else TAIL + HIST
                    mm = pe.matmul(flat(bank, POOL_AT + a, b - a), h_tok[0:w, t, cols], band_r[t][0:w, g, :],
                                   start=True, stop=True)
                mm.then_inc(pooled, 1)

            def pool_product(e, b):
                g, o = divmod(e, 2)
                m = U_C + g // 2
                s = m % NSPLIT
                if b == 0 and o == 0:
                    pe.wait_ge(w_lo, m + 1)
                    pe.wait_ge(x_lo, X_POOL + 2 * (g + 1))
                ring = POOL_BANKS[b]
                if e >= len(ring):
                    pe.wait_ge(z_evacuated, Z_BEFORE[2] + KC * b + e - len(ring) + 1)
                for k in range(2):
                    w = slice(((g % 2 * 2 + k) * 2 + o) * P, ((g % 2 * 2 + k) * 2 + o + 1) * P)
                    mm = product(flat(ring[e % len(ring)], 0, HALF), whi[:, s, w], wlo[:, s, w],
                                 xhi[:, 2 * g + k, frames(b)], xlo[:, 2 * g + k, frames(b)], k == 0, k == 1)
                if b and e % 4 == 3:
                    mm.then_inc(w_used, 1)
                else:
                    mm.then_inc(pool_done, 1)

            for j in range(len(POOLS) + 1):
                for o in range(2):
                    if j < len(POOLS):
                        pool_chunk(2 * j + o)
                for o in range(2):
                    if j:
                        pool_product(2 * (j - 1) + o, 0)
            for e in range(KC):
                pool_product(e, 1)
                if e == 2:
                    pe.wait_ge(acc_added, Z_BEFORE[2] + KC)
                    sum_squares_half(7, 0)
                if e == 5:
                    spread_half(7, 0)
            ffn_layer(1, 8)

            for b in range(2):
                for k in range(KC):
                    n = KC * b + k
                    pe.wait_ge(h_added, H_BEFORE[3] + n + 1)
                    if b == 1 and k == 0:
                        pe.wait_ge(y_ready_act, 1)
                    for t in ((0, 1), (2, 3, 4))[b]:
                        t0, w = TILES[t]
                        mm = pe.transpose(flat(2 * (t % 4), k * P, P, w), h[:, k, t0:t0 + w], ident[:, :])
                        if b == 1 and k == KC - 1:
                            mm.then_inc(y_turned, 1)
                    if k == 3 or (b == 0 and k == KC - 1):
                        mm.then_inc(y_turned, 1)
                    if b == 0 and k == 3:
                        spread_half(11, 1)

        @block.scalar
        def _(act):
            def hi_part(m, i=0, step=0):
                if step:
                    act.wait_ge(w_loaded[m % NRAW], i * (16 * step // NRAW) + loaded(m))
                    act.wait_ge(w_used, i * step + (m - NSPLIT + 1))
                else:
                    act.wait_ge(w_loaded[m % NRAW], loaded(m))
                    if m >= NSPLIT:
                        act.wait_ge(w_used, m - NSPLIT + 1)
                n = unit_columns(m)
                act.activation(whi[:, m % NSPLIT, 0:n], raw[:, m % NRAW, 0:n], ACT.Copy).then_inc(w_hi, 1)

            def root_half(n, b):
                act.wait_ge(sum_ready, n)
                c = slice(3 * b, 3 * b + 3)
                act.activation(rms[:, c], flat(6, 3 * b, 3), ACT.Sqrt, scale=1.0 / D, bias=eps[:, :]).then_inc(rms_ready, 1)

            def keep_spread_half(n, b):
                act.wait_ge(rstd_spread, spreads(n))
                act.activation(r_post[:, frames(b)], flat(6, P, HALF), ACT.Copy).then_inc(r_ready, 1)

            def root(n):
                if n == 0:
                    act.wait_ge(x_squared, NT)
                    src = ssq[:, :]
                else:
                    act.wait_ge(sum_ready, n)
                    src = flat(6, 0, NT)
                if n == 6:
                    act.activation(rms[0:TAIL, NT - 1:NT], flat(6, NT - 1, 1, TAIL), ACT.Sqrt, scale=1.0 / D,
                                   bias=eps[0:TAIL, :])
                    act.activation(rms[:, 0:NT - 1], flat(6, 0, NT - 1), ACT.Sqrt, scale=1.0 / D, bias=eps[:, :])\
                        .then_inc(rms_ready, 1)
                    return
                act.activation(rms[:, 0:NT], src, ACT.Sqrt, scale=1.0 / D, bias=eps[:, :]).then_inc(rms_ready, 1)

            def keep_spread(n, dst):
                act.wait_ge(rstd_spread, spreads(n))
                act.activation(dst[:, :], flat(6, P, TOK), ACT.Copy).then_inc(r_ready, 1)

            def warm(func):
                act.activation(warmed[:, :], eps[:, :], func)

            act.dma_start(ident[:, :], constants[:, 0:P]).then_inc(ident_loaded, 16)
            act.dma_start(gain_rows[0:64, :], norm_g.rearrange("l j (k p) -> (l j k) p", p=P)).then_inc(gains_loaded, 16)
            act.dma_start(gain_rows[64:72, :], c_scale[0].rearrange("(k p) -> k p", p=P)).then_inc(gains_loaded, 16)
            act.dma_start(ws[:, :, :], a_ws[0].rearrange("h i j -> i h j")).then_inc(ws_loaded, 16)
            act.dma_start(k_cache[:, :], cache_k[0, 0, WIN - CHUNK:WIN].rearrange("t g d -> t (g d)")).then_inc(kc_loaded, 16)
            act.dma_start(v_s[CHUNK:P, :], cache_v[0, 0, WIN - CHUNK:WIN].rearrange("t g d -> t (g d)")).then_inc(vc_loaded, 16)
            act.dma_start(cossin[:, :, :], constants[:, P:P + 2 * TOK].rearrange("p (a n) -> p a n", a=2)).then_inc(rope_loaded, 16)
            act.dma_start(ln_gb[:, 0, :], ln_g[0].partition_broadcast(P)).then_inc(ln_loaded, 16)
            act.dma_start(ln_gb[:, 1, :], ln_b[0].partition_broadcast(P)).then_inc(ln_loaded, 16)
            act.dma_start(bs_b[:, :, :].rearrange("p h i -> p (h i)"),
                          a_bs[0].rearrange("h i -> (h i)").partition_broadcast(P)).then_inc(bs_loaded, 16)
            act.dma_start(sinks[:, :], b_sinks[0].partition_broadcast(P)).then_inc(sinks_loaded, 16)

            act.wait_ge(set_up, 1)
            act.wait_ge(gains_turned, 1)
            act.activation(gains[:, :], flat(7, 0, 72), ACT.Copy).then_inc(gains_ready, 1)
            act.wait_ge(gains_ready, 1)
            for k in range(KC):
                odd = 2 * k + 1
                if odd < KC:
                    act.wait_ge(x_turned, odd + 1)
                    act.activation(h[:, odd, :], flat(2 * (odd % 4), 0, TOK), ACT.Copy).then_inc(h_first_odd, 1)
                h_first_wait(act, k)
                act.activation(xhi[:, k, :], h[:, k, :], ACT.Copy, scale=gain(0, 0, k)).then_inc(x_hi, 1)
                if k in (0, 4):
                    hi_part(k // 4)
            for t, (t0, n) in enumerate(TILES):
                act.wait_ge(x_loaded[t], 16)
                if t:
                    act.wait_ge(x_squared, t)
                act.activation(u_raw[0:n, 0:2, 0:512], x_tok[0:n, t, :].rearrange("p (a b) -> p a b", a=2), ACT.Square,
                               accum_out=ssq[0:n, t:t + 1]).then_inc(x_squared, 1)
                if t in (0, 3):
                    hi_part(2 + t // 3)
            root(0)
            hi_part(4)
            act.wait_ge(rstd_ready, 1)
            hi_part(5)
            hi_part(6)
            act.wait_ge(w_used, 4)
            for t, (t0, n) in enumerate(TILES):
                act.activation(va[0:n, t, :], flat(t, 0, AW, n), ACT.Gelu_apprx_tanh, scale=rstd[0:n, t:t + 1])\
                    .then_inc(va_gelu, 1)
            keep_spread(0, r_pre)
            act.wait_ge(w_used, 5)
            for b, bank in enumerate((5, 0)):
                act.activation(gated[:, AH - 1, frames(b)], flat(bank, 0, HALF), ACT.Copy).then_inc(v_copied, 1)
            act.wait_ge(va_bn, NT)
            act.activation(ln_rms[:, :], mean_var[:, :, 1], ACT.Sqrt, bias=eps[:, :]).then_inc(ln_rms_ready, 1)
            hi_part(7)
            act.wait_ge(v_evacuated, 1)
            act.activation(v_even[0:CHUNK, :, :], v_t[0:CHUNK, :, :], ACT.Copy).then_inc(v_ready, 1)
            act.activation(v_even[CHUNK:P, 1:4, :], v_t[CHUNK:P, 0:3, :], ACT.Copy).then_inc(v_ready, 1)
            for m in range(8, 14):
                hi_part(m)
                if m == 11:
                    act.wait_ge(k_turned, 1)
                    act.activation(k_out[:, 0, :], flat(6, 0, P), ACT.Copy)
                    act.activation(k_out[0:DEC, 1, :], flat(6, P, P, DEC), ACT.Copy).then_inc(k_out_ready, 1)

            def exps(c):
                w = CHUNK if c == 0 else P
                n = 2 if c == NCH else 4
                s = s_sb[:, c % 2, 0:n * P].rearrange("p (c s) -> p c s", c=n)[:, :, 0:w]
                act.wait_ge(sink_shifted, c + 1)
                act.activation(den[:, c % 2, 0:n], sunk[:, c % 2, 0:n], ACT.Exp)
                act.activation(s, s, ACT.Exp).then_inc(exp_done, 1)

            def keep_turned(c):
                act.wait_ge(p_turned, c + 1)
                if c >= 1:
                    act.wait_ge(pv_done, c)
                w = CHUNK if c == 0 else P
                n = (2 if c == NCH else 4) * P
                act.activation(p_t[0:w, 0:n], flat(6, 0, n, w), ACT.Copy).then_inc(p_t_ready, 1)

            def attended(c):
                n = DEC if c == NCH else CHUNK
                return slice(c * CHUNK, c * CHUNK + n), flat(7, 0, 4 * n).rearrange("p (t q) -> p t q", t=4)

            def attended_hi(c):
                act.wait_ge(pv_done, c + 1)
                cols, src = attended(c)
                act.activation(yhi[:, 4:8, cols], src, ACT.Copy).then_inc(att_hi, 1)

            for i in range(NCH + 3):
                if i <= NCH:
                    exps(i)
                if 1 <= i <= NCH + 1:
                    keep_turned(i - 1)
                if i >= 2:
                    attended_hi(i - 2)
                if i in U_THROUGH:
                    hi_part(14 + U_THROUGH.index(i))
            for t in range(3):
                act.wait_ge(u_evacuated, t + 1)
                act.activation(u_raw[:, t, :], u_raw[:, t, :], ACT.Gelu_apprx_tanh).then_inc(u_gelu, 1)
            act.wait_ge(u_evacuated, 4)
            act.activation(u_raw[:, 3, :], u_raw[:, 3, :], ACT.Gelu_apprx_tanh).then_inc(u_gelu, 1)
            hi_part(17)
            for t in range(AH):
                if t < 3:
                    act.wait_ge(ya_ready, t + 1)
                else:
                    act.wait_ge(ya_last, 1)
                act.activation(yhi[:, t, :], gated[:, t, :], ACT.Copy).then_inc(ya_hi, 1)

            def evacuate_z(e, out, squares, src, scale=1.0):
                act.activation(out, src, ACT.Copy, scale=scale)
                if e >= 2:
                    act.wait_ge(acc_added, e - 1)
                act.activation(squares, src, ACT.Square, scale=scale).then_inc(z_evacuated, 1)

            def evacuate_out(e):
                d, b = OUT_STEPS[e]
                bank = OUT_BANKS[e % 3]
                if b == 0:
                    act.wait_ge(out_half_done, e - 3)
                else:
                    act.wait_ge(w_used, U_OUT + d + 1)
                if b is None:
                    evacuate_z(e, halves(z[:, d, :]), halves(tmp2[:, e % 2, :]), pair(bank))
                else:
                    evacuate_z(e, z[:, d, frames(b)], tmp2[:, e % 2, frames(b)], flat(bank + b, 0, HALF))

            def residual_half(s, b, split, between, follow=None):
                for k in range(KC):
                    n = H_BEFORE[s] + KC * b + k
                    act.wait_ge(h_added, n + 1)
                    if split:
                        act.activation(xhi[:, k, frames(b)], h[:, k, frames(b)], ACT.Copy, scale=split(k)).then_inc(x_hi, 1)
                    if k == 0:
                        act.activation(acc_pre[:, frames(b)], h[:, k, frames(b)], ACT.Square).then_inc(h_squared, 1)
                    else:
                        if k >= 3:
                            act.wait_ge(pre_added, n - 1)
                        act.activation(tmp2[:, k % 2, frames(b)], h[:, k, frames(b)], ACT.Square).then_inc(h_squared, 1)
                    if follow and k:
                        follow(b, k - 1)
                    if k in between:
                        between[k]()
                if follow:
                    follow(b, KC - 1)

            def after_mixer_ab():
                def step(e):
                    evacuate_out(e)
                    hi_part(U_OUT + e)

                for e in range(8):
                    evacuate_out(e)
                    if e < 4:
                        hi_part(U_OUT + 4 + e)
                warm(ACT.Sqrt)
                step(8)
                root_half(1, 0)
                step(9)
                keep_spread_half(1, 0)
                split = lambda k: gain(0, 2, k)
                residual_half(0, 0, split, {0: lambda: step(10), 2: lambda: evacuate_out(11), 4: lambda: root_half(2, 1)})
                keep_spread_half(2, 1)
                residual_half(0, 1, split, {5: lambda: hi_part(U_FI[0] + 3)})

            after_mixer_ab()

            def ffn_layer(layer, n_post):
                root(n_post + 1)
                keep_spread(n_post + 1, r_pre)
                warm(ACT.Silu)
                act.wait_ge(out_stored, 16 * MIXER_STORES[layer])
                base = U_FI[layer]

                def tiles_pair(i, following, i2, step2):
                    for f in range(2):
                        act.wait_ge(gu_scaled, i * 2 + (FC * layer + f + 1))
                        act.activation(tmp2[:, 0, :], tmp[:, 0, :], ACT.Silu).then_inc(silu_done, 1)
                        hi_part(following + 2 * f, i2, step2)
                        act.wait_ge(m_ready, i * 2 + (FC * layer + f + 1))
                        act.activation(mhi[:, bass.ds(i * 2 + f, 1), :].rearrange("p o n -> p (o n)"), tmp2[:, 1, :],
                                       ACT.Copy).then_inc(m_hi, 1)
                        hi_part(following + 2 * f + 1, i2, step2)

                with act.Fori(0, FC // 2 - 1) as i:
                    tiles_pair(i, base + 4, i, 4)
                tiles_pair(FC // 2 - 1, U_FO[layer], 0, 0)
                base = U_FO[layer]
                s = 2 * layer + 1

                def evacuate_z_loop(s, d, i, bank, used):
                    act.wait_ge(w_used, i * 8 + used)
                    act.activation(halves(z[:, bass.ds(i * 2 + d, 1), :].rearrange("p o n -> p (o n)")), pair(bank), ACT.Copy)
                    act.wait_ge(acc_added, i * 2 + (Z_BEFORE[s] + d - 1))
                    act.activation(halves(tmp2[:, d, :]), pair(bank), ACT.Square).then_inc(z_evacuated, 1)

                with act.Fori(0, KC // 2 - 1) as i:
                    for d in range(2):
                        for j in range(4):
                            hi_part(base + 4 * d + j + 4, i, 8)
                        evacuate_z_loop(s, d, i, 2 * d, base + 4 * d + 4)
                for j in range(4):
                    hi_part(base + 4 * (KC - 1) + j)
                act.wait_ge(w_used, base + 4 * (KC - 1))
                evacuate_z(Z_BEFORE[s] + KC - 2, halves(z[:, KC - 2, :]), halves(tmp2[:, 0, :]), pair(0))

            def evacuate_last(s, b):
                if b == 0:
                    act.wait_ge(ffn_half_done, s // 2 + 1)
                else:
                    act.wait_ge(w_used, U_FO[s // 2] + 4 * KC)
                evacuate_z(Z_BEFORE[s] + KC - 1 + b, z[:, KC - 1, frames(b)], tmp2[:, 1, frames(b)], flat(2 + b, 0, HALF))

            ffn_layer(0, 2)

            def keep_turned_h(b, k):
                act.wait_ge(h_turned, KC * b + k + 1)
                c = slice(k * P, (k + 1) * P)
                bank = 2 * (k % 3) + b
                if b:
                    act.activation(h_tok[0:TAIL, NT - 1, c], flat(bank, 2 * P, P, TAIL), ACT.Copy)
                act.activation(h_tok[:, 2 * b:2 * b + 2, c], flat(bank, 0, 2 * P).rearrange("p (t n) -> p t n", n=P),
                               ACT.Copy).then_inc(h_tok_ready, 1)

            evacuate_last(1, 0)
            warm(ACT.Sqrt)
            hi_part(U_C)
            root_half(4, 0)
            hi_part(U_C + 1)
            keep_spread_half(4, 0)

            def last_and_diagonals():
                evacuate_last(1, 1)
                for k in range(KC):
                    op = act.activation(gain_diag[:, k, :], ident[:, :], ACT.Copy, scale=gain(1, 0, k))
                op.then_inc(diag_ready, 1)

            residual_half(1, 0, None, {0: last_and_diagonals, 3: lambda: root_half(5, 1),
                                       5: lambda: keep_spread_half(5, 1)}, keep_turned_h)
            residual_half(1, 1, None, {}, keep_turned_h)
            root(6)
            act.wait_ge(band_loaded, 64)
            act.wait_ge(rstd_ready, 7)
            for t in (2, 3):
                op = act.activation(band_r[t][:, :, :], band_later[:, :, :], ACT.Copy, scale=rstd[:, t:t + 1])
            op.then_inc(band_act, 1)

            def pool_evacuate(e, b):
                if b and e % 4 == 3:
                    act.wait_ge(w_used, U_C + e // 4 + 1)
                else:
                    act.wait_ge(pool_done, KC + e - e // 4 + 1 if b else e + 1)
                if b:
                    act.wait_ge(acc_added, Z_BEFORE[2] + KC + e - 1)
                    act.activation(tmp2[:, e % 2, frames(1)], flat(POOL_BANKS[1][e % 4], 0, HALF), ACT.Square,
                                   scale=scale_c(e)).then_inc(z_squared, 1)
                    return
                evacuate_z(Z_BEFORE[2] + KC * b + e, z_pool[:, e, frames(b)], tmp2[:, e % 2, frames(b)],
                           flat(POOL_BANKS[b][e % len(POOL_BANKS[b])], 0, HALF), scale_c(e))

            for j in range(len(POOLS) + 1):
                for o in range(2):
                    if j < len(POOLS):
                        n = 2 * j + o
                        act.wait_ge(pooled, n + 1)
                        act.activation(xhi[:, n, :], flat(2 * o, POOL_AT, TOK), ACT.Copy).then_inc(x_hi, 1)
                for o in range(2):
                    if j:
                        pool_evacuate(2 * (j - 1) + o, 0)
                if j in (1, 2):
                    hi_part(U_FI[1] + j - 1)
            for e in range(KC):
                pool_evacuate(e, 1)
                if e == 3:
                    root_half(7, 0)
                if e == 4:
                    hi_part(U_FI[1] + 2)
                if e == 6:
                    keep_spread_half(7, 0)
            split_1 = lambda k: gain(1, 2, k)
            residual_half(2, 0, split_1, {4: lambda: root_half(8, 1)})
            keep_spread_half(8, 1)
            residual_half(2, 1, split_1, {5: lambda: hi_part(U_FI[1] + 3)})
            ffn_layer(1, 8)
            evacuate_last(3, 0)
            warm(ACT.Sqrt)
            root_half(10, 0)
            keep_spread_half(10, 0)
            evacuate_last(3, 1)
            root_half(11, 1)

            def keep_y(t, upper):
                n = TILES[t][1]
                op = act.activation(y_tok[0:n, t, 512 * upper:512 * (upper + 1)], flat(2 * (t % 4) + upper, 0, 512, n), ACT.Copy)
                if upper:
                    op.then_inc(y_ready_act, 1)

            act.wait_ge(y_turned, 1)
            keep_y(0, 0)
            keep_y(1, 0)
            keep_spread_half(11, 1)
            act.wait_ge(y_turned, 2)
            keep_y(0, 1)
            keep_y(1, 1)
            act.wait_ge(y_turned, 3)
            for t in (2, 3, 4):
                keep_y(t, 0)
            act.wait_ge(y_turned, 4)
            keep_y(2, 1)
            act.wait_ge(y_turned, 6)
            keep_y(4, 1)

        @block.vector
        def _(dve):
            def lo_part(m, i=0, step=0):
                dve.wait_ge(w_hi, i * step + (m + 1) if step else m + 1)
                s, n = m % NSPLIT, unit_columns(m)
                dve.tensor_tensor(wlo[:, s, 0:n], raw[:, m % NRAW, 0:n], whi[:, s, 0:n].bitcast(F32), ALU.subtract)\
                    .then_inc(w_lo, 1)

            def invert(n):
                dve.wait_ge(rms_ready, n + 1)
                if n == 6:
                    dve.reciprocal(rstd[0:TAIL, NT - 1:NT], rms[0:TAIL, NT - 1:NT])
                    dve.reciprocal(rstd[:, 0:NT - 1], rms[:, 0:NT - 1]).then_inc(rstd_ready, 1)
                    return
                dve.reciprocal(rstd[:, 0:NT], rms[:, 0:NT]).then_inc(rstd_ready, 1)

            def invert_half(n, b):
                dve.wait_ge(rms_ready, n + 1)
                if n == 7:
                    dve.wait_ge(pool_out_ready, 1)
                c = slice(3 * b, 3 * b + 3)
                dve.reciprocal(rstd[:, c], rms[:, c]).then_inc(rstd_ready, 1)

            dve.memset(wm_t[CHUNK:P, :, 0:CHUNK], 0.0)
            dve.memset(v_s[DEC:CHUNK, :], 0.0).then_inc(set_gaps, 1)
            for k in range(KC):
                if 2 * k < KC:
                    dve.wait_ge(x_turned, 2 * k + 1)
                    dve.tensor_copy(h[:, 2 * k, :], flat(2 * (2 * k % 4), 0, TOK)).then_inc(h_first_even, 1)
                h_first_wait(dve, k)
                dve.wait_ge(x_hi, k + 1)
                dve.scalar_tensor_tensor(xlo[:, k, :], h[:, k, :], gain(0, 0, k),
                                         xhi[:, k, :].bitcast(F32), ALU.mult, ALU.subtract).then_inc(x_lo, 1)
                if k in (0, 4):
                    lo_part(k // 4)
            lo_part(2)
            lo_part(3)
            invert(0)

            lo_part(4)
            dve.wait_ge(sinks_loaded, 16)
            dve.tensor_copy(sink_p[0:CHUNK, :], sinks[0:CHUNK, 0:NQ:2])
            dve.tensor_copy(sink_p[CHUNK:P, :], sinks[CHUNK:P, 1:NQ:2])
            for a in range(4):
                op = dve.tensor_copy(sink_s[a * DEC:(a + 1) * DEC, :], sinks[a * DEC:(a + 1) * DEC, a:NQ:4])
            op.then_inc(sinks_ready, 1)
            lo_part(5)
            lo_part(6)
            for t, (t0, n) in enumerate(TILES):
                dve.wait_ge(va_gelu, t + 1)
                dve.bn_stats(stats[0:n, t, :], va[0:n, t, :]).then_inc(va_stats, 1)
            dve.wait_ge(set_stats, 1)
            for t, (t0, n) in enumerate(TILES):
                dve.wait_ge(va_stats, t + 1)
                dve.bn_aggr(mean_var[0:n, t, :], stats[0:n, t, :]).then_inc(va_bn, 1)
            dve.wait_ge(ln_rms_ready, 1)
            dve.reciprocal(ln_rstd[:, :], ln_rms[:, :]).then_inc(ln_rstd_ready, 1)
            dve.wait_ge(ln_rstd_ready, 1)
            for t, (t0, n) in enumerate(TILES):
                dve.tensor_scalar(va[0:n, t, :], va[0:n, t, :], mean_var[0:n, t, 0:1], ln_rstd[0:n, t:t + 1],
                                  ALU.subtract, ALU.mult).then_inc(va_normed, 1)
            lo_part(7)

            half = ROPE // 2
            swap = [*range(half, ROPE), *range(half), *range(ROPE, 32)]

            def rope_parts(r):
                dve.wait_ge(w_used, U_IN + 6 + r)
                if r >= 2:
                    dve.wait_ge(rope_done, r - 1)
                elif r == 0:
                    dve.wait_ge(x_lo, KC)
                src = pair((6, 0, 2, 4, 6)[r])
                dve.stream_shuffle(halves(tmp[:, r % 2, :]), src, swap).then_inc(rope_swapped, 1)
                dve.tensor_tensor(halves(tmp2[:, r % 2, :]), src, halves(cossin[:, 0, :]), ALU.mult).then_inc(rope_cosined, 1)
                dve.wait_ge(rope_swapped, r + 1)
                dve.tensor_tensor(tmp[:, r % 2, :], tmp[:, r % 2, :], cossin[:, 1, :], ALU.mult).then_inc(rope_sined, 1)

            def rope_sum(r):
                dve.wait_ge(rope_sined, r + 1)
                dve.wait_ge(rope_cosined, r + 1)
                a, b = tmp[:, r % 2, :], tmp2[:, r % 2, :]
                if r == 0:
                    dve.tensor_tensor(k_r[:, :], a, b, ALU.add).then_inc(rope_done, 1)
                    return
                t = r - 1
                by_chunk = lambda ap: ap[:, 0:SEQ].rearrange("p (c q) -> p c q", c=NCH)
                dst = q_r[:, 0:4 * SEQ].rearrange("p (c t q) -> p c t q", c=NCH, t=4)[:, :, t, :]
                dve.tensor_tensor(dst, by_chunk(a), by_chunk(b), ALU.add)
                dve.tensor_tensor(q_r[:, 4 * SEQ + t * DEC:4 * SEQ + (t + 1) * DEC], a[:, SEQ:TOK], b[:, SEQ:TOK],
                                  ALU.add).then_inc(rope_done, 1)

            dve.wait_ge(rope_loaded, 16)
            dve.wait_ge(r_ready, 1)
            for a in range(2):
                dve.tensor_tensor(cossin[:, a, :], cossin[:, a, :], r_pre[:, :], ALU.mult).then_inc(rope_scaled, 1)
            dve.wait_ge(v_turned, 1)
            dve.tensor_tensor(v_t[:, :, :], flat(5, 0, 512).rearrange("p (j n) -> p j n", j=4),
                              rstd[:, 0:4].unsqueeze(2).broadcast_to([P, 4, P]), ALU.mult).then_inc(v_evacuated, 1)
            dve.tensor_scalar(v_s[0:DEC, :], flat(4, 0, P, DEC), rstd[0:DEC, 4:5], None, ALU.mult).then_inc(v_evacuated, 1)
            dve.wait_ge(rope_scaled, 2)

            def rope_step(r):
                if r == 2:
                    dve.wait_ge(ws_turned, 1)
                    turned = flat(4, 0, 512).rearrange("p (h i) -> p h i", h=AH)
                    dve.tensor_copy(wm_t[0:CHUNK, :, :], turned[0:CHUNK])
                    dve.tensor_copy(wm_t[CHUNK:P, :, CHUNK:P], turned[CHUNK:P, :, CHUNK:P]).then_inc(wm_ready, 1)
                    dve.wait_ge(kc_turned, 1)
                    dve.tensor_copy(k_s[:, CHUNK:P], flat(5, 0, CHUNK)).then_inc(kc_ready, 1)
                rope_parts(r)
                lo_part(8 + r)
                rope_sum(r)

            def bias_gate(a):
                dve.wait_ge(gate_done, a + 1)
                bank = GATE_BANKS[a]
                dve.tensor_tensor(gated[:, a, 0:SEQ].rearrange("p (n i) -> p n i", i=P),
                                  flat(bank, 0, SEQ).rearrange("p (n i) -> p n i", i=P),
                                  bs_b[:, a:a + 1, :].broadcast_to([P, SEQ // P, P]), ALU.add)
                dve.tensor_tensor(gated[:, a, SEQ:TOK], flat(bank, SEQ, DEC), bs_b[:, a, 0:DEC], ALU.add)\
                    .then_inc(gate_biased, 1)

            for r in range(5):
                rope_step(r)
                if r == 3:
                    dve.wait_ge(bs_loaded, 16)
                    bias_gate(0)
                    bias_gate(1)
            bias_gate(2)
            bias_gate(3)
            lo_part(13)

            def shift(c):
                n, b = (2, c % 2) if c == NCH else (4, c % 2)
                w = CHUNK if c == 0 else P
                sink = sink_s[:, :] if c == NCH else sink_p[:, :]
                npg = n // NKV
                dst = s_sb[:, b, 0:n * P].rearrange("p (c s) -> p c s", c=n)[:, :, 0:w]
                srcs = [flat(2 + 2 * (c % 2) + g, 0, npg * P).rearrange("p (c s) -> p c s", c=npg)[:, :, 0:w]
                        for g in range(NKV)]
                scale = SCALE
                dve.wait_ge(scored, c + 1)
                if c >= 2:
                    dve.wait_ge(p_turned, c - 1)
                if c == NCH:
                    for g in range(NKV):
                        dve.scalar_tensor_tensor(dst[:, g, :], srcs[g][:, 0, :], SCALE, mask_s[:, :],
                                                 ALU.mult, ALU.add).then_inc(s_masked, 1)
                    dve.wait_ge(s_masked, NKV)
                    srcs, scale = [dst[:, g:g + 1, :] for g in range(NKV)], 1.0
                for g in range(NKV):
                    dve.tensor_reduce(top[:, b, g * npg:(g + 1) * npg], srcs[g], AX.X, ALU.max).then_inc(topped, 1)
                dve.wait_ge(topped, NKV * (c + 1))
                dve.scalar_tensor_tensor(peak[:, b, 0:n], top[:, b, 0:n], scale, sink, ALU.mult, ALU.max).then_inc(peaked, 1)
                dve.wait_ge(peaked, c + 1)
                for g in range(NKV):
                    part = slice(g * npg, (g + 1) * npg)
                    dve.scalar_tensor_tensor(dst[:, part, :], srcs[g], scale,
                                             peak[:, b, part].unsqueeze(2).broadcast_to([P, npg, w]),
                                             ALU.mult, ALU.subtract).then_inc(shifted, 1)
                dve.tensor_tensor(sunk[:, b, 0:n], sink, peak[:, b, 0:n], ALU.subtract).then_inc(sink_shifted, 1)

            def denominator(c):
                n, b = (2, c % 2) if c == NCH else (4, c % 2)
                w = CHUNK if c == 0 else P
                p = s_sb[:, b, 0:n * P].rearrange("p (c s) -> p c s", c=n)[:, :, 0:w]
                dve.wait_ge(exp_done, c + 1)
                dve.tensor_reduce(den2[:, b, 0:n], p, AX.X, ALU.add).then_inc(summed, 1)
                dve.wait_ge(summed, c + 1)
                dve.tensor_tensor(den2[:, b, 0:n], den2[:, b, 0:n], den[:, b, 0:n], ALU.add).then_inc(den_ready, 1)
                dve.wait_ge(den_ready, c + 1)
                dve.reciprocal(rden[:, b, 0:n], den2[:, b, 0:n]).then_inc(rden_ready, 1)

            def attended_lo(c):
                n = DEC if c == NCH else CHUNK
                cols, src = slice(c * CHUNK, c * CHUNK + n), flat(7, 0, 4 * n).rearrange("p (t q) -> p t q", t=4)
                dve.wait_ge(att_hi, c + 1)
                dve.tensor_tensor(ylo[:, 4:8, cols], src, yhi[:, 4:8, cols].bitcast(F32), ALU.subtract).then_inc(att_lo, 1)

            def evacuate_u(t):
                dve.wait_ge(w_used, U_IN + 11 + t)
                dve.tensor_tensor(halves(u_raw[:, t, :]), pair(0), halves(r_pre[:, :]), ALU.mult).then_inc(u_evacuated, 1)

            dve.wait_ge(sinks_ready, 1)
            dve.wait_ge(set_sample, 1)
            for i in range(NCH + 3):
                if i <= NCH:
                    shift(i)
                    denominator(i)
                if i in U_THROUGH:
                    evacuate_u(U_THROUGH.index(i))
                if i >= 2:
                    attended_lo(i - 2)
                if i in U_THROUGH:
                    lo_part(14 + U_THROUGH.index(i))
            evacuate_u(3)
            dve.wait_ge(u_gelu, AH)
            dve.tensor_tensor(gated[:, AH - 1, :], gated[:, AH - 1, :], u_raw[:, AH - 1, :], ALU.mult).then_inc(ya_last, 1)
            lo_part(17)
            for t in range(AH):
                dve.wait_ge(ya_hi, t + 1)
                dve.tensor_tensor(ylo[:, t, :], gated[:, t, :], yhi[:, t, :].bitcast(F32), ALU.subtract).then_inc(ya_lo, 1)

            def add_squares(s, n, slot, i=0, step=0, b=None):
                n += Z_BEFORE[s]
                if step:
                    dve.wait_ge(z_evacuated, i * step + (n + 1))
                    dve.wait_ge(acc_added, i * step + n)
                else:
                    dve.wait_ge(z_evacuated, n + 1)
                    if n:
                        dve.wait_ge(acc_added, n)
                c = slice(0, TOK) if b is None else frames(b)
                dve.tensor_tensor(acc_post[:, c], acc_post[:, c], tmp2[:, slot, c], ALU.add).then_inc(acc_added, 1)

            def residual_half(s, b, layer, source, between):
                c = frames(b)

                def scale(k):
                    n = H_BEFORE[s] + KC * b + k
                    if n >= 4:
                        dve.wait_ge(h_added, n - 3)
                    dve.tensor_tensor(quarter(k), source[:, k, c], r_post[:, c], ALU.mult).then_inc(half_scaled_dve, 1)

                def lo(k):
                    dve.wait_ge(x_hi, X_FFN[layer] + KC * b + k + 1)
                    dve.scalar_tensor_tensor(xlo[:, k, c], h[:, k, c], gain(layer, 2, k), xhi[:, k, c].bitcast(F32),
                                             ALU.mult, ALU.subtract).then_inc(x_lo, 1)

                scale(0)
                for k in range(KC):
                    if k < KC - 1 and (k % 2 or s not in SHARED):
                        scale(k + 1)
                    if s not in SHARED:
                        dve.wait_ge(half_scaled_dve, SCALED_DVE_BEFORE[s] + KC * b + k + 1)
                    elif k % 2:
                        dve.wait_ge(half_scaled_pool, SCALED_POOL_BEFORE[s] + KC // 2 * b + k // 2 + 1)
                    else:
                        dve.wait_ge(half_scaled_dve, SCALED_DVE_BEFORE[s] + KC // 2 * b + k // 2 + 1)
                    dve.scalar_tensor_tensor(h[:, k, c], quarter(k), gain(layer, 3 if s % 2 else 1, k), h[:, k, c],
                                             ALU.mult, ALU.add).then_inc(h_added, 1)
                    if k and s % 2 == 0:
                        lo(k - 1)
                    if k in between:
                        between[k]()
                if s % 2 == 0:
                    lo(KC - 1)

            def after_mixer_ab():
                def step(e):
                    add_squares(0, e, e % 2, b=1)
                    lo_part(U_OUT + e)

                dve.wait_ge(acc_zeroed, 1)
                for e in range(8):
                    if e < 4:
                        lo_part(U_OUT + 4 + e)
                    add_squares(0, e, e % 2, b=OUT_STEPS[e][1])
                step(8)
                invert_half(1, 0)
                step(9)
                dve.wait_ge(r_ready, spreads(1))
                residual_half(0, 0, 0, z, {0: lambda: step(10), 2: lambda: add_squares(0, 11, 1, b=1),
                                            4: lambda: invert_half(2, 1)})
                dve.wait_ge(r_ready, spreads(2))
                residual_half(0, 1, 0, z, {5: lambda: lo_part(U_FI[0] + 3)})

            after_mixer_ab()

            def ffn_layer(layer, n_post):
                invert(n_post + 1)
                dve.wait_ge(r_ready, spreads(n_post + 1))
                dve.wait_ge(out_stored, 16 * MIXER_STORES[layer])
                base = U_FI[layer]
                fb = FC * layer

                def tiles_pair(i, following, i2, step2):
                    for f in range(2):
                        at = (lambda v: i * 2 + (fb + f + v))
                        gate, up = pair(4 * f), pair(4 * f + 2)
                        r = halves(r_pre[:, :])
                        dve.wait_ge(w_used, i * 4 + (base + 2 * f + 2))
                        dve.wait_ge(w_lo, i * 4 + (base + 4 + 2 * f))
                        dve.tensor_tensor(halves(tmp[:, 0, :]), gate, r, ALU.mult)
                        dve.tensor_tensor(halves(tmp[:, 1, :]), up, r, ALU.mult).then_inc(gu_scaled, 1)
                        lo_part(following + 2 * f, i2, step2)
                        dve.wait_ge(silu_done, at(1))
                        dve.tensor_tensor(tmp2[:, 1, :], tmp2[:, 0, :], tmp[:, 1, :], ALU.mult).then_inc(m_ready, 1)
                        dve.wait_ge(m_hi, at(1))
                        c = bass.ds(i * 2 + f, 1)
                        dve.tensor_tensor(mlo[:, c, :].rearrange("p o n -> p (o n)"), tmp2[:, 1, :],
                                          mhi[:, c, :].rearrange("p o n -> p (o n)").bitcast(F32), ALU.subtract)\
                            .then_inc(m_lo, 1)
                        lo_part(following + 2 * f + 1, i2, step2)

                with dve.Fori(0, FC // 2 - 1) as i:
                    tiles_pair(i, base + 4, i, 4)
                tiles_pair(FC // 2 - 1, U_FO[layer], 0, 0)
                base = U_FO[layer]
                s = 2 * layer + 1
                dve.wait_ge(acc_zeroed, s + 1)
                with dve.Fori(0, KC // 2 - 1) as i:
                    for d in range(2):
                        for j in range(4):
                            lo_part(base + 4 * d + j + 4, i, 8)
                        add_squares(s, d, d, i, 2)
                for j in range(4):
                    lo_part(base + 4 * (KC - 1) + j)
                add_squares(s, KC - 2, 0)
                add_squares(s, KC - 1, 1, b=0)

            ffn_layer(0, 2)
            lo_part(U_C)
            invert_half(4, 0)
            lo_part(U_C + 1)
            dve.wait_ge(r_ready, spreads(4))
            residual_half(1, 0, 0, z, {0: lambda: add_squares(1, KC, 1, b=1), 3: lambda: invert_half(5, 1)})
            dve.wait_ge(r_ready, spreads(5))
            residual_half(1, 1, 0, z, {})

            invert(6)
            dve.wait_ge(band_loaded, 64)
            dve.wait_ge(rstd_ready, 7)
            dve.tensor_scalar(band_r[0][:, :, :], band_first[:, :, :], rstd[:, 0:1], None, ALU.mult)
            dve.tensor_scalar(band_r[NT - 1][0:TAIL, :, :], band_last[0:TAIL, :, :], rstd[0:TAIL, NT - 1:NT], None, ALU.mult)
            dve.tensor_scalar(band_r[1][:, :, :], band_later[:, :, :], rstd[:, 1:2], None, ALU.mult).then_inc(band_dve, 1)
            dve.wait_ge(acc_zeroed, 3)
            for j in range(len(POOLS) + 1):
                for o in range(2):
                    if j < len(POOLS):
                        c = 2 * j + o
                        dve.wait_ge(x_hi, X_POOL + 2 * j + o + 1)
                        dve.tensor_tensor(xlo[:, c, :], flat(2 * o, POOL_AT, TOK), xhi[:, c, :].bitcast(F32), ALU.subtract)\
                            .then_inc(x_lo, 1)
                for o in range(2):
                    if j:
                        add_squares(2, 2 * (j - 1) + o, o, b=0)
                if j in (1, 2):
                    lo_part(U_FI[1] + j - 1)
            for e in range(KC):
                dve.wait_ge(z_squared, e + 1)
                dve.tensor_scalar(z_pool[:, e, frames(1)], flat(POOL_BANKS[1][e % 4], 0, HALF), scale_c(e), None, ALU.mult)\
                    .then_inc(z_evacuated, 1)
                add_squares(2, KC + e, e % 2, b=1)
                if e == 3:
                    invert_half(7, 0)
            dve.wait_ge(r_ready, spreads(7))
            residual_half(2, 0, 1, z_pool, {4: lambda: invert_half(8, 1)})
            dve.wait_ge(r_ready, spreads(8))
            dve.wait_ge(w_lo, U_FI[1] + 3)
            residual_half(2, 1, 1, z_pool, {5: lambda: lo_part(U_FI[1] + 3)})
            ffn_layer(1, 8)
            invert_half(10, 0)
            dve.wait_ge(r_ready, spreads(10))
            residual_half(3, 0, 1, z, {0: lambda: add_squares(3, KC, 1, b=1), 3: lambda: invert_half(11, 1)})
            dve.wait_ge(r_ready, spreads(11))
            residual_half(3, 1, 1, z, {})
            dve.wait_ge(y_turned, 5)
            dve.tensor_copy(y_tok[:, 3, 512:D], flat(7, 0, 512)).then_inc(y_ready_dve, 1)

        @block.gpsimd
        def _(pool):
            pool.memset(eps[:, :], EPS)
            pool.memset(ssq[:, :], 1.0)
            pool.memset(ones[:, :], 1.0).then_inc(set_up, 1)
            pool.memset(k_s[:, DEC:CHUNK], 0.0)
            pool.memset(mask_s[:, 0:DEC], 0.0)
            pool.memset(mask_s[:, CHUNK:P], 0.0)
            pool.memset(mask_s[:, DEC:CHUNK], MASKED).then_inc(set_sample, 1)
            pool.memset(mean_var[:, :, :], 1.0).then_inc(set_stats, 1)
            pool.memset(acc_post[:, :], 0.0).then_inc(acc_zeroed, 1)
            pool.wait_ge(ln_loaded, 32)
            for t, (t0, n) in enumerate(TILES):
                pool.wait_ge(va_normed, t + 1)
                pool.tensor_tensor(va[0:n, t, :], va[0:n, t, :], ln_gb[0:n, 0, :], ALU.mult).then_inc(va_scaled, 1)
            for t, (t0, n) in enumerate(TILES):
                pool.wait_ge(va_scaled, t + 1)
                pool.tensor_tensor(va[0:n, t, :], va[0:n, t, :], ln_gb[0:n, 1, :], ALU.add).then_inc(va_ready, 1)
            pool.wait_ge(va_ready, NT)
            pool.dma_start(av_s[0, 0].rearrange("t h c -> t (h c)"), va[0:DEC, NT - 1, :]).then_inc(out_stored, 16)
            pool.wait_ge(v_evacuated, 2)
            pool.dma_start(bv_p[0, 0].rearrange("t g d -> t (g d)"), v_t[:, 3, :]).then_inc(out_stored, 16)
            pool.dma_start(bv_s[0, 0].rearrange("t g d -> t (g d)"), v_s[0:DEC, :]).then_inc(out_stored, 16)
            pool.wait_ge(rope_done, 1)
            pool.tensor_copy(k_s[:, 0:DEC], k_r[:, SEQ:TOK]).then_inc(k_s_ready, 1)
            pool.wait_ge(k_out_ready, 1)
            pool.dma_start(bk_p[0, 0].rearrange("t g d -> t (g d)"), k_out[:, 0, :]).then_inc(out_stored, 16)
            pool.dma_start(bk_s[0, 0].rearrange("t g d -> t (g d)"), k_out[0:DEC, 1, :]).then_inc(out_stored, 16)
            for c in range(NCH + 1):
                n, b = (2, c % 2) if c == NCH else (4, c % 2)
                w = CHUNK if c == 0 else P
                p = s_sb[:, b, 0:n * P].rearrange("p (c s) -> p c s", c=n)[:, :, 0:w]
                pool.wait_ge(rden_ready, c + 1)
                pool.tensor_tensor(p, p, rden[:, b, 0:n].unsqueeze(2).broadcast_to([P, n, w]), ALU.mult).then_inc(p_ready, 1)
            for t in range(AH - 1):
                pool.wait_ge(u_gelu, t + 1)
                pool.wait_ge(gate_biased, t + 1)
                pool.tensor_tensor(gated[:, t, :], gated[:, t, :], u_raw[:, t, :], ALU.mult).then_inc(ya_ready, 1)

            def add_square(s, b, k):
                n = H_BEFORE[s] + KC * b + k
                pool.wait_ge(h_squared, n + 1)
                if k == 0:
                    pool.sem_inc(pre_added, 1)
                    return
                pool.wait_ge(pre_added, n)
                pool.tensor_tensor(acc_pre[:, frames(b)], acc_pre[:, frames(b)], tmp2[:, k % 2, frames(b)], ALU.add)\
                    .then_inc(pre_added, 1)

            def residual_halves(s, source):
                def scale(b, k):
                    n = H_BEFORE[s] + KC * b + k
                    if n >= 4:
                        pool.wait_ge(h_added, n - 3)
                    pool.tensor_tensor(quarter(k), source[:, k, frames(b)], r_post[:, frames(b)], ALU.mult)\
                        .then_inc(half_scaled_pool, 1)

                for b in range(2):
                    if s in SHARED:
                        pool.wait_ge(r_ready, spreads(NORM_POST[s] + b))
                        scale(b, 1)
                        scale(b, 3)
                    for k in range(KC):
                        if s < 3:
                            add_square(s, b, k)
                        if s in SHARED and k in (1, 3):
                            scale(b, k + 4)

            def zero_sum(n):
                pool.wait_ge(sum_ready, n)
                pool.memset(acc_post[:, :], 0.0).then_inc(acc_zeroed, 1)

            residual_halves(0, z)
            zero_sum(2)
            residual_halves(1, z)
            zero_sum(5)
            pool.wait_ge(h_tok_ready, 2 * KC)
            pool.wait_ge(rstd_ready, 7)
            pool.tensor_scalar(pool_out[0:TAIL, :], h_tok[0:TAIL, NT - 1, :], rstd[0:TAIL, NT - 1:NT], None, ALU.mult)\
                .then_inc(pool_out_ready, 1)
            pool.wait_ge(pool_out_ready, 1)
            pool.dma_start(cp_p[0, 0], pool_out[TAIL_SEQ - HIST:TAIL_SEQ, :]).then_inc(out_stored, 16)
            pool.dma_start(cp_s[0, 0], pool_out[TAIL - HIST:TAIL, :]).then_inc(out_stored, 16)
            m = U_FI[1] + 2
            pool.wait_ge(w_hi, m + 1)
            pool.wait_ge(w_lo, m)
            pool.tensor_tensor(wlo[:, m % NSPLIT, :], raw[:, m % NRAW, :], whi[:, m % NSPLIT, :].bitcast(F32), ALU.subtract)\
                .then_inc(w_lo, 1)
            pool.wait_ge(out_stored, 16 * MIXER_STORES[1])
            residual_halves(2, z_pool)
            zero_sum(8)
            residual_halves(3, z)


_INS = ["x_prompt", "x_sample", "cache_b_k", "cache_b_v", "state_c_pool", "norm_g", "ab_w_in", "a_ln_g", "a_ln_b",
        "a_ws", "a_bs", "b_sinks", "ab_w_out", "c_w", "c_scale", "ffn_w_in", "ffn_w_out"]
_OUTS = [(1, SEQ, D), (1, DEC, D), (1, 1, WIN, NKV, HD), (1, 1, WIN, NKV, HD), (1, 1, HIST, D),
         (1, 1, DEC, NKV, HD), (1, 1, DEC, NKV, HD), (1, 1, HIST, D), (1, 1, DEC, AH, P)]


def kernel(**inputs):
    import numpy as _np
    import concourse.bacc as _bacc
    from concourse import mybir as _mybir
    from concourse.bass_utils import run_bass_kernel_spmd as _run

    nc = _bacc.Bacc("TRN2", target_bir_lowering=False, num_devices=1)
    arrays, args = {}, []
    named = [(name, _np.ascontiguousarray(inputs[name])) for name in _INS] + [("constants", shape_constants())]
    for name, a in named:
        arrays[f"in_{name}_dram"] = a
        args.append(nc.dram_tensor(f"in_{name}_dram", a.shape, _mybir.dt.from_np(a.dtype), kind="ExternalInput").ap())
    for i, shape in enumerate(_OUTS):
        args.append(nc.dram_tensor(f"out_{i}_dram", shape, _mybir.dt.float32, kind="ExternalOutput").ap())
    build(nc, *args)
    r = _run(nc, [arrays], core_ids=[0])
    return tuple(r.results[0][f"out_{i}_dram"] for i in range(len(_OUTS)))
```
